# Optimizing a Trainium2 kernel written in Bass

```python
import math
import jax
import jax.numpy as jnp
from jax import lax
import numpy as np

D_MODEL = 1024
BATCH = 1
SEQ = 128
DEPTH = 2
DEC_BATCH = 1
DEC_SEQ = 1024
PAST_LEN = 128

GRID_W = 64
N_EVEN = (DEPTH + 1) // 2
N_ODD = DEPTH // 2
RMS_EPS = 1e-6
N_MOD = 6
D_FF = 4 * D_MODEL
CONV_K = 3
Q_BLOCK = 128

NA_HEADS = 8
NA_HEAD_DIM = 64
NA_WIDTH = NA_HEADS * NA_HEAD_DIM
NA_WIN_ROWS = 8
NA_WIN_COLS = 16
NA_RPB_ROWS = 2 * NA_WIN_ROWS - 1
NA_RPB_COLS = 2 * NA_WIN_COLS - 1

SSD_INNER = D_MODEL
SSD_HEAD_DIM = 64
SSD_HEADS = SSD_INNER // SSD_HEAD_DIM
SSD_GROUPS = 2
SSD_RPG = SSD_HEADS // SSD_GROUPS
SSD_STATE = 128
SSD_GN = SSD_GROUPS * SSD_STATE
SSD_CONV_DIM = SSD_INNER + 2 * SSD_GN
SSD_CHUNK = 128

ML_HEADS = 8
ML_QK_DIM = D_MODEL // 16
ML_V_DIM = D_MODEL // 8
ML_QK_WIDTH = ML_HEADS * ML_QK_DIM
ML_V_WIDTH = ML_HEADS * ML_V_DIM
ML_CHUNK = 64

EVEN_SPLITS = (NA_WIDTH, 2 * NA_WIDTH, 3 * NA_WIDTH, 3 * NA_WIDTH + SSD_INNER, 3 * NA_WIDTH + 2 * SSD_INNER + 2 * SSD_GN)
EVEN_IN = 3 * NA_WIDTH + 2 * SSD_INNER + 2 * SSD_GN + 2 * SSD_HEADS
EVEN_MIX = NA_WIDTH + SSD_INNER
ODD_SPLITS = (2 * ML_QK_WIDTH, 2 * ML_QK_WIDTH + ML_V_WIDTH, 2 * ML_QK_WIDTH + 2 * ML_V_WIDTH)
ODD_IN = 2 * ML_QK_WIDTH + 2 * ML_V_WIDTH + 4 * ML_HEADS

kernel_name = "hybrid_na_ssd_mlstm_prefix_dit_step"

def rmsnorm(x, g):
    xf = x.astype(jnp.float32)
    y = xf * lax.rsqrt(jnp.mean(xf * xf, axis=-1, keepdims=True) + RMS_EPS)
    return (y * g.astype(jnp.float32)).astype(x.dtype)

def modulate(x, g, shift, scale):
    return rmsnorm(x, g) * (1 + scale[:, None, :]) + shift[:, None, :]

def adaln_params(cond, w, b):
    return jnp.split(jax.nn.silu(cond) @ w + b, N_MOD, axis=-1)

def dwconv_same(x, w, b):
    L = x.shape[1]
    pad = CONV_K // 2
    xp = jnp.pad(x, ((0, 0), (pad, pad), (0, 0)))
    y = xp[:, 0:L] * w[0]
    for j in range(1, CONV_K):
        y = y + xp[:, j:j + L] * w[j]
    return y + b

def sqrelu_mlp(h, w1, w2):
    return jnp.square(jax.nn.relu(h @ w1)) @ w2

def even_inputs(h, w_in):
    b, L, _ = h.shape
    q, k, v, z, xbc, dt = jnp.split(h @ w_in, EVEN_SPLITS, axis=-1)
    heads = lambda t: t.reshape(b, L, NA_HEADS, NA_HEAD_DIM)
    return heads(q) * NA_HEAD_DIM ** -0.5, heads(k), heads(v), z, xbc, dt

def ctx_attention(q, k, v):
    b, S, H, dh = q.shape
    qb = jnp.moveaxis(q.reshape(b, S // Q_BLOCK, Q_BLOCK, H, dh), 1, 0)

    def block(qi):
        s = jnp.einsum('bqhd,bkhd->bhqk', qi, k).astype(jnp.float32)
        p = jax.nn.softmax(s, axis=-1).astype(v.dtype)
        return jnp.einsum('bhqk,bkhd->bqhd', p, v)

    o = lax.map(block, qb)
    return jnp.moveaxis(o, 0, 1).reshape(b, S, H * dh)

def na_latent(q, k, v, k_ctx, v_ctx, rpb):
    b, L, H, dh = q.shape
    rows = L // GRID_W
    wr = min(NA_WIN_ROWS, rows)
    r = jnp.arange(rows)
    key_rows = jnp.clip(r - NA_WIN_ROWS // 2, 0, rows - wr)[:, None] + jnp.arange(wr)[None]
    col = jnp.arange(GRID_W)
    col_start = jnp.clip(col - NA_WIN_COLS // 2, 0, GRID_W - NA_WIN_COLS)
    col_in = (col[None, :] >= col_start[:, None]) & (col[None, :] < col_start[:, None] + NA_WIN_COLS)
    rel_r = key_rows - r[:, None] + NA_WIN_ROWS - 1
    rel_c = jnp.clip(col[None, :] - col[:, None] + NA_WIN_COLS - 1, 0, NA_RPB_COLS - 1)
    bias = rpb[:, rel_r[:, None, :, None], rel_c[None, :, None, :]].astype(jnp.float32)
    bias = jnp.where(col_in[None, None, :, None, :], bias, -jnp.inf).reshape(H, rows, GRID_W, wr * GRID_W)
    qg = q.reshape(b, rows, GRID_W, H, dh)
    kg = k.reshape(b, rows, GRID_W, H, dh)[:, key_rows].reshape(b, rows, wr * GRID_W, H, dh)
    vg = v.reshape(b, rows, GRID_W, H, dh)[:, key_rows].reshape(b, rows, wr * GRID_W, H, dh)
    s_loc = jnp.einsum('brqhd,brkhd->bhrqk', qg, kg).astype(jnp.float32) + bias[None]
    s_ctx = jnp.einsum('brqhd,bhcd->bhrqc', qg, k_ctx).astype(jnp.float32)
    p = jax.nn.softmax(jnp.concatenate([s_loc, s_ctx], axis=-1), axis=-1).astype(v.dtype)
    n_loc = wr * GRID_W
    o = jnp.einsum('bhrqk,brkhd->brqhd', p[..., :n_loc], vg) + jnp.einsum('bhrqc,bhcd->brqhd', p[..., n_loc:], v_ctx)
    return o.reshape(b, L, H * dh)

def ssd_scan(x, dt, A, Bm, Cm, h0):
    b, L, G, R, P = x.shape
    nc = L // SSD_CHUNK
    chunks = lambda t: jnp.moveaxis(t.reshape((b, nc, SSD_CHUNK) + t.shape[2:]), 1, 0)
    causal = jnp.tril(jnp.ones((SSD_CHUNK, SSD_CHUNK), bool))[None, :, :, None, None]

    def step(h, inp):
        xc, dtc, Bc, Cc = inp
        cum = jnp.cumsum(dtc * A, axis=1)
        seg = jnp.where(causal, cum[:, :, None] - cum[:, None], -jnp.inf)
        wts = jnp.einsum('bign,bjgn->bijg', Cc, Bc)[..., None] * jnp.exp(seg) * dtc[:, None]
        y = jnp.einsum('bijgr,bjgrp->bigrp', wts, xc)
        y = y + jnp.einsum('bign,bgrpn->bigrp', Cc, h) * jnp.exp(cum)[..., None]
        w_end = jnp.exp(cum[:, -1:] - cum) * dtc
        h = h * jnp.exp(cum[:, -1])[..., None, None] + jnp.einsum('bjgn,bjgr,bjgrp->bgrpn', Bc, w_end, xc)
        return h, y

    h, ys = lax.scan(step, h0, (chunks(x), chunks(dt), chunks(Bm), chunks(Cm)))
    return jnp.moveaxis(ys, 0, 1).reshape(b, L, G, R, P), h

def ssd_branch(z, xbc, dt_raw, conv_w, conv_b, dt_bias, a_log, d_skip, norm_g, h0_f, h0_b):
    b, L, _ = z.shape
    f32 = jnp.float32
    xbc = jax.nn.silu(dwconv_same(xbc, conv_w, conv_b)).astype(f32)
    xs, Bm, Cm = jnp.split(xbc, (SSD_INNER, SSD_INNER + SSD_GN), axis=-1)
    xs = xs.reshape(b, L, SSD_GROUPS, SSD_RPG, SSD_HEAD_DIM)
    Bm = Bm.reshape(b, L, SSD_GROUPS, SSD_STATE)
    Cm = Cm.reshape(b, L, SSD_GROUPS, SSD_STATE)
    dt = jax.nn.softplus(dt_raw.astype(f32).reshape(b, L, 2, SSD_GROUPS, SSD_RPG)
                         + dt_bias.astype(f32).reshape(2, SSD_GROUPS, SSD_RPG))
    A = -jnp.exp(a_log.astype(f32)).reshape(2, SSD_GROUPS, SSD_RPG)
    st = lambda h: h.astype(f32).reshape(b, SSD_GROUPS, SSD_RPG, SSD_HEAD_DIM, SSD_STATE)
    flip = lambda t: jnp.flip(t, axis=1)
    y_f, hf = ssd_scan(xs, dt[:, :, 0], A[0], Bm, Cm, st(h0_f))
    y_b, hb = ssd_scan(flip(xs), flip(dt[:, :, 1]), A[1], flip(Bm), flip(Cm), st(h0_b))
    y = y_f + flip(y_b) + d_skip.astype(f32).reshape(SSD_GROUPS, SSD_RPG, 1) * xs
    y = y.reshape(b, L, SSD_INNER).astype(z.dtype)
    y = rmsnorm(y * jax.nn.silu(z), norm_g)
    unst = lambda h: h.reshape(b, SSD_HEADS, SSD_HEAD_DIM, SSD_STATE).astype(z.dtype)
    return y, unst(hf), unst(hb)

def mlstm_scan(q, k, v, log_i, log_f, c0, n0, m0):
    b, L, H, _ = q.shape
    nc = L // ML_CHUNK
    chunks = lambda t: jnp.moveaxis(t.reshape((b, nc, ML_CHUNK) + t.shape[2:]), 1, 0)
    causal = jnp.tril(jnp.ones((ML_CHUNK, ML_CHUNK), bool))[None, :, :, None]

    def step(carry, inp):
        c, n, m = carry
        qc, kc, vc, li, lf = inp
        cum = jnp.cumsum(lf, axis=1)
        dmat = jnp.where(causal, cum[:, :, None] - cum[:, None] + li[:, None], -jnp.inf)
        m_inter = cum + m[:, None]
        m_t = jnp.maximum(m_inter, jnp.max(dmat, axis=2))
        w_intra = jnp.exp(dmat - m_t[:, :, None])
        w_inter = jnp.exp(m_inter - m_t)
        s = jnp.einsum('bihd,bjhd->bijh', qc, kc) * w_intra
        num = jnp.einsum('bijh,bjhe->bihe', s, vc) + w_inter[..., None] * jnp.einsum('bhed,bihd->bihe', c, qc)
        den = jnp.sum(s, axis=2) + w_inter * jnp.einsum('bhd,bihd->bih', n, qc)
        h = num / jnp.maximum(jnp.abs(den), jnp.exp(-m_t))[..., None]
        g = cum[:, -1:] - cum + li
        m_new = jnp.maximum(cum[:, -1] + m, jnp.max(g, axis=1))
        wk = jnp.exp(g - m_new[:, None])
        wc = jnp.exp(cum[:, -1] + m - m_new)
        c_new = wc[..., None, None] * c + jnp.einsum('bjh,bjhe,bjhd->bhed', wk, vc, kc)
        n_new = wc[..., None] * n + jnp.einsum('bjh,bjhd->bhd', wk, kc)
        return (c_new, n_new, m_new), h

    xs = (chunks(q), chunks(k), chunks(v), chunks(log_i), chunks(log_f))
    (c, n, m), hs = lax.scan(step, (c0, n0, m0), xs)
    return jnp.moveaxis(hs, 0, 1).reshape(b, L, H, v.shape[-1]), c, n, m

def mlstm_branch(h, w_in, conv_w, conv_b, gate_b, st_f, st_b):
    b, L, _ = h.shape
    f32 = jnp.float32
    qk, v, o, gates = jnp.split(h @ w_in, ODD_SPLITS, axis=-1)
    qk = jax.nn.silu(dwconv_same(qk, conv_w, conv_b)).astype(f32)
    q, k = jnp.split(qk, 2, axis=-1)
    q = q.reshape(b, L, ML_HEADS, ML_QK_DIM) * ML_QK_DIM ** -0.5
    k = k.reshape(b, L, ML_HEADS, ML_QK_DIM)
    v = v.astype(f32).reshape(b, L, ML_HEADS, ML_V_DIM)
    gates = gates.astype(f32).reshape(b, L, 2, 2, ML_HEADS) + gate_b.astype(f32)
    log_i = gates[:, :, 0]
    log_f = jax.nn.log_sigmoid(gates[:, :, 1])
    flip = lambda t: jnp.flip(t, axis=1)
    hf, cf, nf, mf = mlstm_scan(q, k, v, log_i[:, :, 0], log_f[:, :, 0], st_f[0], st_f[1], st_f[2])
    hb, cb, nb, mb = mlstm_scan(flip(q), flip(k), flip(v), flip(log_i[:, :, 1]), flip(log_f[:, :, 1]),
                                st_b[0], st_b[1], st_b[2])
    y = (hf + flip(hb)).reshape(b, L, ML_V_WIDTH).astype(h.dtype) * jax.nn.sigmoid(o)
    return y, (cf, nf, mf), (cb, nb, mb)

def setup_inputs(seed: int = 0) -> dict:
    key = jax.random.key(seed)
    ks = jax.random.split(key, 40)
    f32 = jnp.float32
    nrm = lambda i, shape, s: s * jax.random.normal(ks[i], shape, f32)
    gain = lambda i, shape: 1.0 + 0.05 * jax.random.normal(ks[i], shape, f32)
    dt0 = jnp.exp(jax.random.uniform(ks[20], (N_EVEN, 2, SSD_HEADS), f32, math.log(1e-3), math.log(1e-1)))
    i_bias = nrm(30, (N_ODD, 1, 2, ML_HEADS), 0.1)
    f_bias = 3.0 + 3.0 * jax.random.uniform(ks[31], (N_ODD, 1, 2, ML_HEADS), f32)
    return {
        'x_prompt': nrm(0, (BATCH, SEQ, D_MODEL), 1.0),
        'x_sample': nrm(1, (DEC_BATCH, DEC_SEQ, D_MODEL), 1.0),
        'c': nrm(2, (DEC_BATCH, D_MODEL), 1.0),
        'cache_na_k': nrm(3, (DEC_BATCH, N_EVEN, NA_HEADS, PAST_LEN, NA_HEAD_DIM), 1.0),
        'cache_na_v': nrm(4, (DEC_BATCH, N_EVEN, NA_HEADS, PAST_LEN, NA_HEAD_DIM), 1.0),
        'state_ssd': nrm(5, (DEC_BATCH, N_EVEN, 2, SSD_HEADS, SSD_HEAD_DIM, SSD_STATE), 0.5),
        'state_mlstm_c': nrm(6, (DEC_BATCH, N_ODD, 2, ML_HEADS, ML_V_DIM, ML_QK_DIM), 0.5),
        'state_mlstm_n': nrm(7, (DEC_BATCH, N_ODD, 2, ML_HEADS, ML_QK_DIM), 0.5),
        'state_mlstm_m': nrm(8, (DEC_BATCH, N_ODD, 2, ML_HEADS), 1.0),
        'c_ctx': nrm(9, (D_MODEL,), 1.0),
        'w_mod': nrm(10, (DEPTH, D_MODEL, N_MOD * D_MODEL), 0.5 * D_MODEL ** -0.5),
        'b_mod': nrm(11, (DEPTH, N_MOD * D_MODEL), 0.02),
        'norm_mix': gain(12, (DEPTH, D_MODEL)),
        'norm_ffn': gain(13, (DEPTH, D_MODEL)),
        'w_in_even': nrm(14, (N_EVEN, D_MODEL, EVEN_IN), D_MODEL ** -0.5),
        'w_out_even': nrm(15, (N_EVEN, EVEN_MIX, D_MODEL), EVEN_MIX ** -0.5),
        'na_rpb': nrm(16, (N_EVEN, NA_HEADS, NA_RPB_ROWS, NA_RPB_COLS), 0.5),
        'ssd_conv_w': nrm(17, (N_EVEN, CONV_K, SSD_CONV_DIM), CONV_K ** -0.5),
        'ssd_conv_b': nrm(18, (N_EVEN, SSD_CONV_DIM), 0.02),
        'ssd_dt_bias': dt0 + jnp.log(-jnp.expm1(-dt0)),
        'ssd_a_log': jnp.log(jax.random.uniform(ks[21], (N_EVEN, 2, SSD_HEADS), f32, 1.0, 16.0)),
        'ssd_d': 1.0 + nrm(22, (N_EVEN, SSD_HEADS), 0.1),
        'ssd_norm': gain(23, (N_EVEN, SSD_INNER)),
        'w_in_odd': nrm(24, (N_ODD, D_MODEL, ODD_IN), D_MODEL ** -0.5),
        'w_out_odd': nrm(25, (N_ODD, ML_V_WIDTH, D_MODEL), ML_V_WIDTH ** -0.5),
        'ml_conv_w': nrm(26, (N_ODD, CONV_K, 2 * ML_QK_WIDTH), CONV_K ** -0.5),
        'ml_conv_b': nrm(27, (N_ODD, 2 * ML_QK_WIDTH), 0.02),
        'ml_gate_b': jnp.concatenate([i_bias, f_bias], axis=1),
        'w_ff1': nrm(32, (DEPTH, D_MODEL, D_FF), D_MODEL ** -0.5),
        'w_ff2': nrm(33, (DEPTH, D_FF, D_MODEL), D_FF ** -0.5),
        'norm_f': gain(34, (D_MODEL,)),
    }

def reference(x_prompt, x_sample, c, cache_na_k, cache_na_v, state_ssd, state_mlstm_c, state_mlstm_n, state_mlstm_m,
              c_ctx, w_mod, b_mod, norm_mix, norm_ffn, w_in_even, w_out_even, na_rpb, ssd_conv_w, ssd_conv_b,
              ssd_dt_bias, ssd_a_log, ssd_d, ssd_norm, w_in_odd, w_out_odd, ml_conv_w, ml_conv_b, ml_gate_b,
              w_ff1, w_ff2, norm_f):
    f32 = jnp.float32
    bp = x_prompt.shape[0]
    xp, xs = x_prompt, x_sample
    cond_ctx = c_ctx[None, :]
    out_k, out_v, out_ssd, out_c, out_n, out_m = [], [], [], [], [], []
    for l in range(DEPTH):
        sh_p, sc_p, g_p, sh2_p, sc2_p, g2_p = adaln_params(cond_ctx, w_mod[l], b_mod[l])
        sh_s, sc_s, g_s, sh2_s, sc2_s, g2_s = adaln_params(c, w_mod[l], b_mod[l])
        hp = modulate(xp, norm_mix[l], sh_p, sc_p)
        hs = modulate(xs, norm_mix[l], sh_s, sc_s)
        if l % 2 == 0:
            e = l // 2
            ssd_w = (ssd_conv_w[e], ssd_conv_b[e], ssd_dt_bias[e], ssd_a_log[e], ssd_d[e], ssd_norm[e])
            q, k, v, z, xbc, dt = even_inputs(hp, w_in_even[e])
            zero = jnp.zeros((bp, SSD_HEADS, SSD_HEAD_DIM, SSD_STATE), hp.dtype)
            y_ssd, s_f, s_b = ssd_branch(z, xbc, dt, *ssd_w, zero, zero)
            mp = jnp.concatenate([ctx_attention(q, k, v), y_ssd], axis=-1) @ w_out_even[e]
            out_k.append(jnp.swapaxes(k, 1, 2))
            out_v.append(jnp.swapaxes(v, 1, 2))
            out_ssd.append(jnp.stack([s_f, s_b], axis=1))
            q, k, v, z, xbc, dt = even_inputs(hs, w_in_even[e])
            y_ssd, _, _ = ssd_branch(z, xbc, dt, *ssd_w, state_ssd[:, e, 0], state_ssd[:, e, 1])
            y_na = na_latent(q, k, v, cache_na_k[:, e], cache_na_v[:, e], na_rpb[e])
            ms = jnp.concatenate([y_na, y_ssd], axis=-1) @ w_out_even[e]
        else:
            o = l // 2
            ml_w = (w_in_odd[o], ml_conv_w[o], ml_conv_b[o], ml_gate_b[o])
            zc = jnp.zeros((bp, ML_HEADS, ML_V_DIM, ML_QK_DIM), f32)
            zn = jnp.zeros((bp, ML_HEADS, ML_QK_DIM), f32)
            zm = jnp.zeros((bp, ML_HEADS), f32)
            y, (cf, nf, mf), (cb, nb, mb) = mlstm_branch(hp, *ml_w, (zc, zn, zm), (zc, zn, zm))
            mp = y @ w_out_odd[o]
            out_c.append(jnp.stack([cf, cb], axis=1).astype(xp.dtype))
            out_n.append(jnp.stack([nf, nb], axis=1).astype(xp.dtype))
            out_m.append(jnp.stack([mf, mb], axis=1).astype(xp.dtype))
            st_f = (state_mlstm_c[:, o, 0].astype(f32), state_mlstm_n[:, o, 0].astype(f32), state_mlstm_m[:, o, 0].astype(f32))
            st_b = (state_mlstm_c[:, o, 1].astype(f32), state_mlstm_n[:, o, 1].astype(f32), state_mlstm_m[:, o, 1].astype(f32))
            y, _, _ = mlstm_branch(hs, *ml_w, st_f, st_b)
            ms = y @ w_out_odd[o]
        xp = xp + g_p[:, None, :] * mp
        xs = xs + g_s[:, None, :] * ms
        xp = xp + g2_p[:, None, :] * sqrelu_mlp(modulate(xp, norm_ffn[l], sh2_p, sc2_p), w_ff1[l], w_ff2[l])
        xs = xs + g2_s[:, None, :] * sqrelu_mlp(modulate(xs, norm_ffn[l], sh2_s, sc2_s), w_ff1[l], w_ff2[l])
    y_prompt = rmsnorm(xp, norm_f)
    y_sample = rmsnorm(xs, norm_f)
    new_na_k = jnp.stack(out_k, axis=1)
    new_na_v = jnp.stack(out_v, axis=1)
    new_ssd = jnp.stack(out_ssd, axis=1)
    new_mlstm_c = jnp.stack(out_c, axis=1)
    new_mlstm_n = jnp.stack(out_n, axis=1)
    new_mlstm_m = jnp.stack(out_m, axis=1)
    return (y_prompt, y_sample, new_na_k, new_na_v, new_ssd, new_mlstm_c, new_mlstm_n, new_mlstm_m)


_drawn_inputs = setup_inputs


def setup_inputs(seed=0):
    import zlib

    import numpy as np

    out = dict(_drawn_inputs(seed))
    spreads = {}
    factors = {'cache_na_k': 4.788,
     'cache_na_v': 3.987,
     'state_mlstm_c': 5.728,
     'state_mlstm_n': 8.0,
     'state_mlstm_m': 6.228,
     'na_rpb': 5.812,
     'ssd_norm': 3.219}
    for name, (base, spread) in spreads.items():
        noise = np.random.default_rng([zlib.crc32(name.encode()), seed]).standard_normal(out[name].shape)
        drawn = base * np.exp(spread * noise) if base else spread * noise
        out[name] = jnp.asarray(drawn.astype(out[name].dtype))
    for name, factor in factors.items():
        out[name] = (out[name] * factor).astype(out[name].dtype)
    return out
```

```python
import numpy as np

import concourse.bass as bass
from concourse import mybir
from contextlib import ExitStack

F32 = mybir.dt.float32
ALU = mybir.AluOpType
ACT = mybir.ActivationFunctionType
AX = mybir.AxisListType

P = 128
D = 1024
KD = D // P
CTX, LAT = 128, 1024
T = CTX + LAT
NT = T // P
TC = 384
NC = T // TC
EPS = 1e-6
FF = 4 * D
NG = FF // 512
NH, HD = 8, 64
SH, SP, SN = 16, 64, 128
MH, MQ, MV = 8, 64, 128
V1 = MV + 1
ROWS = 40
NEG = -1e30
SEGS = [(0, 128, 0, 0), (128, 384, 1, 0), (384, 768, 1, 1), (768, 1152, 1, 2)]

CONSTS = {}


def const_table():
    k = np.arange(P)[:, None]
    i = np.arange(P)[None, :]
    parts = {
        "ident": (k == i) * 1.0,
        "ones": np.ones((P, P)),
        "le": (k <= i) * 1.0,
        "ge": (k >= i) * 1.0,
        "gt": (k > i) * 1.0,
        "lt": (k < i) * 1.0,
        "neg_f": np.where(k <= i, 0.0, NEG),
        "neg_b": np.where(k >= i, 0.0, NEG),
    }
    c = np.arange(P) % 64
    start = np.clip(c - 8, 0, 48)
    cc = np.arange(64)[None, :]
    parts["col"] = np.where((cc >= start[:, None]) & (cc < start[:, None] + 16), 0.0, NEG)
    sel = np.zeros((P, 16, P))
    for d in range(2):
        for h in range(8):
            sel[32 * d + h, 8 * d + h, :] = 1.0
    parts["sel"] = sel.reshape(P, -1)
    reset = np.ones((P, NT, P))
    reset[0:8, :, 0] = 0.0
    reset[32:40, :, P - 1] = 0.0
    parts["reset"] = reset.reshape(P, -1)
    at, cols = 0, []
    for name, a in parts.items():
        CONSTS[name] = (at, a.shape[1])
        at += a.shape[1]
        cols.append(a)
    return np.concatenate(cols, 1).astype(np.float32)


def row_consts():
    base = const_table()
    row = np.arange(P)[:, None]
    m = np.arange(P)[None, :]
    half = (row % 2 == m // 64) * 1.0
    n = np.arange(8)[None, :]
    pair = (row // 32 == n // 4) & (row % 32 // 2 == n % 4)
    return np.concatenate([base, half.astype(np.float32), pair.astype(np.float32)], 1)


const_table()
NCONST = 8 * P + 64

VECS = {}
for _name, _n in [("cond", 16), ("b_mod", 96), ("norm_mix", 16), ("norm_ffn", 16), ("norm_f", 8), ("ssd_norm", 8),
                  ("cw", 36), ("cb", 12), ("mw", 24), ("mb", 8), ("dt_bias", 32), ("a_log", 32), ("ssd_d", 16),
                  ("gate_b", 32), ("m0", 1)]:
    VECS[_name] = (sum(n for _, n in VECS.values()), _n)
NVEC = sum(n for _, n in VECS.values())

S_MOD, S_QKV, S_Z, S_XBC, S_OUTE, S_W1E, S_QK, S_VO, S_OUTO, S_W1O = 0, 24, 27, 29, 32, 36, 44, 46, 50, 52
NSLOT = 60


class Count:

    def __init__(self, sem):
        self.sem, self.base = sem, 0

    def at(self, n):
        return self.base + n

    def close(self, n):
        self.base += n


class Chain:

    def __init__(self, sem):
        self.sem, self.n = sem, 0

    def one(self):
        self.n += 1
        return 1


def hybrid_step(nc, xT, vec, consts, wslots, w2, wsmall, rpbT, kcT, vc, ssd0, mls0, yT, o_k, o_v, o_ssd, o_mls, o_m):
    ctx = ExitStack()
    with ctx:
        def sb(name, shape):
            return ctx.enter_context(nc.sbuf_tensor(name, shape, F32))

        def count(name):
            return Count(ctx.enter_context(nc.semaphore(name)))

        XT = sb("XT", [P, 9288])
        HT = sb("HT", [P, 9216])
        F0 = sb("F0", [P, 9216])
        F1 = sb("F1", [P, 9216])
        WR = sb("WR", [P, 2, 4096])
        CO = sb("CO", [P, NCONST])
        VE = sb("VE", [P, NVEC])
        WS = sb("WS", [P, 2, KD, 32])
        MOD = sb("MOD", [P, 2, 48, 2])
        GM = sb("GM", [P, 2, 2, KD, 2])
        MI = sb("MI", [P, 4096])
        SM = sb("SM", [P, 1472])
        PS = ctx.enter_context(nc.psum_tensor("PS", [P, 8, 512], F32))

        x_spill = nc.dram_tensor("x_spill", (P, 9216), F32).ap()
        z_spill = nc.dram_tensor("z_spill", (NT, P, D), F32).ap()

        def const(name):
            a, n = CONSTS[name]
            return CO[:, a:a + n]

        def vecs(name):
            a, n = VECS[name]
            return VE[:, a:a + n]

        ident, ones = const("ident"), const("ones")
        xk = XT[:, 0:9216].rearrange("p (k t) -> p k t", k=KD)
        hk = HT[:, :].rearrange("p (k t) -> p k t", k=KD)
        f0k = F0[:, :].rearrange("p (k t) -> p k t", k=8)
        f1k = F1[:, :].rearrange("p (k t) -> p k t", k=8)

        w_ready = [count("w_ready0"), count("w_ready1")]
        w_used = count("w_used")
        w2_ready = [count("w2_ready0"), count("w2_ready1")]
        w2_used = count("w2_used")
        tile_done = count("tile_done")
        tile_free = count("tile_free")
        first_in = count("first_in")
        spilled = count("spilled")
        xback = count("xback")
        stored = count("stored")
        loaded = count("loaded")
        cond_silu = count("cond_silu")
        squares_ready = count("squares_ready")
        squares_summed = count("squares_summed")
        mean_ready = count("mean_ready")
        rms_ready = count("rms_ready")
        scaled_ready = count("scaled_ready")
        scores_taken = count("scores_taken")
        scores_done = count("scores_done")
        max_ready = count("max_ready")
        probs_ready = count("probs_ready")
        probs_turned = count("probs_turned")
        probsT_ready = count("probsT_ready")
        values_summed = count("values_summed")
        output_taken = count("output_taken")
        bias_ready = count("bias_ready")
        attn_turned = count("attn_turned")
        attn_taken = count("attn_taken")
        borders_zero = count("borders_zero")
        conv_done = count("conv_done")
        silu_done = count("silu_done")
        block_turned = count("block_turned")
        turned_taken = count("turned_taken")
        softplus_dve_part = count("softplus_dve_part")
        softplus_act_part = count("softplus_act_part")
        decay_ready = count("decay_ready")
        decay_summed = count("decay_summed")
        cb_done = count("cb_done")
        cb_masked = count("cb_masked")
        masked_decay_ready = count("masked_decay_ready")
        decays_summed = count("decays_summed")
        decays_taken = count("decays_taken")
        x_scaled = count("x_scaled")
        state_read = count("state_read")
        weights_ready = count("weights_ready")
        chunk_summed = count("chunk_summed")
        step_taken = count("step_taken")
        update_summed = count("update_summed")
        gated = count("gated")
        square_sum_ready = count("square_sum_ready")
        gate_mean_ready = count("gate_mean_ready")
        gate_rms_ready = count("gate_rms_ready")
        gate_scaled = count("gate_scaled")
        mix_turned = count("mix_turned")
        mix_taken = count("mix_taken")
        relu_ready = count("relu_ready")
        hidden_ready = count("hidden_ready")
        gates_ready = count("gates_ready")
        rows_turned = count("rows_turned")
        logs_ready = count("logs_ready")
        exps_ready = count("exps_ready")
        rows_ready = count("rows_ready")
        rows_back = count("rows_back")
        exponents_done = count("exponents_done")
        exponents_masked = count("exponents_masked")
        qk_done = count("qk_done")
        exp_ready = count("exp_ready")
        scores_weighted = count("scores_weighted")
        intra_taken = count("intra_taken")
        memory_summed = count("memory_summed")
        tail_done = count("tail_done")
        values_weighted = count("values_weighted")
        intra_summed = count("intra_summed")
        z_stage = [count(f"z_stage{n}") for n in range(4)]
        bias_loaded = [count(f"bias_loaded{n}") for n in range(2)]
        gate_loaded = [count(f"gate_loaded{n}") for n in range(2)]
        dve_own = Chain(count("dve_own").sem)
        act_own = Chain(count("act_own").sem)
        pool_own = Chain(count("pool_own").sem)

        fed = [0]

        free_at = {n: (w_used.sem, n + 1) for n in range(S_QKV)}

        def feed(sp, upto):
            while fed[0] < upto:
                n = fed[0]
                if n >= 2:
                    sp.wait_ge(*free_at[n - 2])
                cols = 3072 if S_OUTE <= n < S_W1E else 4096
                sp.dma_start(WR[:, n % 2, 0:cols], wslots[n, :, 0:cols]).then_inc(w_ready[n % 2].sem, 16)
                fed[0] += 1

        def landed(n):
            return w_ready[n % 2].sem, 16 * (n // 2 + 1)

        with nc.Block() as block:
            @block.sync
            def _(sp):
                sp.dma_start(VE[:, :], vec).then_inc(first_in.sem, 16)
                sp.dma_start(CO[:, :], consts[:, 0:NCONST]).then_inc(first_in.sem, 16)
                feed(sp, 2)
                sp.dma_start(WS[:, :, :, :], wsmall).then_inc(first_in.sem, 16)
                sp.dma_start(XT[:, 0:9216], xT).then_inc(first_in.sem, 16)

            @block.scalar
            def _(act):
                act.wait_ge(first_in.sem, 64)
                act.activation(SM[:, 0:16], vecs("cond"), ACT.Silu).then_inc(cond_silu.sem, 1)
        cond_silu.close(1)
        condT = SM[:, 0:16].rearrange("p (k c) -> p k c", k=KD)

        with nc.Block() as block:
            @block.sync
            def _(sp):
                with sp.Fori(2, 24, 2) as n:
                    for s in range(2):
                        sp.wait_ge(w_used.sem, n + s - 1)
                        sp.dma_start(WR[:, s, :], wslots[bass.ds(n + s, 1), :, :].rearrange("a p n -> p (a n)"))\
                          .then_inc(w_ready[s].sem, 16)
                fed[0] = 24
                feed(sp, S_QKV + 2)

            @block.tensor
            def _(pe):
                with pe.Fori(0, 12) as i:
                    for s in range(2):
                        pe.wait_ge(w_ready[s].sem, i * 16 + 16)
                        w = WR[:, s, :].rearrange("p (k n) -> p k n", k=KD)
                        for j in range(4):
                            for k in range(KD):
                                mm = nc.tensor.matmul(PS[:, 0, bass.ds(i * 16 + (s * 8 + j * 2), 2)],
                                                      w[:, k, j * P:(j + 1) * P], condT[:, k, :],
                                                      start=(k == 0), stop=(k == KD - 1))
                        mm.then_inc(w_used.sem, 1)

            @block.vector
            def _(dve):
                dve.wait_ge(w_used.sem, 24)
                b = vecs("b_mod").rearrange("p (l j) -> p l j", l=2)
                raw = PS[:, 0, 0:192].rearrange("p (l j c) -> p l j c", l=2, c=2)
                for c in range(2):
                    nc.vector.tensor_tensor(MOD[:, :, :, c], raw[:, :, :, c], b, ALU.add).then_inc(dve_own.sem, dve_own.one())
                dve.wait_ge(dve_own.sem, dve_own.n)
                for l in range(2):
                    for n, name in enumerate(("norm_mix", "norm_ffn")):
                        g = vecs(name).rearrange("p (l k) -> p l k", l=2)[:, l, :]
                        for c in range(2):
                            nc.vector.scalar_tensor_tensor(out=GM[:, l, n, :, c],
                                                           in0=MOD[:, l, (3 * n + 1) * 8:(3 * n + 1) * 8 + 8, c],
                                                           scalar=1.0, in1=g, op0=ALU.add, op1=ALU.mult)

        def norm(l, which):
            SQ = F1[:, 4608:4608 + 3072].rearrange("p (n t) -> p n t", n=8)
            RB = F1[:, 7680:7680 + T]
            final = which == 2
            with nc.Block() as block:
                @block.scalar
                def _(act):
                    for i in range(NC * KD):
                        c, k = i // KD, i % KD
                        if i >= 8:
                            act.wait_ge(squares_summed.sem, squares_summed.at(i - 7))
                        act.activation(SQ[:, i % 8, :], xk[:, k, c * TC:(c + 1) * TC], ACT.Square)\
                           .then_inc(squares_ready.sem, 1)
                    for c in range(NC):
                        act.wait_ge(mean_ready.sem, mean_ready.at(c + 1))
                        act.activation(RB[:, c * TC:(c + 1) * TC], RB[:, c * TC:(c + 1) * TC], ACT.Sqrt)\
                           .then_inc(rms_ready.sem, 1)
                    if not final:
                        n = 0
                        for a, b, c, _ in SEGS:
                            for k in range(KD):
                                n += 1
                                act.wait_ge(scaled_ready.sem, scaled_ready.at(n))
                                act.activation(hk[:, k, a:b], hk[:, k, a:b], ACT.Identity,
                                               bias=MOD[:, l, 24 * which + k, c:c + 1])

                @block.tensor
                def _(pe):
                    for i in range(NC * KD):
                        pe.wait_ge(squares_ready.sem, squares_ready.at(i + 1))
                        nc.tensor.matmul(PS[:, i // KD, 0:TC], ones, SQ[:, i % 8, :],
                                         start=(i % KD == 0), stop=(i % KD == KD - 1)).then_inc(squares_summed.sem, 1)

                @block.vector
                def _(dve):
                    for c in range(NC):
                        dve.wait_ge(squares_summed.sem, squares_summed.at(KD * (c + 1)))
                        r = RB[:, c * TC:(c + 1) * TC]
                        nc.vector.tensor_scalar(r, PS[:, c, 0:TC], 1.0 / D, EPS, ALU.mult, ALU.add).then_inc(dve_own.sem, dve_own.one())
                        dve.wait_ge(dve_own.sem, dve_own.n)
                        nc.vector.reciprocal(r, r).then_inc(mean_ready.sem, 1)
                    n = 0
                    for a, b, cond, c in SEGS:
                        dve.wait_ge(rms_ready.sem, rms_ready.at(c + 1))
                        for k in range(KD):
                            g = vecs("norm_f")[:, k:k + 1] if final else GM[:, l, which, k, cond:cond + 1]
                            nc.vector.scalar_tensor_tensor(out=hk[:, k, a:b], in0=xk[:, k, a:b], scalar=g,
                                                           in1=RB[:, a:b], op0=ALU.mult, op1=ALU.mult)\
                              .then_inc(scaled_ready.sem, 1)
                            n += 1

                if final:
                    @block.sync
                    def _(sp):
                        for s, (a, b, _, _) in enumerate(SEGS):
                            sp.wait_ge(scaled_ready.sem, scaled_ready.at(KD * (s + 1)))
                            sp.dma_start(yT[:, :, a:b], hk[:, :, a:b]).then_inc(stored.sem, 16)
                        sp.wait_ge(stored.sem, stored.at(64))
            squares_ready.close(24)
            squares_summed.close(24)
            mean_ready.close(NC)
            rms_ready.close(NC)
            scaled_ready.close(4 * KD)
            if final:
                stored.close(64)

        def tile_products(pe, i, m, n, terms, banks=8):
            if i >= banks:
                pe.wait_ge(tile_free.sem, tile_free.at(i - banks + 1))
            for t, (lhs, rhs) in enumerate(terms):
                mm = nc.tensor.matmul(PS[0:m, i % banks, 0:n], lhs, rhs, start=(t == 0), stop=(t == len(terms) - 1))
            mm.then_inc(tile_done.sem, 1)

        def feature_tile(pe, i, w, col, c, banks=8):
            tile_products(pe, i, P, TC, [(w[:, k, col:col + P], hk[:, k, c * TC:(c + 1) * TC]) for k in range(KD)], banks)

        def token_tile(pe, i, w, t):
            tile_products(pe, i, P, 512, [(hk[:, k, t * P:(t + 1) * P], w[:, k, :]) for k in range(KD)])

        def slot_k(n):
            return WR[:, n % 2, :].rearrange("p (k n) -> p k n", k=KD)

        def frees(slots, per_slot):
            at = 0
            for n, k in zip(slots, per_slot):
                at += k
                free_at[n] = (tile_done.sem, tile_done.at(at))

        def close_tiles(n):
            tile_done.close(n)
            tile_free.close(n)

        zst = MI[:, 0:2048].rearrange("p (s n) -> p s n", s=4)

        def spill_gate_act(act, i, func):
            for z in range(2 * NT):
                act.wait_ge(tile_done.sem, tile_done.at(i + 1))
                if z >= 4:
                    act.wait_ge(z_stage[z % 4].sem, z_stage[z % 4].at(16 * (z // 4)))
                act.activation(zst[:, z % 4, :], PS[:, i % 8, :], func).then_inc(tile_free.sem, 1)
                i += 1

        def spill_gate_sp(sp, i):
            for z in range(2 * NT):
                s, t = z // NT, z % NT
                sp.wait_ge(tile_free.sem, tile_free.at(i + z + 1))
                sp.dma_start(z_spill[t, :, s * 512:(s + 1) * 512], zst[:, z % 4, :]).then_inc(z_stage[z % 4].sem, 16)
            for n in range(4):
                sp.wait_ge(z_stage[n].sem, z_stage[n].at(16 * len(range(n, 18, 4))))

        def close_gate():
            for n in range(4):
                z_stage[n].close(16 * len(range(n, 18, 4)))

        norm(0, 0)

        qT = F0[:, 0:4608].rearrange("p (b t) -> p b t", b=4)
        kT = F0[:, 4608:9216].rearrange("p (b t) -> p b t", b=4)
        vtok = F1[:, 0:4608].rearrange("p (t n) -> p t n", t=NT)
        frees(range(S_QKV, S_XBC), (12, 12, 9, 9, 9))

        with nc.Block() as block:
            @block.sync
            def _(sp):
                sp.dma_start(x_spill, XT[:, 0:9216]).then_inc(spilled.sem, 16)
                feed(sp, S_XBC)
                spill_gate_sp(sp, 33)
                feed(sp, S_XBC + 2)
                sp.wait_ge(spilled.sem, spilled.at(16))

            @block.tensor
            def _(pe):
                i = 0
                for s in range(2):
                    pe.wait_ge(*landed(S_QKV + s))
                    for b in range(4):
                        for c in range(NC):
                            feature_tile(pe, i, slot_k(S_QKV + s), b * P, c)
                            i += 1
                for s in (S_QKV + 2, S_Z, S_Z + 1):
                    pe.wait_ge(*landed(s))
                    for t in range(NT):
                        token_tile(pe, i, slot_k(s), t)
                        i += 1

            @block.scalar
            def _(act):
                i = 0
                for s in range(2):
                    for b in range(4):
                        for c in range(NC):
                            act.wait_ge(tile_done.sem, tile_done.at(i + 1))
                            act.activation((qT, kT)[s][:, b, c * TC:(c + 1) * TC], PS[:, i % 8, 0:TC], ACT.Copy,
                                           scale=(HD ** -0.5, 1.0)[s]).then_inc(tile_free.sem, 1)
                            i += 1
                for t in range(NT):
                    act.wait_ge(tile_done.sem, tile_done.at(i + 1))
                    act.activation(vtok[:, t, :], PS[:, i % 8, :], ACT.Copy).then_inc(tile_free.sem, 1)
                    i += 1
                spill_gate_act(act, i, ACT.Silu)
        close_tiles(51)
        spilled.close(16)
        close_gate()

        T2 = F1[:, 4608:6400].rearrange("p (s r c) -> p s r c", s=2, r=14)
        TI = F1[:, 6400:7552].rearrange("p (s r c) -> p s r c", s=2, r=9)
        kcT_sb = F1[:, 7552:8064].rearrange("p (b t) -> p b t", b=4)
        vc_sb = F1[:, 8064:8576]
        yna = XT[:, 0:4608].rearrange("p (t n) -> p t n", t=NT)
        SS = XT[:, 4608:6016].rearrange("p (s n) -> p s n", s=2)
        PT = XT[:, 6016:7552].rearrange("p (s n) -> p s n", s=2)
        mx, nmx, rs, ri = (XT[:, 7552 + 2 * n:7554 + 2 * n] for n in range(4))
        ynaT = F1[:, 4608:9216].rearrange("p (b t) -> p b t", b=4)
        NA = 72

        def na_step(n):
            if n >= 64:
                return n - 64, 0, False, 0, 0
            h, j = n // 8, n % 8
            s = min(max(2 * j - 4, 0), 8)
            return h, s // 2, 2 <= j <= 5, s - 2 * j + 6, 1 + j

        def width(n):
            return 128 if n >= 64 else (704 if na_step(n)[2] else 640)

        def chunks(n):
            h, kt, nine, _, _ = na_step(n)
            v = slice(h * HD, (h + 1) * HD)
            if n >= 64:
                return [(0, P, vtok[:, 0, v])]
            out = [(i * P, P, vtok[:, 1 + kt + i, v]) for i in range(4)] + [(512, P, vc_sb[:, v])]
            if nine:
                out.append((640, 64, vtok[0:64, 1 + kt + 4, v]))
            return out

        with nc.Block() as block:
            @block.sync
            def _(sp):
                sp.dma_start(kcT_sb, kcT).then_inc(loaded.sem, 16)
                sp.dma_start(vc_sb, vc).then_inc(loaded.sem, 16)
                sp.dma_start(o_k, kT[:, :, 0:P]).then_inc(stored.sem, 16)
                sp.dma_start(o_v, vtok[:, 0, :]).then_inc(stored.sem, 16)
                for h in range(NH):
                    if h >= 2:
                        sp.wait_ge(scores_taken.sem, scores_taken.at(8 * (h - 1)))
                        sp.wait_ge(bias_ready.sem, bias_ready.at(h - 1))
                    sp.dma_start(T2[:, h % 2, :, :], rpbT[h]).then_inc(bias_loaded[h % 2].sem, 16)
                sp.wait_ge(stored.sem, stored.at(32))

            @block.gpsimd
            def _(pool):
                col = const("col").unsqueeze(1)
                for h in range(NH):
                    pool.wait_ge(bias_loaded[h % 2].sem, bias_loaded[h % 2].at(16 * (h // 2 + 1)))
                    if h >= 2:
                        pool.wait_ge(scores_taken.sem, scores_taken.at(8 * (h - 1)))
                    nc.gpsimd.tensor_tensor(T2[:, h % 2, :, :], T2[:, h % 2, :, :],
                                                            col.broadcast_to((P, 14, 64)), ALU.add).then_inc(pool_own.sem, pool_own.one())
                    pool.wait_ge(pool_own.sem, pool_own.n)
                    nc.gpsimd.tensor_copy(TI[:, h % 2, :, :], T2[:, h % 2, 2:11, :]).then_inc(pool_own.sem, pool_own.one())
                    pool.wait_ge(pool_own.sem, pool_own.n)
                    nc.gpsimd.memset(TI[0:64, h % 2, 8, :], NEG).then_inc(pool_own.sem, pool_own.one())
                    nc.gpsimd.memset(TI[64:128, h % 2, 0, :], NEG).then_inc(pool_own.sem, pool_own.one())
                    pool.wait_ge(pool_own.sem, pool_own.n)
                    pool.sem_inc(bias_ready.sem, 1)

            @block.tensor
            def _(pe):
                def scores(n):
                    h, kt, nine, _, qt = na_step(n)
                    r = slice(64 * (h % 2), 64 * (h % 2) + 64)
                    q = qT[r, h // 2, qt * P:(qt + 1) * P]
                    b = 2 * (n % 2)
                    if n >= 2:
                        pe.wait_ge(scores_taken.sem, scores_taken.at(n - 1))
                    if n >= 64:
                        nc.tensor.matmul(PS[:, b, 0:P], q, kT[r, h // 2, 0:P], start=True, stop=True).then_inc(scores_done.sem, 1)
                        return
                    if n == 0:
                        pe.wait_ge(loaded.sem, loaded.at(32))
                    k0 = (1 + kt) * P
                    nc.tensor.matmul(PS[:, b, :], q, kT[r, h // 2, k0:k0 + 512], start=True, stop=True)
                    mm = nc.tensor.matmul(PS[:, b + 1, 0:P], q, kcT_sb[r, h // 2, :], start=True, stop=True)
                    if nine:
                        mm = nc.tensor.matmul(PS[:, b + 1, P:P + 64], q, kT[r, h // 2, k0 + 512:k0 + 576],
                                              start=True, stop=True)
                    mm.then_inc(scores_done.sem, 1)

                def turn(n):
                    pe.wait_ge(probs_ready.sem, probs_ready.at(n + 1))
                    if n >= 1:
                        pe.wait_ge(probsT_ready.sem, probsT_ready.at(n))
                    for i, (a, m, _) in enumerate(chunks(n)):
                        mm = nc.tensor.transpose(PS[0:m, 4 + i // 4, (i % 4) * P:(i % 4) * P + P],
                                                 SS[:, n % 2, a:a + m], ident)
                    mm.then_inc(probs_turned.sem, 1)

                def values(n):
                    pe.wait_ge(probsT_ready.sem, probsT_ready.at(n + 1))
                    if n >= 2:
                        pe.wait_ge(output_taken.sem, output_taken.at(n - 1))
                    cs = chunks(n)
                    for i, (_, m, v) in enumerate(cs):
                        mm = nc.tensor.matmul(PS[:, 6 + n % 2, 0:HD], PT[0:m, n % 2, i * P:(i + 1) * P], v,
                                              start=(i == 0), stop=(i == len(cs) - 1))
                    mm.then_inc(values_summed.sem, 1)

                scores(0)
                for n in range(NA):
                    if n + 1 < NA:
                        scores(n + 1)
                    turn(n)
                    if n >= 1:
                        values(n - 1)
                values(NA - 1)

            @block.vector
            def _(dve):
                def softmax_max(n):
                    h, _, nine, r0, _ = na_step(n)
                    b = 2 * (n % 2)
                    dve.wait_ge(scores_done.sem, scores_done.at(n + 1))
                    if n >= 2:
                        dve.wait_ge(probs_turned.sem, probs_turned.at(n - 1))
                    s = SS[:, n % 2, :]
                    if n >= 64:
                        nc.vector.tensor_copy(s[:, 0:P], PS[:, b, 0:P]).then_inc(scores_taken.sem, 1)
                    else:
                        if n % 8 == 0:
                            dve.wait_ge(bias_ready.sem, bias_ready.at(h + 1))
                        bias = (TI[:, h % 2, :, :] if nine else T2[:, h % 2, r0:r0 + 8, :]).rearrange("p r c -> p (r c)")
                        nc.vector.tensor_tensor(s[:, 0:512], PS[:, b, :], bias[:, 0:512], ALU.add).then_inc(dve_own.sem, dve_own.one())
                        if nine:
                            nc.vector.tensor_tensor(s[:, 640:704], PS[:, b + 1, P:P + 64],
                                                                   bias[:, 512:576], ALU.add).then_inc(dve_own.sem, dve_own.one())
                        dve.wait_ge(dve_own.sem, dve_own.n)
                        nc.vector.tensor_copy(s[:, 512:640], PS[:, b + 1, 0:P]).then_inc(scores_taken.sem, 1)
                    dve.wait_ge(scores_taken.sem, scores_taken.at(n + 1))
                    nc.vector.tensor_reduce(mx[:, n % 2:n % 2 + 1], s[:, 0:width(n)], AX.X, ALU.max).then_inc(dve_own.sem, dve_own.one())
                    dve.wait_ge(dve_own.sem, dve_own.n)
                    nc.vector.tensor_scalar(nmx[:, n % 2:n % 2 + 1], mx[:, n % 2:n % 2 + 1], -1.0, None, ALU.mult)\
                      .then_inc(max_ready.sem, 1)

                def normalise(n):
                    h, _, _, _, qt = na_step(n)
                    dve.wait_ge(values_summed.sem, values_summed.at(n + 1))
                    nc.vector.reciprocal(ri[:, n % 2:n % 2 + 1], rs[:, n % 2:n % 2 + 1]).then_inc(dve_own.sem, dve_own.one())
                    dve.wait_ge(dve_own.sem, dve_own.n)
                    nc.vector.tensor_scalar(yna[:, qt, h * HD:(h + 1) * HD], PS[:, 6 + n % 2, 0:HD],
                                            ri[:, n % 2:n % 2 + 1], None, ALU.mult).then_inc(output_taken.sem, 1)

                for n in range(NA):
                    softmax_max(n)
                    if n >= 2:
                        normalise(n - 2)
                normalise(NA - 2)
                normalise(NA - 1)

            @block.scalar
            def _(act):
                def probs(n):
                    act.wait_ge(max_ready.sem, max_ready.at(n + 1))
                    if n >= 2:
                        act.wait_ge(output_taken.sem, output_taken.at(n - 1))
                    s = SS[:, n % 2, 0:width(n)]
                    act.activation(s, s, ACT.Exp, bias=nmx[:, n % 2:n % 2 + 1], accum_out=rs[:, n % 2:n % 2 + 1])\
                       .then_inc(probs_ready.sem, 1)

                def take(n):
                    act.wait_ge(probs_turned.sem, probs_turned.at(n + 1))
                    if n >= 2:
                        act.wait_ge(values_summed.sem, values_summed.at(n - 1))
                    cs = chunks(n)
                    k = min(len(cs), 4) * P
                    ins = act.activation(PT[:, n % 2, 0:k], PS[:, 4, 0:k], ACT.Copy)
                    if len(cs) > 5:
                        ins = act.activation(PT[0:64, n % 2, 640:768], PS[0:64, 5, P:2 * P], ACT.Copy)
                    if len(cs) > 4:
                        ins.then_inc(act_own.sem, act_own.one())
                        ins = act.activation(PT[:, n % 2, 512:640], PS[:, 5, 0:P], ACT.Copy)
                    ins.then_inc(probsT_ready.sem, 1)

                probs(0)
                for n in range(1, NA):
                    probs(n)
                    take(n - 1)
                take(NA - 1)
        loaded.close(32)
        stored.close(32)
        bias_loaded[0].close(64)
        bias_loaded[1].close(64)
        for e in (scores_taken, scores_done, max_ready, probs_ready, probs_turned, probsT_ready, values_summed, output_taken):
            e.close(NA)
        bias_ready.close(NH)

        with nc.Block() as block:
            @block.tensor
            def _(pe):
                for t in range(NT):
                    if t >= 4:
                        pe.wait_ge(attn_taken.sem, attn_taken.at(t - 3))
                    for b in range(4):
                        mm = nc.tensor.transpose(PS[:, t % 4, b * P:(b + 1) * P], yna[:, t, b * P:(b + 1) * P], ident)
                    mm.then_inc(attn_turned.sem, 1)

            @block.scalar
            def _(act):
                for t in range(NT):
                    act.wait_ge(attn_turned.sem, attn_turned.at(t + 1))
                    act.activation(ynaT[:, :, t * P:(t + 1) * P], PS[:, t % 4, :].rearrange("p (b n) -> p b n", b=4),
                                   ACT.Copy).then_inc(attn_taken.sem, 1)
        attn_turned.close(NT)
        attn_taken.close(NT)

        def conv_phase(s0, nblocks, raw, cv, silu_out, turned, w, bias, spill_x=False):
            turns = [b for b in range(nblocks) if turned(b) is not None]
            frees(range(s0, s0 + nblocks // 4), [12] * (nblocks // 4))
            with nc.Block() as block:
                @block.sync
                def _(sp):
                    if spill_x:
                        sp.dma_start(x_spill, XT[:, 0:9216]).then_inc(spilled.sem, 16)
                        sp.wait_ge(spilled.sem, spilled.at(16))
                    feed(sp, s0 + nblocks // 4 + (2 if s0 == S_QK else 0))

                @block.gpsimd
                def _(pool):
                    for n in range(2):
                        for a, z in ((0, 1), (129, 131), (1155, 1156)):
                            nc.gpsimd.memset(raw[:, n, a:z], 0.0).then_inc(borders_zero.sem, 1)

                @block.tensor
                def _(pe):
                    def turn(b):
                        n = turns.index(b)
                        pe.wait_ge(silu_done.sem, silu_done.at(b + 1))
                        for c in range(3):
                            j = 3 * n + c
                            if j >= 3:
                                pe.wait_ge(turned_taken.sem, turned_taken.at(j - 2))
                            for t in range(3):
                                mm = nc.tensor.transpose(PS[:, 5 + j % 3, t * P:(t + 1) * P],
                                                         silu_out(b)[:, (3 * c + t) * P:(3 * c + t + 1) * P], ident)
                            mm.then_inc(block_turned.sem, 1)

                    for b in range(nblocks):
                        if b % 4 == 0:
                            pe.wait_ge(*landed(s0 + b // 4))
                        for c in range(NC):
                            feature_tile(pe, b * NC + c, slot_k(s0 + b // 4), (b % 4) * P, c, banks=5)
                        if b >= 1 and (b - 1) in turns:
                            turn(b - 1)
                    if nblocks - 1 in turns:
                        turn(nblocks - 1)

                @block.scalar
                def _(act):
                    def silu(b):
                        act.wait_ge(conv_done.sem, conv_done.at(b + 1))
                        if turned(b) is not None and turns.index(b) >= 2:
                            act.wait_ge(block_turned.sem, block_turned.at(3 * (turns.index(b) - 1)))
                        dst = silu_out(b)
                        act.activation(dst[:, 0:CTX], cv[:, b % 2, 0:CTX], ACT.Silu).then_inc(act_own.sem, act_own.one())
                        act.activation(dst[:, CTX:T], cv[:, b % 2, CTX + 2:T + 2], ACT.Silu).then_inc(silu_done.sem, 1)

                    act.wait_ge(borders_zero.sem, borders_zero.at(6))
                    for b in range(nblocks):
                        if b >= 2:
                            act.wait_ge(conv_done.sem, conv_done.at(b - 1))
                        for c in range(NC):
                            i = b * NC + c
                            act.wait_ge(tile_done.sem, tile_done.at(i + 1))
                            r = raw[:, b % 2, :]
                            if c == 0:
                                act.activation(r[:, 1:129], PS[:, i % 5, 0:CTX], ACT.Copy).then_inc(act_own.sem, act_own.one())
                                act.activation(r[:, 131:387], PS[:, i % 5, CTX:TC], ACT.Copy).then_inc(tile_free.sem, 1)
                            else:
                                act.activation(r[:, c * TC + 3:(c + 1) * TC + 3], PS[:, i % 5, 0:TC], ACT.Copy)\
                                   .then_inc(tile_free.sem, 1)
                        if b >= 1:
                            silu(b - 1)
                    silu(nblocks - 1)

                @block.vector
                def _(dve):
                    def take(b):
                        n = turns.index(b)
                        for c in range(3):
                            dve.wait_ge(block_turned.sem, block_turned.at(3 * n + c + 1))
                            nc.vector.tensor_copy(turned(b)[:, 3 * c:3 * c + 3, :],
                                                  PS[:, 5 + (3 * n + c) % 3, 0:TC].rearrange("p (t n) -> p t n", t=3))\
                              .then_inc(turned_taken.sem, 1)

                    dve.wait_ge(borders_zero.sem, borders_zero.at(6))
                    for b in range(nblocks):
                        dve.wait_ge(tile_free.sem, tile_free.at(NC * (b + 1)))
                        if b >= 2:
                            dve.wait_ge(silu_done.sem, silu_done.at(b - 1))
                        r, o = raw[:, b % 2, :], cv[:, b % 2, :]
                        nc.vector.tensor_scalar(o, r[:, 1:1155], w[:, b, 1:2], bias[:, b:b + 1],
                                                               ALU.mult, ALU.add).then_inc(dve_own.sem, dve_own.one())
                        dve.wait_ge(dve_own.sem, dve_own.n)
                        nc.vector.scalar_tensor_tensor(out=o, in0=r[:, 0:1154], scalar=w[:, b, 0:1],
                                                                      in1=o, op0=ALU.mult, op1=ALU.add).then_inc(dve_own.sem, dve_own.one())
                        dve.wait_ge(dve_own.sem, dve_own.n)
                        nc.vector.scalar_tensor_tensor(out=o, in0=r[:, 2:1156], scalar=w[:, b, 2:3],
                                                       in1=o, op0=ALU.mult, op1=ALU.add).then_inc(conv_done.sem, 1)
                        if b >= 1 and (b - 1) in turns:
                            take(b - 1)
                    if nblocks - 1 in turns:
                        take(nblocks - 1)
            close_tiles(NC * nblocks)
            borders_zero.close(6)
            conv_done.close(nblocks)
            silu_done.close(nblocks)
            block_turned.close(3 * len(turns))
            turned_taken.close(3 * len(turns))

        xs = F0[:, :].rearrange("p (t n) -> p t n", t=NT)
        bcT = F1[:, 0:4608].rearrange("p (b t) -> p b t", b=4)
        btok = XT[:, 0:2304].rearrange("p (t n) -> p t n", t=NT)
        cs = XT[:, 6924:9228].rearrange("p (s t) -> p s t", s=2)

        conv_phase(S_XBC, 12,
                   XT[:, 2304:4616].rearrange("p (s t) -> p s t", s=2), XT[:, 4616:6924].rearrange("p (s t) -> p s t", s=2),
                   lambda b: cs[:, b % 2, :] if b < 8 else bcT[:, b - 8, :],
                   lambda b: xs[:, :, b * P:(b + 1) * P] if b < 8 else (btok[:, :, (b - 8) * P:(b - 7) * P] if b < 10 else None),
                   vecs("cw").rearrange("p (b j) -> p b j", j=3), vecs("cb"))

        def softplus_dve(dve, x, out, s):
            e, u, l, d, r = (s[:, n, :] for n in range(1, 6))

            def chained(ins):
                ins.then_inc(dve_own.sem, dve_own.one())
                dve.wait_ge(dve_own.sem, dve_own.n)
            dve.wait_ge(softplus_act_part.sem, softplus_act_part.at(1))
            nc.vector.tensor_scalar(u, e, 1.0, None, ALU.add).then_inc(softplus_dve_part.sem, 1)
            dve.wait_ge(softplus_dve_part.sem, softplus_dve_part.at(2))
            chained(nc.vector.tensor_scalar(d, u, -1.0, None, ALU.add))
            chained(nc.vector.tensor_scalar(r, d, 1e-30, None, ALU.max))
            chained(nc.vector.reciprocal(r, r))
            chained(nc.vector.tensor_tensor(r, r, e, ALU.mult))
            dve.wait_ge(softplus_act_part.sem, softplus_act_part.at(2))
            chained(nc.vector.tensor_tensor(r, r, l, ALU.mult))
            chained(nc.vector.scalar_tensor_tensor(out=d, in0=d, scalar=0.0, in1=e, op0=ALU.is_equal, op1=ALU.mult))
            chained(nc.vector.tensor_tensor(d, d, r, ALU.add))
            chained(nc.vector.scalar_tensor_tensor(out=out, in0=x, scalar=0.0, in1=d, op0=ALU.max, op1=ALU.add))

        def softplus_act(act, x, s):
            a, e, u, l = (s[:, n, :] for n in range(4))
            act.wait_ge(softplus_dve_part.sem, softplus_dve_part.at(1))
            act.activation(a, x, ACT.Abs).then_inc(act_own.sem, act_own.one())
            act.wait_ge(act_own.sem, act_own.n)
            act.activation(e, a, ACT.Exp, scale=-1.0).then_inc(softplus_act_part.sem, 1)
            act.wait_ge(softplus_dve_part.sem, softplus_dve_part.at(2))
            act.activation(l, u, ACT.Ln).then_inc(softplus_act_part.sem, 1)

        def small_products(pe, l):
            for t in range(NT):
                for k in range(KD):
                    mm = nc.tensor.matmul(PS[:, 0, 32 * t:32 * t + 32], hk[:, k, t * P:(t + 1) * P], WS[:, l, k, :],
                                          start=(k == 0), stop=(k == KD - 1))
            mm.then_inc(tile_done.sem, 1)

        DT, DTA, ECUM, WEND, TOT = (SM[:, 16 + 288 * n:304 + 288 * n].rearrange("p (t c) -> p t c", t=NT) for n in range(5))
        flat = lambda a: a.rearrange("p t c -> p (t c)")
        GB = XT[:, 2304:6912].rearrange("p (t d g i) -> p t d g i", t=NT, d=2, g=2)
        ytok = HT[:, :].rearrange("p (t n) -> p t n", t=NT)
        sp_s = MI[:, 0:1728].rearrange("p (n c) -> p n c", n=6)
        negA = MI[:, 1728:1760]
        x0 = MI[:, 1760:2048]

        with nc.Block() as block:
            @block.tensor
            def _(pe):
                small_products(pe, 0)
                for t in range(NT):
                    if t >= 3:
                        pe.wait_ge(cb_masked.sem, cb_masked.at(2 * (t - 2)))
                    for g in range(2):
                        mm = nc.tensor.matmul(PS[:, 1 + t % 3, g * P:(g + 1) * P], bcT[:, g, t * P:(t + 1) * P],
                                              bcT[:, 2 + g, t * P:(t + 1) * P], start=True, stop=True)
                    mm.then_inc(cb_done.sem, 1)
                pe.wait_ge(decay_ready.sem, decay_ready.at(1))
                for bank, (f, b) in enumerate((("le", "ge"), ("gt", "lt"), ("ones", "ones"))):
                    for d, m in enumerate((f, b)):
                        mm = nc.tensor.matmul(PS[:, 4 + bank, 0:288].rearrange("p (t c) -> p t c", t=NT)[:, :, 16 * d:16 * d + 16],
                                              const(m), DTA[:, :, 16 * d:16 * d + 16], start=True, stop=True)
                mm.then_inc(decay_summed.sem, 1)

            @block.scalar
            def _(act):
                act.activation(negA, vecs("a_log"), ACT.Exp).then_inc(act_own.sem, act_own.one())
                softplus_act(act, x0, sp_s)
                act.wait_ge(decay_summed.sem, decay_summed.at(1))
                for bank, dst in enumerate((ECUM, WEND, TOT)):
                    act.activation(flat(dst), PS[:, 4 + bank, 0:288], ACT.Exp).then_inc(softplus_act_part.sem, 1)

            @block.vector
            def _(dve):
                dve.wait_ge(tile_done.sem, tile_done.at(1))
                bias = vecs("dt_bias").unsqueeze(1).broadcast_to((P, NT, 32))
                nc.vector.tensor_tensor(x0.rearrange("p (t c) -> p t c", t=NT),
                                        PS[:, 0, 0:288].rearrange("p (t c) -> p t c", t=NT), bias, ALU.add)\
                  .then_inc(softplus_dve_part.sem, 1)
                softplus_dve(dve, x0, flat(DT), sp_s)
                nc.vector.scalar_tensor_tensor(out=DTA, in0=DT, scalar=-1.0,
                                               in1=negA.unsqueeze(1).broadcast_to((P, NT, 32)),
                                               op0=ALU.mult, op1=ALU.mult).then_inc(decay_ready.sem, 1)
                for t in range(NT):
                    dve.wait_ge(cb_done.sem, cb_done.at(t + 1))
                    for d, m in enumerate(("le", "ge")):
                        nc.vector.tensor_tensor(GB[:, t, d, :, :], PS[:, 1 + t % 3, 0:256].rearrange("p (g i) -> p g i", g=2),
                                                const(m).unsqueeze(1).broadcast_to((P, 2, P)), ALU.mult).then_inc(cb_masked.sem, 1)
                dve.wait_ge(softplus_act_part.sem, softplus_act_part.at(5))
                nc.vector.tensor_tensor(flat(WEND), flat(WEND), flat(DT), ALU.mult)

            @block.gpsimd
            def _(pool):
                pool.wait_ge(tile_done.sem, tile_done.at(1))
                for t in range(NT):
                    nc.gpsimd.tensor_tensor(ytok[:, t, :].rearrange("p (h n) -> p h n", h=SH),
                                            xs[:, t, :].rearrange("p (h n) -> p h n", h=SH),
                                            vecs("ssd_d").unsqueeze(2).broadcast_to((P, SH, SP)), ALU.mult)
        tile_done.close(1)
        for e, n in ((softplus_dve_part, 2), (softplus_act_part, 5), (decay_ready, 1), (decay_summed, 1), (cb_done, NT), (cb_masked, 2 * NT)):
            e.close(n)

        EW = WR[:, 0, :].rearrange("p (s h i) -> p s h i", s=2, h=SH)
        RW = WR[:, 1, :].rearrange("p (s h i) -> p s h i", s=2, h=SH)
        xdt = MI[:, 0:2048].rearrange("p (s h n) -> p s h n", s=2, h=SH)
        xw = MI[:, 2048:4096].rearrange("p (s h n) -> p s h n", s=2, h=SH)
        HS = XT[:, 6912:8960].rearrange("p (d n) -> p d n", d=2)
        steps = [(0, 0), (1, 0)] + [x for t in range(8) for x in ((0, 1 + t), (1, 8 - t))]
        NS = len(steps)

        with nc.Block() as block:
            @block.sync
            def _(sp):
                for d in range(2):
                    sp.wait_ge(step_taken.sem, step_taken.at(d + 1))
                    sp.dma_start(o_ssd[:, d, :], HS[:, d, :]).then_inc(stored.sem, 16)
                sp.wait_ge(stored.sem, stored.at(32))
                for d in range(2):
                    sp.dma_start(HS[:, d, :], ssd0[:, d, :]).then_inc(loaded.sem, 16)

            @block.gpsimd
            def _(pool):
                for n, (d, t) in enumerate(steps):
                    hs = slice(16 * d, 16 * d + 16)
                    if n >= 2:
                        pool.wait_ge(decays_summed.sem, decays_summed.at(4 * (n - 1)))
                    nc.gpsimd.tensor_tensor(RW[:, n % 2, :, :], DTA[:, t, hs].unsqueeze(2).broadcast_to((P, SH, P)),
                                            const(("le", "ge")[d]).unsqueeze(1).broadcast_to((P, SH, P)), ALU.mult)\
                      .then_inc(masked_decay_ready.sem, 1)
                    if n >= 2:
                        pool.wait_ge(chunk_summed.sem, chunk_summed.at(n - 1))
                    x = xs[:, t, :].rearrange("p (h n) -> p h n", h=SH)
                    nc.gpsimd.tensor_tensor(xdt[:, n % 2, :, :], x,
                                                            DT[:, t, hs].unsqueeze(2).broadcast_to((P, SH, SP)), ALU.mult).then_inc(pool_own.sem, pool_own.one())
                    pool.wait_ge(pool_own.sem, pool_own.n)
                    nc.gpsimd.tensor_tensor(xw[:, n % 2, :, :], x, WEND[:, t, hs].unsqueeze(2).broadcast_to((P, SH, SP)),
                                            ALU.mult).then_inc(x_scaled.sem, 1)

            @block.tensor
            def _(pe):
                def decays(n):
                    pe.wait_ge(masked_decay_ready.sem, masked_decay_ready.at(n + 1))
                    for q in range(4):
                        j = 4 * n + q
                        if j >= 2:
                            pe.wait_ge(decays_taken.sem, decays_taken.at(j - 1))
                        nc.tensor.matmul(PS[:, q % 2, :], const(("gt", "lt")[steps[n][0]]),
                                         RW[:, n % 2, 4 * q:4 * q + 4, :], start=True, stop=True).then_inc(decays_summed.sem, 1)

                decays(0)
                for n, (d, t) in enumerate(steps):
                    if n + 1 < NS:
                        decays(n + 1)
                    if n >= 2:
                        if n == 2:
                            pe.wait_ge(loaded.sem, loaded.at(32))
                        pe.wait_ge(step_taken.sem, step_taken.at(n - 1))
                        if n >= 3:
                            pe.wait_ge(step_taken.sem, step_taken.at(n))
                        for g in range(2):
                            mm = nc.tensor.matmul(PS[:, 3 + g, :], bcT[:, 2 + g, t * P:(t + 1) * P],
                                                  HS[:, d, 512 * g:512 * g + 512], start=True, stop=True)
                        mm.then_inc(state_read.sem, 1)
                    pe.wait_ge(x_scaled.sem, x_scaled.at(n + 1))
                    if n >= 1:
                        pe.wait_ge(step_taken.sem, step_taken.at(n))
                    for g, bank in enumerate((2, 7)):
                        mm = nc.tensor.matmul(PS[:, bank, :], btok[:, t, g * P:(g + 1) * P],
                                              xw[:, n % 2, 8 * g:8 * g + 8, :], start=True, stop=True)
                    mm.then_inc(update_summed.sem, 1)
                    pe.wait_ge(weights_ready.sem, weights_ready.at(n + 1))
                    for h in range(SH):
                        mm = nc.tensor.matmul(PS[:, 5 + h // 8, (h % 8) * SP:(h % 8 + 1) * SP], EW[:, n % 2, h, :],
                                              xdt[:, n % 2, h, :], start=True, stop=True)
                    mm.then_inc(chunk_summed.sem, 1)

            @block.scalar
            def _(act):
                for n in range(NS):
                    if n >= 2:
                        act.wait_ge(chunk_summed.sem, chunk_summed.at(n - 1))
                    for q in range(4):
                        act.wait_ge(decays_summed.sem, decays_summed.at(4 * n + q + 1))
                        act.activation(EW[:, n % 2, 4 * q:4 * q + 4, :], PS[:, q % 2, :].rearrange("p (h i) -> p h i", h=4),
                                       ACT.Exp).then_inc(decays_taken.sem, 1)

            @block.vector
            def _(dve):
                def weights(n):
                    d, t = steps[n]
                    dve.wait_ge(decays_taken.sem, decays_taken.at(4 * n + 4))
                    for g in range(2):
                        e = EW[:, n % 2, 8 * g:8 * g + 8, :]
                        ins = nc.vector.tensor_tensor(e, e, GB[:, t, d, g, :].unsqueeze(1).broadcast_to((P, 8, P)), ALU.mult)
                        if g == 0:
                            ins.then_inc(dve_own.sem, dve_own.one())
                    ins.then_inc(weights_ready.sem, 1)

                weights(0)
                for n, (d, t) in enumerate(steps):
                    if n + 1 < NS:
                        weights(n + 1)
                    hs = slice(16 * d, 16 * d + 16)
                    y = ytok[:, t, :]
                    ci = PS[:, 3:5, :].rearrange("p b (h n) -> p (b h) n", h=8)
                    if n >= 2:
                        dve.wait_ge(state_read.sem, state_read.at(n - 1))
                        dve.wait_ge(dve_own.sem, dve_own.n)
                        nc.vector.tensor_tensor(ci, ci, ECUM[:, t, hs].unsqueeze(2).broadcast_to((P, SH, SP)),
                                                               ALU.mult).then_inc(dve_own.sem, dve_own.one())
                        dve.wait_ge(dve_own.sem, dve_own.n)
                        nc.vector.tensor_tensor(y, y, PS[:, 3:5, :].rearrange("p b n -> p (b n)"), ALU.add).then_inc(dve_own.sem, dve_own.one())
                        h = HS[:, d, :].rearrange("p (h n) -> p h n", h=SH)
                        dve.wait_ge(update_summed.sem, update_summed.at(n + 1))
                        nc.vector.tensor_tensor(h, h, TOT[:, t, hs].unsqueeze(2).broadcast_to((P, SH, SP)),
                                                               ALU.mult).then_inc(dve_own.sem, dve_own.one())
                        dve.wait_ge(dve_own.sem, dve_own.n)
                        for g, bank in enumerate((2, 7)):
                            s = HS[:, d, 512 * g:512 * g + 512]
                            nc.vector.tensor_tensor(s, s, PS[:, bank, :], ALU.add).then_inc(dve_own.sem, dve_own.one())
                        dve.wait_ge(chunk_summed.sem, chunk_summed.at(n + 1))
                        dve.wait_ge(dve_own.sem, dve_own.n)
                        nc.vector.tensor_tensor(y, y, PS[:, 5:7, :].rearrange("p b n -> p (b n)"), ALU.add)\
                          .then_inc(step_taken.sem, 1)
                    else:
                        dve.wait_ge(update_summed.sem, update_summed.at(n + 1))
                        for g, bank in enumerate((2, 7)):
                            nc.vector.tensor_copy(HS[:, d, 512 * g:512 * g + 512], PS[:, bank, :]).then_inc(dve_own.sem, dve_own.one())
                        dve.wait_ge(chunk_summed.sem, chunk_summed.at(n + 1))
                        dve.wait_ge(dve_own.sem, dve_own.n)
                        nc.vector.tensor_tensor(y, y, PS[:, 5:7, :].rearrange("p b n -> p (b n)"), ALU.add).then_inc(dve_own.sem, dve_own.one())
                        dve.wait_ge(dve_own.sem, dve_own.n)
                        dve.sem_inc(step_taken.sem, 1)
                        if n == 1:
                            dve.wait_ge(loaded.sem, loaded.at(32))
        stored.close(32)
        loaded.close(32)
        for e, n in ((masked_decay_ready, NS), (decays_summed, 4 * NS), (decays_taken, 4 * NS), (x_scaled, NS), (state_read, NS - 2), (weights_ready, NS), (chunk_summed, NS),
                     (step_taken, NS), (update_summed, NS)):
            e.close(n)

        def gate(l, next_slot):
            zt = MI[:, 0:2048].rearrange("p (s n) -> p s n", s=2)
            sq = MI[:, 2048:3072]
            ss = MI[:, 3072:3072 + 4 * NT].rearrange("p (n t) -> p n t", n=4)
            normed = l == 0
            with nc.Block() as block:
                @block.sync
                def _(sp):
                    sp.dma_start(XT[:, 0:9216], x_spill).then_inc(xback.sem, 16)
                    for t in range(NT):
                        if t >= 2:
                            sp.wait_ge(gated.sem, gated.at(t - 1))
                        sp.dma_start(zt[:, t % 2, :], z_spill[t, :, :]).then_inc(gate_loaded[t % 2].sem, 16)
                    feed(sp, next_slot + 2)

                def scaled(dve, t):
                    dve.wait_ge(gate_rms_ready.sem, gate_rms_ready.at(t + 1))
                    nc.vector.tensor_scalar(ytok[:, t, :], ytok[:, t, :], ss[:, 3, t:t + 1], None, ALU.mult)\
                      .then_inc(gate_scaled.sem, 1)

                @block.vector
                def _(dve):
                    for t in range(NT):
                        y = ytok[:, t, :]
                        dve.wait_ge(gate_loaded[t % 2].sem, gate_loaded[t % 2].at(16 * (t // 2 + 1)))
                        nc.vector.tensor_tensor(y, y, zt[:, t % 2, :], ALU.mult).then_inc(gated.sem, 1)
                        if normed:
                            dve.wait_ge(square_sum_ready.sem, square_sum_ready.at(t + 1))
                            nc.vector.tensor_scalar(ss[:, 1, t:t + 1], ss[:, 0, t:t + 1], 1.0 / D, EPS,
                                                                   ALU.mult, ALU.add).then_inc(dve_own.sem, dve_own.one())
                            dve.wait_ge(dve_own.sem, dve_own.n)
                            nc.vector.reciprocal(ss[:, 2, t:t + 1], ss[:, 1, t:t + 1]).then_inc(gate_mean_ready.sem, 1)
                        if normed and t >= 1:
                            scaled(dve, t - 1)
                    if normed:
                        scaled(dve, NT - 1)

                ready = gate_scaled if normed else gated

                @block.tensor
                def _(pe):
                    for t in range(NT):
                        pe.wait_ge(ready.sem, ready.at(t + 1))
                        for g in range(2):
                            j = 2 * t + g
                            if j >= 4:
                                pe.wait_ge(mix_taken.sem, mix_taken.at(j - 3))
                            for b in range(4):
                                mm = nc.tensor.transpose(PS[:, j % 4, b * P:(b + 1) * P],
                                                         ytok[:, t, (4 * g + b) * P:(4 * g + b + 1) * P], ident)
                            mm.then_inc(mix_turned.sem, 1)

                @block.scalar
                def _(act):
                    def take(t):
                        for g in range(2):
                            j = 2 * t + g
                            act.wait_ge(mix_turned.sem, mix_turned.at(j + 1))
                            for b in range(4):
                                ins = act.activation(f0k[:, 4 * g + b, t * P:(t + 1) * P], PS[:, j % 4, b * P:(b + 1) * P],
                                                     ACT.Copy) if not normed else \
                                    act.activation(f0k[:, 4 * g + b, t * P:(t + 1) * P], PS[:, j % 4, b * P:(b + 1) * P],
                                                   ACT.Identity, scale=vecs("ssd_norm")[:, 4 * g + b:4 * g + b + 1])
                                if b < 3:
                                    ins.then_inc(act_own.sem, act_own.one())
                            act.wait_ge(act_own.sem, act_own.n)
                            ins.then_inc(mix_taken.sem, 1)

                    for t in range(NT):
                        if normed:
                            act.wait_ge(gated.sem, gated.at(t + 1))
                            if t >= 1:
                                act.wait_ge(act_own.sem, act_own.n)
                            act.activation(sq, ytok[:, t, :], ACT.Square, accum_out=ss[:, 0, t:t + 1]).then_inc(act_own.sem, act_own.one())
                            act.wait_ge(act_own.sem, act_own.n)
                            act.sem_inc(square_sum_ready.sem, 1)
                            act.wait_ge(gate_mean_ready.sem, gate_mean_ready.at(t + 1))
                            act.activation(ss[:, 3, t:t + 1], ss[:, 2, t:t + 1], ACT.Sqrt).then_inc(gate_rms_ready.sem, 1)
                        if t >= 1:
                            take(t - 1)
                    take(NT - 1)
            for e in (gate_loaded[0], gate_loaded[1]):
                e.close(16 * len(range(gate_loaded.index(e), NT, 2)))
            gated.close(NT)
            if normed:
                for e in (square_sum_ready, gate_mean_ready, gate_rms_ready, gate_scaled):
                    e.close(NT)
            mix_turned.close(2 * NT)
            mix_taken.close(2 * NT)

        def add_gated(dve, l, gate_at, b, c, bank, last):
            for a, e, cond, tc in SEGS:
                if tc != c:
                    continue
                x = xk[:, b, a:e]
                ins = nc.vector.scalar_tensor_tensor(out=x, in0=PS[:, bank, a - c * TC:e - c * TC],
                                                     scalar=MOD[:, l, gate_at + b, cond:cond + 1], in1=x,
                                                     op0=ALU.mult, op1=ALU.add)
                if e != (c + 1) * TC:
                    ins.then_inc(dve_own.sem, dve_own.one())
            last(ins)

        def out_projection(l, s0, nslots, blocks, next_slot):
            per = KD // nslots
            kk = len(blocks)
            frees(range(s0, s0 + nslots), [per * NC] * nslots)
            with nc.Block() as block:
                @block.sync
                def _(sp):
                    feed(sp, next_slot + 2)

                @block.tensor
                def _(pe):
                    i = 0
                    for s in range(nslots):
                        pe.wait_ge(*landed(s0 + s))
                        w = WR[:, (s0 + s) % 2, 0:kk * per * P].rearrange("p (k n) -> p k n", k=kk)
                        for b in range(per):
                            for c in range(NC):
                                tile_products(pe, i, P, TC, [(w[:, k, b * P:(b + 1) * P], blocks[k][:, c * TC:(c + 1) * TC])
                                                             for k in range(kk)])
                                i += 1

                @block.vector
                def _(dve):
                    dve.wait_ge(xback.sem, xback.at(16))
                    for i in range(KD * NC):
                        dve.wait_ge(tile_done.sem, tile_done.at(i + 1))
                        add_gated(dve, l, 16, i // NC, i % NC, i % 8, lambda ins: ins.then_inc(tile_free.sem, 1))
            close_tiles(KD * NC)
            xback.close(16)

        h1 = F1[:, 0:4608].rearrange("p (b t) -> p b t", b=4)
        W2R = F0[:, 0:8192].rearrange("p (s k n) -> p s k n", s=2, k=4)

        def mlp(l, s0, next_slot):
            rt = MI[:, 0:3072].rearrange("p (s t) -> p s t", s=8)
            first = 12 + 24
            tpi = 2 * first
            assert s0 % 2 == 0
            with nc.Block() as block:
                @block.sync
                def _(sp):
                    for s in range(2):
                        sp.dma_start(W2R[:, s, :, :].rearrange("p k n -> p (k n)"), w2[8 * l + s, :, :])\
                          .then_inc(w2_ready[s].sem, 16)
                    with sp.Fori(0, 3) as i:
                        for s in range(2):
                            sp.wait_ge(tile_done.sem, i * tpi + tile_done.at(s * first + 12))
                            sp.dma_start(WR[:, s, :], wslots[bass.ds(i * 2 + (s0 + 2 + s), 1), :, :].rearrange("a p n -> p (a n)"))\
                              .then_inc(w_ready[s].sem, 16)
                            sp.wait_ge(tile_done.sem, i * tpi + tile_done.at(s * first + 36))
                            sp.dma_start(W2R[:, s, :, :].rearrange("p k n -> p (k n)"),
                                         w2[bass.ds(i * 2 + (8 * l + 2 + s), 1), :, :].rearrange("a p n -> p (a n)"))\
                              .then_inc(w2_ready[s].sem, 16)
                    fed[0] = s0 + 8
                    free_at[s0 + 6] = (tile_done.sem, tile_done.at(3 * tpi + 12))
                    free_at[s0 + 7] = (tile_done.sem, tile_done.at(3 * tpi + first + 12))
                    feed(sp, min(next_slot + 2, NSLOT))

                @block.tensor
                def _(pe):
                    with pe.Fori(0, 4) as i:
                        for s in range(2):
                            pe.wait_ge(w_ready[s].sem, i * 16 + 16 * (s0 // 2 + 1))
                            w = WR[:, s, :].rearrange("p (k n) -> p k n", k=KD)
                            for j in range(first):
                                n = s * first + j
                                if n == 0:
                                    pe.wait_ge(relu_ready.sem, i * 24 + relu_ready.at(0))
                                    pe.wait_ge(tile_free.sem, i * 48 + tile_free.at(0))
                                elif n >= 8:
                                    ps, pj = (n - 8) // first, (n - 8) % first
                                    if pj < 12:
                                        pe.wait_ge(relu_ready.sem, i * 24 + relu_ready.at(12 * ps + pj + 1))
                                    else:
                                        pe.wait_ge(tile_free.sem, i * 48 + tile_free.at(24 * ps + pj - 11))
                                if j < 12:
                                    terms = [(w[:, k, (j // NC) * P:(j // NC + 1) * P],
                                              hk[:, k, (j % NC) * TC:(j % NC + 1) * TC]) for k in range(KD)]
                                else:
                                    if j == 12:
                                        pe.wait_ge(w2_ready[s].sem, i * 16 + w2_ready[s].at(16))
                                        pe.wait_ge(hidden_ready.sem, i * 24 + hidden_ready.at(12 * s + 12))
                                    m = j - 12
                                    b, c = m // NC, m % NC
                                    terms = [(W2R[:, s, k, b * P:(b + 1) * P], h1[:, k, c * TC:(c + 1) * TC])
                                             for k in range(4)]
                                for t, (lhs, rhs) in enumerate(terms):
                                    mm = nc.tensor.matmul(PS[:, n % 8, 0:TC], lhs, rhs, start=(t == 0),
                                                          stop=(t == len(terms) - 1))
                                mm.then_inc(tile_done.sem, 1)

                @block.scalar
                def _(act):
                    with act.Fori(0, 4) as i:
                        for s in range(2):
                            for j in range(12):
                                n = s * first + j
                                act.wait_ge(tile_done.sem, i * tpi + tile_done.at(n + 1))
                                act.wait_ge(hidden_ready.sem, i * 24 + hidden_ready.at(max(12 * s + j - 7, 0)))
                                act.activation(rt[:, (12 * s + j) % 8, :], PS[:, n % 8, 0:TC], ACT.Relu)\
                                   .then_inc(relu_ready.sem, 1)

                @block.gpsimd
                def _(pool):
                    with pool.Fori(0, 4) as i:
                        for s in range(2):
                            for j in range(12):
                                q = 12 * s + j
                                pool.wait_ge(relu_ready.sem, i * 24 + relu_ready.at(q + 1))
                                if j == 0:
                                    pool.wait_ge(tile_done.sem, i * tpi + tile_done.at(s * first))
                                r = rt[:, q % 8, :]
                                nc.gpsimd.tensor_tensor(h1[:, j // NC, (j % NC) * TC:(j % NC + 1) * TC], r, r, ALU.mult)\
                                  .then_inc(hidden_ready.sem, 1)

                @block.vector
                def _(dve):
                    with dve.Fori(0, 4) as i:
                        for s in range(2):
                            for m in range(24):
                                n = s * first + 12 + m
                                dve.wait_ge(tile_done.sem, i * tpi + tile_done.at(n + 1))
                                if m == 0:
                                    dve.wait_ge(tile_free.sem, i * 48 + tile_free.at(24 * s))
                                b, c = m // NC, m % NC
                                for a, e, cond, tc in SEGS:
                                    if tc == c:
                                        x = xk[:, b, a:e]
                                        ins = nc.vector.scalar_tensor_tensor(
                                            out=x, in0=PS[:, n % 8, a - c * TC:e - c * TC],
                                            scalar=MOD[:, l, 40 + b, cond:cond + 1], in1=x, op0=ALU.mult, op1=ALU.add)
                                ins.then_inc(tile_free.sem, 1)
            tile_done.close(4 * tpi)
            tile_free.close(4 * 48)
            relu_ready.close(96)
            hidden_ready.close(96)
            for s in range(2):
                w2_ready[s].close(64)

        gate(0, S_OUTE)
        out_projection(0, S_OUTE, 4, [ynaT[:, b, :] for b in range(4)] + [f0k[:, b, :] for b in range(8)], S_W1E)
        norm(0, 1)
        mlp(0, S_W1E, S_QK)
        norm(1, 0)

        ktok = F1[:, 0:4608].rearrange("p (t n) -> p t n", t=NT)
        conv_phase(S_QK, 8,
                   F1[:, 4608:6920].rearrange("p (s t) -> p s t", s=2), MI[:, 0:2308].rearrange("p (s t) -> p s t", s=2),
                   lambda b: (qT[:, b, :] if b < 4 else kT[:, b - 4, :]),
                   lambda b: ktok[:, :, (b - 4) * P:(b - 3) * P] if b >= 4 else None,
                   vecs("mw").rearrange("p (b j) -> p b j", j=3), vecs("mb"),
                   spill_x=True)
        spilled.close(16)

        v1 = XT[:, :].rearrange("p (t h e) -> p t h e", t=NT, h=MH)
        x1 = MI[:, 2048:2336]
        frees(range(S_VO, S_OUTO), (9, 9, 9, 9))
        with nc.Block() as block:
            @block.sync
            def _(sp):
                feed(sp, S_OUTO)
                spill_gate_sp(sp, 18)

            @block.tensor
            def _(pe):
                i = 0
                for s in range(S_VO, S_OUTO):
                    pe.wait_ge(*landed(s))
                    for t in range(NT):
                        token_tile(pe, i, slot_k(s), t)
                        i += 1
                pe.wait_ge(tile_free.sem, tile_free.at(i))
                small_products(pe, 1)

            @block.gpsimd
            def _(pool):
                nc.gpsimd.memset(v1[:, :, :, MV:V1], 1.0)

            @block.scalar
            def _(act):
                i = 0
                for s in range(2):
                    for t in range(NT):
                        act.wait_ge(tile_done.sem, tile_done.at(i + 1))
                        act.activation(v1[:, t, 4 * s:4 * s + 4, 0:MV], PS[:, i % 8, :].rearrange("p (h e) -> p h e", h=4),
                                       ACT.Copy).then_inc(tile_free.sem, 1)
                        i += 1
                spill_gate_act(act, i, ACT.Sigmoid)

            @block.vector
            def _(dve):
                dve.wait_ge(tile_done.sem, tile_done.at(37))
                nc.vector.tensor_tensor(x1.rearrange("p (t c) -> p t c", t=NT),
                                        PS[:, 0, 0:288].rearrange("p (t c) -> p t c", t=NT),
                                        vecs("gate_b").unsqueeze(1).broadcast_to((P, NT, 32)), ALU.add)
        tile_done.close(37)
        tile_free.close(36)
        close_gate()

        R40 = slice(0, ROWS)
        row = lambda n: HT[R40, n * T:(n + 1) * T]
        LI, LF, M, CU, A, WI, EN, WK = (row(n) for n in range(8))
        B = F1[R40, 4608:4608 + T]
        CST = F1[:, 5760:6792].rearrange("p (d b e) -> p d b e", d=2, b=4)
        WCB = F1[:, 6792:6864].rearrange("p (d b t) -> p d b t", d=2, b=4)
        TA = SM[:, 0:1440].rearrange("p (t n r) -> p t n r", t=NT, n=4)
        SEL = WR[R40, 0, 0:2048].rearrange("p (n m) -> p n m", n=16)
        RST = WR[R40, 0, 2048:3200]
        HALF = WR[R40, 0, 3200:3328]
        PAIR = WR[R40, 0, 3328:3336]
        lf = MI[:, 0:144].rearrange("p (t c) -> p t c", t=NT)
        xf = MI[:, 144:288].rearrange("p (t c) -> p t c", t=NT)
        g_s = MI[:, 288:1152].rearrange("p (n c) -> p n c", n=6)
        tokG = MI[:, 1152:1872].rearrange("p (n t r) -> p n t r", n=2, t=NT)
        MP, ML, CL, WC, DL = (MI[R40, 2400 + 9 * n:2409 + 9 * n] for n in range(5))
        WX = MI[R40, 2448:2520].rearrange("p (n t) -> p n t", n=8)

        def seq3(a):
            return a.rearrange("p (t i) -> p t i", t=NT)

        with nc.Block() as block:
            @block.sync
            def _(sp):
                n0 = NCONST
                sp.dma_start(WR[R40, 0, 0:3336], consts[R40, n0:n0 + 3336]).then_inc(loaded.sem, 16)

            @block.vector
            def _(dve):
                def chained(ins):
                    ins.then_inc(dve_own.sem, dve_own.one())
                    dve.wait_ge(dve_own.sem, dve_own.n)
                raw = x1.rearrange("p (t n c) -> p t n c", t=NT, n=2)
                chained(nc.vector.memset(tokG, 0.0))
                nc.vector.tensor_scalar(xf, raw[:, :, 1, :], -1.0, None, ALU.mult).then_inc(softplus_dve_part.sem, 1)
                softplus_dve(dve, xf.rearrange("p t c -> p (t c)"), lf.rearrange("p t c -> p (t c)"), g_s)
                for d in range(2):
                    nc.vector.tensor_copy(tokG[:, 0, :, 32 * d:32 * d + 8], raw[:, :, 0, 8 * d:8 * d + 8]).then_inc(dve_own.sem, dve_own.one())
                    nc.vector.tensor_scalar(tokG[:, 1, :, 32 * d:32 * d + 8], lf[:, :, 8 * d:8 * d + 8],
                                                           -1.0, None, ALU.mult).then_inc(dve_own.sem, dve_own.one())
                dve.wait_ge(dve_own.sem, dve_own.n)
                dve.sem_inc(gates_ready.sem, 1)
                nc.vector.memset(M, 0.0).then_inc(dve_own.sem, dve_own.one())
                nc.vector.memset(CU, 0.0).then_inc(dve_own.sem, dve_own.one())
                nc.vector.memset(MP, 0.0).then_inc(dve_own.sem, dve_own.one())
                dve.wait_ge(rows_turned.sem, rows_turned.at(1))
                for n, dst in enumerate((LI, LF)):
                    nc.vector.tensor_copy(dst[:, 0:1024].rearrange("p (b t) -> p b t", b=2),
                                                         PS[R40, 3 * n:3 * n + 2, :]).then_inc(dve_own.sem, dve_own.one())
                    nc.vector.tensor_copy(dst[:, 1024:T], PS[R40, 3 * n + 2, 0:P]).then_inc(dve_own.sem, dve_own.one())
                dve.wait_ge(dve_own.sem, dve_own.n)
                dve.wait_ge(loaded.sem, loaded.at(16))
                for d in range(2):
                    r = slice(32 * d, 32 * d + 8)
                    way = slice(None, None, 1 if d == 0 else -1)
                    for a, b, m0 in ((0, CTX, 0.0), (CTX, T, vecs("m0")[r, :])):
                        nc.vector.tensor_tensor_scan(M[r, a:b][:, way], LF[r, a:b][:, way], LI[r, a:b][:, way],
                                                                    m0, op0=ALU.add, op1=ALU.max).then_inc(dve_own.sem, dve_own.one())
                    nc.vector.tensor_tensor_scan(CU[r, :][:, way], RST[r, :][:, way], LF[r, :][:, way], 0.0,
                                                                op0=ALU.mult, op1=ALU.add).then_inc(dve_own.sem, dve_own.one())
                dve.wait_ge(dve_own.sem, dve_own.n)
                m3, c3 = seq3(M), seq3(CU)
                nc.vector.tensor_copy(MP[0:8, 1:2], vecs("m0")[0:8, :]).then_inc(dve_own.sem, dve_own.one())
                nc.vector.tensor_copy(MP[0:8, 2:9], m3[0:8, 1:8, P - 1]).then_inc(dve_own.sem, dve_own.one())
                nc.vector.tensor_copy(MP[32:40, 8:9], vecs("m0")[32:40, :]).then_inc(dve_own.sem, dve_own.one())
                nc.vector.tensor_copy(MP[32:40, 1:8], m3[32:40, 2:9, 0]).then_inc(dve_own.sem, dve_own.one())
                for dst, src in ((ML, m3), (CL, c3)):
                    nc.vector.tensor_copy(dst[0:32, :], src[0:32, :, P - 1]).then_inc(dve_own.sem, dve_own.one())
                    nc.vector.tensor_copy(dst[32:40, :], src[32:40, :, 0]).then_inc(dve_own.sem, dve_own.one())
                chained(nc.vector.tensor_tensor(A, LI, CU, ALU.subtract))
                chained(nc.vector.tensor_tensor(B, CU, M, ALU.subtract))
                chained(nc.vector.tensor_tensor(DL, CL, ML, ALU.subtract))
                nc.vector.tensor_tensor(WC, DL, MP, ALU.add).then_inc(dve_own.sem, dve_own.one())
                nc.vector.tensor_tensor(seq3(WI), seq3(B), MP.unsqueeze(2).broadcast_to((ROWS, NT, P)), ALU.add).then_inc(dve_own.sem, dve_own.one())
                nc.vector.tensor_tensor(seq3(WK), seq3(A), DL.unsqueeze(2).broadcast_to((ROWS, NT, P)), ALU.add).then_inc(dve_own.sem, dve_own.one())
                dve.wait_ge(dve_own.sem, dve_own.n)
                dve.sem_inc(logs_ready.sem, 1)
                dve.wait_ge(exps_ready.sem, exps_ready.at(1))
                nc.vector.tensor_scalar(WI, WI, MQ ** -0.5, None, ALU.mult).then_inc(dve_own.sem, dve_own.one())
                nc.vector.tensor_tensor(WX, WC.unsqueeze(1).broadcast_to((ROWS, 8, NT)),
                                                       PAIR.unsqueeze(2).broadcast_to((ROWS, 8, NT)), ALU.mult).then_inc(dve_own.sem, dve_own.one())
                dve.wait_ge(dve_own.sem, dve_own.n)
                dve.sem_inc(rows_ready.sem, 1)
                dve.wait_ge(rows_back.sem, rows_back.at(1))
                for b in range(3):
                    nc.vector.tensor_copy(TA[:, 3 * b:3 * b + 3, :, :].rearrange("p t n r -> p (t n r)"), PS[:, b, 0:480])
                nc.vector.tensor_copy(WCB.rearrange("p d b t -> p (d b t)"), PS[:, 3, 0:72])

            @block.scalar
            def _(act):
                softplus_act(act, xf.rearrange("p t c -> p (t c)"), g_s)
                act.wait_ge(logs_ready.sem, logs_ready.at(1))
                act.activation(WI, WI, ACT.Exp).then_inc(act_own.sem, act_own.one())
                act.activation(WK, WK, ACT.Exp).then_inc(act_own.sem, act_own.one())
                act.activation(EN, M, ACT.Exp, scale=-1.0).then_inc(act_own.sem, act_own.one())
                act.activation(WC, WC, ACT.Exp).then_inc(act_own.sem, act_own.one())
                act.wait_ge(act_own.sem, act_own.n)
                act.sem_inc(exps_ready.sem, 1)

            @block.tensor
            def _(pe):
                pe.wait_ge(gates_ready.sem, gates_ready.at(1))
                for n in range(2):
                    for t in range(NT):
                        mm = nc.tensor.transpose(PS[R40, 3 * n + t // 4, (t % 4) * P:(t % 4 + 1) * P], tokG[:, n, t, :], ident)
                mm.then_inc(rows_turned.sem, 1)
                pe.wait_ge(rows_ready.sem, rows_ready.at(1))
                for t in range(NT):
                    for n, r in enumerate((A, WI, EN, WK)):
                        nc.tensor.transpose(PS[:, t // 3, ((t % 3) * 4 + n) * ROWS:((t % 3) * 4 + n + 1) * ROWS],
                                            r[:, t * P:(t + 1) * P], ident[R40, R40])
                nc.tensor.matmul(PS[:, 3, 0:72], HALF, WX.rearrange("p n t -> p (n t)"), start=True, stop=True)\
                  .then_inc(rows_back.sem, 1)
        for e, n in ((softplus_dve_part, 2), (softplus_act_part, 2), (gates_ready, 1), (rows_turned, 1), (logs_ready, 1), (exps_ready, 1), (rows_ready, 1), (rows_back, 1)):
            e.close(n)
        loaded.close(16)
        ML_out = ML

        XM = MI[:, 0:512].rearrange("p (s h i) -> p s h i", s=2, h=2)
        SW = MI[:, 512:1024].rearrange("p (s h i) -> p s h i", s=2, h=2)
        WV = MI[:, 1024:1540].rearrange("p (s h e) -> p s h e", s=2, h=2)
        IA = MI[:, 1540:2056].rearrange("p (s h e) -> p s h e", s=2, h=2)
        NU = MI[:, 2056:2314].rearrange("p (h e) -> p h e", h=2)
        den = MI[:, 2314:2318]
        msteps = [(d, 0, b) for d in range(2) for b in range(4)]
        msteps += [(d, t if d == 0 else 9 - t, b) for t in range(1, NT) for d in range(2) for b in range(4)]
        NM = len(msteps)

        with nc.Block() as block:
            @block.sync
            def _(sp):
                sp.dma_start(o_m, ML).then_inc(stored.sem, 16)
                sp.wait_ge(tail_done.sem, tail_done.at(8))
                sp.dma_start(o_mls, CST).then_inc(stored.sem, 16)
                sp.wait_ge(stored.sem, stored.at(32))
                sp.dma_start(CST, mls0).then_inc(loaded.sem, 16)

            @block.gpsimd
            def _(pool):
                for n, (d, t, b) in enumerate(msteps):
                    if n >= 2:
                        pool.wait_ge(memory_summed.sem, memory_summed.at(n - 1))
                    wk = TA[:, t, 3, 32 * d + 2 * b:32 * d + 2 * b + 2]
                    nc.gpsimd.tensor_tensor(WV[:, n % 2, :, :], v1[:, t, 2 * b:2 * b + 2, :],
                                            wk.unsqueeze(2).broadcast_to((P, 2, V1)), ALU.mult).then_inc(values_weighted.sem, 1)

            @block.tensor
            def _(pe):
                def exponents(n):
                    d, t, b = msteps[n]
                    if n >= 2:
                        pe.wait_ge(exponents_masked.sem, exponents_masked.at(n - 1))
                    for h in range(2):
                        mm = nc.tensor.matmul(PS[:, n % 2, h * P:(h + 1) * P], SEL[:, 8 * d + 2 * b + h, :],
                                              B[:, t * P:(t + 1) * P], start=True, stop=True)
                    mm.then_inc(exponents_done.sem, 1)

                def scores(n):
                    d, t, b = msteps[n]
                    if n >= 1:
                        pe.wait_ge(scores_weighted.sem, scores_weighted.at(n))
                    for h in range(2):
                        r = slice(64 * h, 64 * h + 64)
                        mm = nc.tensor.matmul(PS[:, 2 + h, 0:P], kT[r, b, t * P:(t + 1) * P], qT[r, b, t * P:(t + 1) * P],
                                              start=True, stop=True)
                    mm.then_inc(qk_done.sem, 1)

                exponents(0)
                scores(0)
                for n, (d, t, b) in enumerate(msteps):
                    if n + 1 < NM:
                        exponents(n + 1)
                    pe.wait_ge(scores_weighted.sem, scores_weighted.at(n + 1))
                    if n >= 1:
                        pe.wait_ge(intra_taken.sem, intra_taken.at(n))
                    for h in range(2):
                        mm = nc.tensor.matmul(PS[:, 4, h * V1:(h + 1) * V1], SW[:, n % 2, h, :], v1[:, t, 2 * b + h, :],
                                              start=True, stop=True)
                    mm.then_inc(intra_summed.sem, 1)
                    if n + 1 < NM:
                        scores(n + 1)
                    if n >= 1:
                        pe.wait_ge(tail_done.sem, tail_done.at(n))
                    if n >= 8:
                        if n == 8:
                            pe.wait_ge(loaded.sem, loaded.at(16))
                        for h in range(2):
                            r = slice(64 * h, 64 * h + 64)
                            nc.tensor.matmul(PS[:, 5 + h, 0:V1], qT[r, b, t * P:(t + 1) * P], CST[r, d, b, :],
                                             start=True, stop=True)
                    pe.wait_ge(values_weighted.sem, values_weighted.at(n + 1))
                    for h in range(2):
                        mm = nc.tensor.matmul(PS[64 * h:64 * h + 64, 7, 0:V1], ktok[:, t, (2 * b + h) * MQ:(2 * b + h + 1) * MQ],
                                              WV[:, n % 2, h, :], start=True, stop=True)
                    mm.then_inc(memory_summed.sem, 1)

            @block.scalar
            def _(act):
                def weights(n):
                    d, t, b = msteps[n]
                    act.wait_ge(exponents_masked.sem, exponents_masked.at(n + 1))
                    for h in range(2):
                        c = 32 * d + 2 * b + h
                        ins = act.activation(XM[:, n % 2, h, :], XM[:, n % 2, h, :], ACT.Exp, bias=TA[:, t, 0, c:c + 1])
                        if h == 0:
                            ins.then_inc(act_own.sem, act_own.one())
                    act.wait_ge(act_own.sem, act_own.n)
                    ins.then_inc(exp_ready.sem, 1)

                weights(0)
                for n in range(NM):
                    if n + 1 < NM:
                        weights(n + 1)
                    act.wait_ge(intra_summed.sem, intra_summed.at(n + 1))
                    if n >= 2:
                        act.wait_ge(tail_done.sem, tail_done.at(n - 1))
                    act.activation(IA[:, n % 2, :, :].rearrange("p h e -> p (h e)"), PS[:, 4, 0:2 * V1], ACT.Copy)\
                       .then_inc(intra_taken.sem, 1)

            @block.vector
            def _(dve):
                def masked(n):
                    d = msteps[n][0]
                    dve.wait_ge(exponents_done.sem, exponents_done.at(n + 1))
                    if n >= 2:
                        dve.wait_ge(scores_weighted.sem, scores_weighted.at(n - 1))
                    nc.vector.tensor_tensor(XM[:, n % 2, :, :], PS[:, n % 2, 0:256].rearrange("p (h i) -> p h i", h=2),
                                            const(("neg_f", "neg_b")[d]).unsqueeze(1).broadcast_to((P, 2, P)), ALU.add)\
                      .then_inc(exponents_masked.sem, 1)

                def weighted(n):
                    dve.wait_ge(qk_done.sem, qk_done.at(n + 1))
                    dve.wait_ge(exp_ready.sem, exp_ready.at(n + 1))
                    if n >= 2:
                        dve.wait_ge(intra_summed.sem, intra_summed.at(n - 1))
                    nc.vector.scalar_tensor_tensor(out=SW[:, n % 2, :, :], in0=PS[:, 2:4, 0:P], scalar=MQ ** -0.5,
                                                   in1=XM[:, n % 2, :, :], op0=ALU.mult, op1=ALU.mult).then_inc(scores_weighted.sem, 1)

                def tail(n):
                    d, t, b = msteps[n]
                    c = 32 * d + 2 * b
                    dve.wait_ge(intra_taken.sem, intra_taken.at(n + 1))
                    dve.wait_ge(memory_summed.sem, memory_summed.at(n + 1))
                    if n >= 8:
                        for h in range(2):
                            nc.vector.scalar_tensor_tensor(
                                out=NU[:, h, :], in0=PS[:, 5 + h, 0:V1], scalar=TA[:, t, 1, c + h:c + h + 1],
                                in1=IA[:, n % 2, h, :], op0=ALU.mult, op1=ALU.add).then_inc(dve_own.sem, dve_own.one())
                        dve.wait_ge(dve_own.sem, dve_own.n)
                        nc.vector.scalar_tensor_tensor(out=CST[:, d, b, :], in0=CST[:, d, b, :],
                                                                      scalar=WCB[:, d, b, t:t + 1], in1=PS[:, 7, 0:V1],
                                                                      op0=ALU.mult, op1=ALU.add).then_inc(dve_own.sem, dve_own.one())
                        nu = NU
                    else:
                        nc.vector.tensor_copy(CST[:, d, b, :], PS[:, 7, 0:V1]).then_inc(dve_own.sem, dve_own.one())
                        nu = IA[:, n % 2, :, :]
                    dd, rd = den[:, 0:2], den[:, 2:4]
                    nc.vector.scalar_tensor_tensor(out=dd, in0=nu[:, :, MV], scalar=-1.0, in1=nu[:, :, MV],
                                                                  op0=ALU.mult, op1=ALU.max).then_inc(dve_own.sem, dve_own.one())
                    dve.wait_ge(dve_own.sem, dve_own.n)
                    nc.vector.tensor_tensor(dd, dd, TA[:, t, 2, c:c + 2], ALU.max).then_inc(dve_own.sem, dve_own.one())
                    dve.wait_ge(dve_own.sem, dve_own.n)
                    nc.vector.reciprocal(rd, dd).then_inc(dve_own.sem, dve_own.one())
                    dve.wait_ge(dve_own.sem, dve_own.n)
                    for h in range(2):
                        y = ytok[:, t, (2 * b + h) * MV:(2 * b + h + 1) * MV]
                        if t == 0 and d == 0 or t > 0 and (d == 0) == (t <= 4):
                            ins = nc.vector.tensor_scalar(y, nu[:, h, 0:MV], rd[:, h:h + 1], None, ALU.mult)
                        else:
                            ins = nc.vector.scalar_tensor_tensor(out=y, in0=nu[:, h, 0:MV], scalar=rd[:, h:h + 1], in1=y,
                                                                 op0=ALU.mult, op1=ALU.add)
                        ins.then_inc(dve_own.sem, dve_own.one())
                    dve.wait_ge(dve_own.sem, dve_own.n)
                    dve.sem_inc(tail_done.sem, 1)
                    if n == 7:
                        dve.wait_ge(loaded.sem, loaded.at(16))

                masked(0)
                for n in range(NM):
                    weighted(n)
                    if n + 1 < NM:
                        masked(n + 1)
                    if n >= 1:
                        tail(n - 1)
                tail(NM - 1)
        stored.close(32)
        loaded.close(16)
        for e in (exponents_done, exponents_masked, qk_done, exp_ready, scores_weighted, intra_taken, memory_summed, tail_done, values_weighted, intra_summed):
            e.close(NM)

        gate(1, S_OUTO)
        out_projection(1, S_OUTO, 2, [f0k[:, b, :] for b in range(8)], S_W1O)
        norm(1, 1)
        mlp(1, S_W1O, NSLOT)
        norm(1, 2)


def kernel(**inputs):
    import numpy as _np
    import concourse.bacc as _bacc
    from concourse import mybir as _mybir
    from concourse.bass_utils import run_bass_kernel_spmd as _run

    a = {k: _np.asarray(v) for k, v in inputs.items()}
    f32 = _np.float32

    def fm(x):
        return x.reshape(x.shape[0], -1, P).transpose(2, 1, 0)

    def cols(x):
        return x.reshape(-1, P).T

    def kslots(w, n):
        k = w.shape[0] // P
        return w.reshape(k, P, -1, n).transpose(2, 1, 0, 3).reshape(-1, P, k * n)

    def rows(x):
        return _np.broadcast_to(x.reshape(1, -1), (P, x.size))

    m0 = _np.zeros((P, 1), f32)
    m0[0:8, 0] = a["state_mlstm_m"][0, 0, 0]
    m0[32:40, 0] = a["state_mlstm_m"][0, 0, 1]
    parts = {
        "cond": fm(_np.concatenate([a["c_ctx"][None], a["c"]], 0)).reshape(P, -1),
        "b_mod": cols(a["b_mod"]), "norm_mix": cols(a["norm_mix"]), "norm_ffn": cols(a["norm_ffn"]),
        "norm_f": cols(a["norm_f"]), "ssd_norm": cols(a["ssd_norm"][0]),
        "cw": fm(a["ssd_conv_w"][0]).reshape(P, -1), "cb": cols(a["ssd_conv_b"][0]),
        "mw": fm(a["ml_conv_w"][0]).reshape(P, -1), "mb": cols(a["ml_conv_b"][0]),
        "dt_bias": rows(a["ssd_dt_bias"][0]), "a_log": rows(a["ssd_a_log"][0]), "ssd_d": rows(a["ssd_d"][0]),
        "gate_b": rows(a["ml_gate_b"][0]), "m0": m0,
    }
    vec = _np.concatenate([parts[k] for k in VECS], 1)

    wi, wo = a["w_in_even"][0], a["w_in_odd"][0]
    out_e = _np.zeros((4, P, 4096), f32)
    out_e[:, :, 0:3072] = kslots(a["w_out_even"][0], 256)
    slots = [kslots(a["w_mod"][0], 512), kslots(a["w_mod"][1], 512),
             kslots(wi[:, 0:1536], 512), kslots(wi[:, 1536:2560], 512), kslots(wi[:, 2560:4096], 512), out_e,
             kslots(a["w_ff1"][0], 512), kslots(wo[:, 0:3072], 512), kslots(a["w_out_odd"][0], 512),
             kslots(a["w_ff1"][1], 512)]
    wslots = _np.concatenate(slots, 0)
    w2 = a["w_ff2"].reshape(2 * NG, 4, P, D).transpose(0, 2, 1, 3).reshape(2 * NG, P, 4096)
    wsmall = _np.stack([kslots(wi[:, 4096:4128], 32)[0], kslots(wo[:, 3072:3104], 32)[0]], 1).reshape(P, 2, KD, 32)

    r = _np.arange(1, 15)[None, :, None]
    half = (_np.arange(P) // 64)[:, None, None]
    c = (_np.arange(P) % 64)[:, None, None]
    cc = _np.clip(_np.arange(64)[None, None, :] - c + 15, 0, 30)
    rpbT = a["na_rpb"][0][:, r - half, cc]

    kc = a["cache_na_k"][0, 0].reshape(4, 2, CTX, HD).transpose(1, 3, 0, 2).reshape(P, 4, CTX)
    vc = a["cache_na_v"][0, 0].transpose(1, 0, 2).reshape(CTX, 512)
    ssd0 = a["state_ssd"][0, 0].transpose(3, 0, 1, 2).reshape(SN, 2, SH * SP)
    mc = a["state_mlstm_c"][0, 0].reshape(2, 4, 2, MV, MQ).transpose(2, 4, 0, 1, 3)
    mn = a["state_mlstm_n"][0, 0].reshape(2, 4, 2, MQ).transpose(2, 3, 0, 1)[..., None]
    mls0 = _np.concatenate([mc, mn], -1).reshape(P, 2, 4, V1)
    xT = fm(_np.concatenate([a["x_prompt"][0], a["x_sample"][0]], 0)).reshape(P, -1)

    given = {"xT": xT, "vec": vec, "consts": row_consts(), "wslots": wslots, "w2": w2, "wsmall": wsmall, "rpbT": rpbT,
             "kcT": kc, "vc": vc, "ssd0": ssd0, "mls0": mls0}
    nc = _bacc.Bacc("TRN2", target_bir_lowering=False, num_devices=1)
    arrays, args = {}, []
    for name, x in given.items():
        x = _np.ascontiguousarray(x)
        arrays[f"in_{name}"] = x
        args.append(nc.dram_tensor(f"in_{name}", x.shape, _mybir.dt.from_np(x.dtype), kind="ExternalInput").ap())
    outs = {"y": (P, KD, T), "k": (P, 4, CTX), "v": (CTX, 512), "ssd": (SN, 2, SH * SP), "mls": (P, 2, 4, V1), "m": (ROWS, NT)}
    for name, shape in outs.items():
        args.append(nc.dram_tensor(f"out_{name}", shape, _mybir.dt.float32, kind="ExternalOutput").ap())
    hybrid_step(nc, *args)
    r = _run(nc, [arrays], core_ids=[0]).results[0]

    y = r["out_y"].transpose(2, 1, 0).reshape(T, D)
    nk = r["out_k"].reshape(2, HD, 4, CTX).transpose(2, 0, 3, 1).reshape(1, 1, NH, CTX, HD)
    nv = r["out_v"].reshape(CTX, NH, HD).transpose(1, 0, 2).reshape(1, 1, NH, CTX, HD)
    ns = r["out_ssd"].reshape(SN, 2, SH, SP).transpose(1, 2, 3, 0).reshape(1, 1, 2, SH, SP, SN)
    m = r["out_mls"].reshape(2, MQ, 2, 4, V1).transpose(2, 3, 0, 4, 1).reshape(2, MH, V1, MQ)
    nm = _np.stack([r["out_m"][0:8, 0], r["out_m"][32:40, 0]], 0).reshape(1, 1, 2, MH)
    return (y[None, 0:CTX], y[None, CTX:T], nk, nv, ns, m[:, :, 0:MV, :].reshape(1, 1, 2, MH, MV, MQ),
            m[:, :, MV, :].reshape(1, 1, 2, MH, MQ), nm)
```

```python
import numpy as np

import concourse.bass as bass
from concourse import mybir
from contextlib import ExitStack

F32 = mybir.dt.float32
F32R = mybir.dt.float32r
ALU = mybir.AluOpType
ACT = mybir.ActivationFunctionType
AX = mybir.AxisListType

P = 128
D = 1024
KD = D // P
CTX, LAT = 128, 1024
T = CTX + LAT
NT = T // P
TC = 384
NC = T // TC
EPS = 1e-6
FF = 4 * D
NH, HD = 8, 64
SH, SP, SN = 16, 64, 128
MH, MQ, MV = 8, 64, 128
V1 = MV + 1
ROWS = 40
NEG = -1e30
SEGS = [(0, 128, 0, 0), (128, 384, 1, 0), (384, 768, 1, 1), (768, 1152, 1, 2)]

CONSTS = {}


def const_table():
    k = np.arange(P)[:, None]
    i = np.arange(P)[None, :]
    parts = {
        "ident": (k == i) * 1.0,
        "ones": np.ones((P, P)),
        "le": (k <= i) * 1.0,
        "ge": (k >= i) * 1.0,
        "gt": (k > i) * 1.0,
        "lt": (k < i) * 1.0,
        "neg_f": np.where(k <= i, 0.0, NEG),
        "neg_b": np.where(k >= i, 0.0, NEG),
    }
    c = np.arange(P) % 64
    start = np.clip(c - 8, 0, 48)
    cc = np.arange(64)[None, :]
    parts["col"] = np.where((cc >= start[:, None]) & (cc < start[:, None] + 16), 0.0, NEG)
    sel = np.zeros((P, 16, P))
    for d in range(2):
        for h in range(8):
            sel[32 * d + h, 8 * d + h, :] = 1.0
    parts["sel"] = sel.reshape(P, -1)
    reset = np.ones((P, NT, P))
    reset[0:8, :, 0] = 0.0
    reset[32:40, :, P - 1] = 0.0
    parts["reset"] = reset.reshape(P, -1)
    at, cols = 0, []
    for name, a in parts.items():
        CONSTS[name] = (at, a.shape[1])
        at += a.shape[1]
        cols.append(a)
    return np.concatenate(cols, 1).astype(np.float32)


def row_consts():
    base = const_table()
    row = np.arange(P)[:, None]
    m = np.arange(P)[None, :]
    half = (row % 2 == m // 64) * 1.0
    n = np.arange(8)[None, :]
    pair = (row // 32 == n // 4) & (row % 32 // 2 == n % 4)
    return np.concatenate([base, half.astype(np.float32), pair.astype(np.float32)], 1)


const_table()
NCONST = 8 * P + 64

VECS = {}
for _name, _n in [("cond", 16), ("b_mod", 96), ("norm_mix", 16), ("norm_ffn", 16), ("norm_f", 8), ("ssd_norm", 8),
                  ("cw", 36), ("cb", 12), ("mw", 24), ("mb", 8), ("dt_bias", 32), ("a_log", 32), ("ssd_d", 16),
                  ("gate_b", 32), ("m0", 1)]:
    VECS[_name] = (sum(n for _, n in VECS.values()), _n)
NVEC = sum(n for _, n in VECS.values())

S_QKV, S_Z, S_XBC, S_OUTE, S_QK, S_VO, S_OUTO = 24, 27, 29, 32, 36, 38, 42
NSLOT = 44
GH = 256
NG = FF // GH


class Count:

    def __init__(self, sem):
        self.sem, self.base = sem, 0

    def at(self, n):
        return self.base + n

    def close(self, n):
        self.base += n


class Chain:

    def __init__(self, sem):
        self.sem, self.n = sem, 0

    def one(self):
        self.n += 1
        return 1


def hybrid_step(nc, xT, vec, consts, wslots, wff, wsmall, rpbT, kcT, vc, ssd0, mls0, yT, o_k, o_v, o_ssd, o_mls, o_m):
    ctx = ExitStack()
    with ctx:
        def sb(name, shape):
            return ctx.enter_context(nc.sbuf_tensor(name, shape, F32))

        def count(name):
            return Count(ctx.enter_context(nc.semaphore(name)))

        XT = sb("XT", [P, 9288])
        CO = sb("CO", [P, NCONST])
        VE = sb("VE", [P, NVEC])
        WS = sb("WS", [P, 2, KD, 32])
        MOD = sb("MOD", [P, 2, 48, 2])
        GM = sb("GM", [P, 2, 2, KD, 2])
        SM = sb("SM", [P, 1472])

        mixer = ExitStack()

        def mixer_tensor(name, shape):
            return mixer.enter_context(nc.sbuf_tensor(name, shape, F32))

        HT = mixer_tensor("HT", [P, 9216])
        F0 = mixer_tensor("F0", [P, 9216])
        F1 = mixer_tensor("F1", [P, 9216])
        WR = mixer_tensor("WR", [P, 2, 4096])
        MI = mixer_tensor("MI", [P, 4096])
        PS = ctx.enter_context(nc.psum_tensor("PS", [P, 8, 512], F32))

        x_spill = nc.dram_tensor("x_spill", (P, 9216), F32).ap()
        z_spill = nc.dram_tensor("z_spill", (NT, P, D), F32).ap()

        def const(name):
            a, n = CONSTS[name]
            return CO[:, a:a + n]

        def vecs(name):
            a, n = VECS[name]
            return VE[:, a:a + n]

        ident, ones = const("ident"), const("ones")
        xk = XT[:, 0:9216].rearrange("p (k t) -> p k t", k=KD)
        hk = HT[:, :].rearrange("p (k t) -> p k t", k=KD)
        f0k = F0[:, :].rearrange("p (k t) -> p k t", k=8)

        w_ready = [count("w_ready0"), count("w_ready1")]
        w_used = count("w_used")
        unit_loaded = [count("unit_loaded0"), count("unit_loaded1")]
        unit_hi = count("unit_hi")
        unit_split = count("unit_split")
        up_done, up_taken = count("up_done"), count("up_taken")
        down_done, down_taken = count("down_done"), count("down_taken")
        squared, hidden_hi, hidden_split = count("squared"), count("hidden_hi"), count("hidden_split")
        shifted, high_ready, low_ready = count("shifted"), count("high_ready"), count("low_ready")
        tile_done = count("tile_done")
        tile_free = count("tile_free")
        first_in = count("first_in")
        spilled = count("spilled")
        xback = count("xback")
        stored = count("stored")
        loaded = count("loaded")
        cond_silu = count("cond_silu")
        squares_ready = count("squares_ready")
        squares_summed = count("squares_summed")
        mean_ready = count("mean_ready")
        rms_ready = count("rms_ready")
        scaled_ready = count("scaled_ready")
        scores_taken = count("scores_taken")
        scores_done = count("scores_done")
        max_ready = count("max_ready")
        probs_ready = count("probs_ready")
        probs_turned = count("probs_turned")
        probsT_ready = count("probsT_ready")
        values_summed = count("values_summed")
        output_taken = count("output_taken")
        bias_ready = count("bias_ready")
        attn_turned = count("attn_turned")
        attn_taken = count("attn_taken")
        borders_zero = count("borders_zero")
        conv_done = count("conv_done")
        silu_done = count("silu_done")
        block_turned = count("block_turned")
        turned_taken = count("turned_taken")
        softplus_dve_part = count("softplus_dve_part")
        softplus_act_part = count("softplus_act_part")
        decay_ready = count("decay_ready")
        decay_summed = count("decay_summed")
        cb_done = count("cb_done")
        cb_masked = count("cb_masked")
        masked_decay_ready = count("masked_decay_ready")
        decays_summed = count("decays_summed")
        decays_taken = count("decays_taken")
        x_scaled = count("x_scaled")
        state_read = count("state_read")
        weights_ready = count("weights_ready")
        chunk_summed = count("chunk_summed")
        step_taken = count("step_taken")
        update_summed = count("update_summed")
        gated = count("gated")
        square_sum_ready = count("square_sum_ready")
        gate_mean_ready = count("gate_mean_ready")
        gate_rms_ready = count("gate_rms_ready")
        gate_scaled = count("gate_scaled")
        mix_turned = count("mix_turned")
        mix_taken = count("mix_taken")
        gates_ready = count("gates_ready")
        rows_turned = count("rows_turned")
        logs_ready = count("logs_ready")
        exps_ready = count("exps_ready")
        rows_ready = count("rows_ready")
        rows_back = count("rows_back")
        exponents_done = count("exponents_done")
        exponents_masked = count("exponents_masked")
        qk_done = count("qk_done")
        exp_ready = count("exp_ready")
        scores_weighted = count("scores_weighted")
        intra_taken = count("intra_taken")
        memory_summed = count("memory_summed")
        tail_done = count("tail_done")
        values_weighted = count("values_weighted")
        intra_summed = count("intra_summed")
        z_stage = [count(f"z_stage{n}") for n in range(4)]
        bias_loaded = [count(f"bias_loaded{n}") for n in range(2)]
        gate_loaded = [count(f"gate_loaded{n}") for n in range(2)]
        dve_own = Chain(count("dve_own").sem)
        act_own = Chain(count("act_own").sem)
        pool_own = Chain(count("pool_own").sem)

        fed = [0]

        free_at = {n: (w_used.sem, n + 1) for n in range(S_QKV)}

        def feed(sp, upto):
            while fed[0] < upto:
                n = fed[0]
                if n >= 2:
                    sp.wait_ge(*free_at[n - 2])
                cols = 3072 if S_OUTE <= n < S_QK else 4096
                sp.dma_start(WR[:, n % 2, 0:cols], wslots[n, :, 0:cols]).then_inc(w_ready[n % 2].sem, 16)
                fed[0] += 1

        def landed(n):
            return w_ready[n % 2].sem, 16 * (n // 2 + 1)

        with nc.Block() as block:
            @block.sync
            def _(sp):
                sp.dma_start(VE[:, :], vec).then_inc(first_in.sem, 16)
                sp.dma_start(CO[:, :], consts[:, 0:NCONST]).then_inc(first_in.sem, 16)
                feed(sp, 2)
                sp.dma_start(WS[:, :, :, :], wsmall).then_inc(first_in.sem, 16)
                sp.dma_start(XT[:, 0:9216], xT).then_inc(first_in.sem, 16)

            @block.scalar
            def _(act):
                act.wait_ge(first_in.sem, 64)
                act.activation(SM[:, 0:16], vecs("cond"), ACT.Silu).then_inc(cond_silu.sem, 1)
        cond_silu.close(1)
        condT = SM[:, 0:16].rearrange("p (k c) -> p k c", k=KD)

        with nc.Block() as block:
            @block.sync
            def _(sp):
                with sp.Fori(2, 24, 2) as n:
                    for s in range(2):
                        sp.wait_ge(w_used.sem, n + s - 1)
                        sp.dma_start(WR[:, s, :], wslots[bass.ds(n + s, 1), :, :].rearrange("a p n -> p (a n)"))\
                          .then_inc(w_ready[s].sem, 16)
                fed[0] = 24
                feed(sp, S_QKV)

            @block.tensor
            def _(pe):
                with pe.Fori(0, 12) as i:
                    for s in range(2):
                        pe.wait_ge(w_ready[s].sem, i * 16 + 16)
                        w = WR[:, s, :].rearrange("p (k n) -> p k n", k=KD)
                        for j in range(4):
                            for k in range(KD):
                                mm = nc.tensor.matmul(PS[:, 0, bass.ds(i * 16 + (s * 8 + j * 2), 2)],
                                                      w[:, k, j * P:(j + 1) * P], condT[:, k, :],
                                                      start=(k == 0), stop=(k == KD - 1))
                        mm.then_inc(w_used.sem, 1)

            @block.vector
            def _(dve):
                dve.wait_ge(w_used.sem, 24)
                b = vecs("b_mod").rearrange("p (l j) -> p l j", l=2)
                raw = PS[:, 0, 0:192].rearrange("p (l j c) -> p l j c", l=2, c=2)
                for c in range(2):
                    nc.vector.tensor_tensor(MOD[:, :, :, c], raw[:, :, :, c], b, ALU.add).then_inc(dve_own.sem, dve_own.one())
                dve.wait_ge(dve_own.sem, dve_own.n)
                for l in range(2):
                    for n, name in enumerate(("norm_mix", "norm_ffn")):
                        g = vecs(name).rearrange("p (l k) -> p l k", l=2)[:, l, :]
                        for c in range(2):
                            nc.vector.scalar_tensor_tensor(out=GM[:, l, n, :, c],
                                                           in0=MOD[:, l, (3 * n + 1) * 8:(3 * n + 1) * 8 + 8, c],
                                                           scalar=1.0, in1=g, op0=ALU.add, op1=ALU.mult)

        def norm(l, which, dst, SQ, RB, upto, split=None, final=False):
            with nc.Block() as block:
                @block.sync
                def _(sp):
                    if final:
                        for s, (a, b, _, _) in enumerate(SEGS):
                            sp.wait_ge(scaled_ready.sem, scaled_ready.at(KD * (s + 1)))
                            sp.dma_start(yT[:, :, a:b], dst[:, :, a:b]).then_inc(stored.sem, 16)
                        sp.wait_ge(stored.sem, stored.at(64))
                    elif upto:
                        feed(sp, upto)
                    else:
                        for s in range(2):
                            sp.dma_start(raw_unit[:, s, :], wff[l, s, :, :]).then_inc(unit_loaded[s].sem, 16)

                @block.scalar
                def _(act):
                    for i in range(NC * KD):
                        c, k = i // KD, i % KD
                        if i >= 8:
                            act.wait_ge(squares_summed.sem, squares_summed.at(i - 7))
                        act.activation(SQ[:, i % 8, :], xk[:, k, c * TC:(c + 1) * TC], ACT.Square)\
                           .then_inc(squares_ready.sem, 1)
                    for c in range(NC):
                        act.wait_ge(mean_ready.sem, mean_ready.at(c + 1))
                        act.activation(RB[:, c * TC:(c + 1) * TC], RB[:, c * TC:(c + 1) * TC], ACT.Sqrt)\
                           .then_inc(rms_ready.sem, 1)
                    if final:
                        return
                    n = 0
                    for a, b, c, _ in SEGS:
                        for k in range(KD):
                            act.wait_ge(scaled_ready.sem, scaled_ready.at(n + 1))
                            x = split[0][:, n % 4, 0:b - a] if split else dst[:, k, a:b]
                            y = split[0][:, 4 + n % 4, 0:b - a] if split else x
                            if split and n >= 4:
                                act.wait_ge(low_ready.sem, low_ready.at(n - 3))
                            act.activation(y, x, ACT.Identity, bias=MOD[:, l, 24 * which + k, c:c + 1])\
                               .then_inc(shifted.sem, 1)
                            n += 1

                @block.tensor
                def _(pe):
                    for i in range(NC * KD):
                        pe.wait_ge(squares_ready.sem, squares_ready.at(i + 1))
                        nc.tensor.matmul(PS[:, i // KD, 0:TC], ones, SQ[:, i % 8, :],
                                         start=(i % KD == 0), stop=(i % KD == KD - 1)).then_inc(squares_summed.sem, 1)

                @block.vector
                def _(dve):
                    for c in range(NC):
                        dve.wait_ge(squares_summed.sem, squares_summed.at(KD * (c + 1)))
                        r = RB[:, c * TC:(c + 1) * TC]
                        nc.vector.tensor_scalar(r, PS[:, c, 0:TC], 1.0 / D, EPS, ALU.mult, ALU.add)\
                          .then_inc(dve_own.sem, dve_own.one())
                        dve.wait_ge(dve_own.sem, dve_own.n)
                        nc.vector.reciprocal(r, r).then_inc(mean_ready.sem, 1)

                    def high(n):
                        a, b, cond, _ = SEGS[n // KD]
                        dve.wait_ge(scaled_ready.sem, scaled_ready.at(n + 1))
                        nc.vector.tensor_scalar(split[1][:, n % KD, a:b], split[0][:, n % 4, 0:b - a],
                                                MOD[:, l, 24 * which + n % KD, cond:cond + 1], None, ALU.add)\
                          .then_inc(high_ready.sem, 1)

                    n = 0
                    for a, b, cond, c in SEGS:
                        dve.wait_ge(rms_ready.sem, rms_ready.at(c + 1))
                        for k in range(KD):
                            if split and n >= 4:
                                dve.wait_ge(shifted.sem, shifted.at(n - 3))
                            g = vecs("norm_f")[:, k:k + 1] if final else GM[:, l, which, k, cond:cond + 1]
                            y = split[0][:, n % 4, 0:b - a] if split else dst[:, k, a:b]
                            nc.vector.scalar_tensor_tensor(out=y, in0=xk[:, k, a:b], scalar=g,
                                                           in1=RB[:, a:b], op0=ALU.mult, op1=ALU.mult)\
                              .then_inc(scaled_ready.sem, 1)
                            if split and n >= 1:
                                high(n - 1)
                            n += 1
                    if split:
                        high(n - 1)

                @block.gpsimd
                def _(pool):
                    if split:
                        for n in range(4 * KD):
                            a, b, _, _ = SEGS[n // KD]
                            pool.wait_ge(shifted.sem, shifted.at(n + 1))
                            pool.wait_ge(high_ready.sem, high_ready.at(n + 1))
                            nc.gpsimd.tensor_tensor(split[2][:, n % KD, a:b], split[0][:, 4 + n % 4, 0:b - a],
                                                    split[1][:, n % KD, a:b].bitcast(F32), ALU.subtract)\
                              .then_inc(low_ready.sem, 1)
            squares_ready.close(24)
            squares_summed.close(24)
            mean_ready.close(NC)
            rms_ready.close(NC)
            scaled_ready.close(4 * KD)
            if final:
                stored.close(64)
            else:
                shifted.close(4 * KD)
            if split:
                high_ready.close(4 * KD)
                low_ready.close(4 * KD)

        def tile_products(pe, i, m, n, terms, banks=8):
            if i >= banks:
                pe.wait_ge(tile_free.sem, tile_free.at(i - banks + 1))
            for t, (lhs, rhs) in enumerate(terms):
                mm = nc.tensor.matmul(PS[0:m, i % banks, 0:n], lhs, rhs, start=(t == 0), stop=(t == len(terms) - 1))
            mm.then_inc(tile_done.sem, 1)

        def feature_tile(pe, i, w, col, c, banks=8):
            tile_products(pe, i, P, TC, [(w[:, k, col:col + P], hk[:, k, c * TC:(c + 1) * TC]) for k in range(KD)], banks)

        def token_tile(pe, i, w, t):
            tile_products(pe, i, P, 512, [(hk[:, k, t * P:(t + 1) * P], w[:, k, :]) for k in range(KD)])

        def slot_k(n):
            return WR[:, n % 2, :].rearrange("p (k n) -> p k n", k=KD)

        def frees(slots, per_slot):
            at = 0
            for n, k in zip(slots, per_slot):
                at += k
                free_at[n] = (tile_done.sem, tile_done.at(at))

        def close_tiles(n):
            tile_done.close(n)
            tile_free.close(n)

        zst = MI[:, 0:2048].rearrange("p (s n) -> p s n", s=4)

        def spill_gate_act(act, i, func):
            for z in range(2 * NT):
                act.wait_ge(tile_done.sem, tile_done.at(i + 1))
                if z >= 4:
                    act.wait_ge(z_stage[z % 4].sem, z_stage[z % 4].at(16 * (z // 4)))
                act.activation(zst[:, z % 4, :], PS[:, i % 8, :], func).then_inc(tile_free.sem, 1)
                i += 1

        def spill_gate_sp(sp, i):
            for z in range(2 * NT):
                s, t = z // NT, z % NT
                sp.wait_ge(tile_free.sem, tile_free.at(i + z + 1))
                sp.dma_start(z_spill[t, :, s * 512:(s + 1) * 512], zst[:, z % 4, :]).then_inc(z_stage[z % 4].sem, 16)
            for n in range(4):
                sp.wait_ge(z_stage[n].sem, z_stage[n].at(16 * len(range(n, 18, 4))))

        def close_gate():
            for n in range(4):
                z_stage[n].close(16 * len(range(n, 18, 4)))

        def norm_mixer(l, upto):
            norm(l, 0, hk, F1[:, 4608:7680].rearrange("p (n t) -> p n t", n=8), F1[:, 7680:7680 + T], upto)

        norm_mixer(0, S_QKV + 2)

        qT = F0[:, 0:4608].rearrange("p (b t) -> p b t", b=4)
        kT = F0[:, 4608:9216].rearrange("p (b t) -> p b t", b=4)
        vtok = F1[:, 0:4608].rearrange("p (t n) -> p t n", t=NT)
        frees(range(S_QKV, S_XBC), (12, 12, 9, 9, 9))

        with nc.Block() as block:
            @block.sync
            def _(sp):
                sp.dma_start(x_spill, XT[:, 0:9216]).then_inc(spilled.sem, 16)
                feed(sp, S_XBC)
                spill_gate_sp(sp, 33)
                feed(sp, S_XBC + 2)
                sp.wait_ge(spilled.sem, spilled.at(16))

            @block.tensor
            def _(pe):
                i = 0
                for s in range(2):
                    pe.wait_ge(*landed(S_QKV + s))
                    for b in range(4):
                        for c in range(NC):
                            feature_tile(pe, i, slot_k(S_QKV + s), b * P, c)
                            i += 1
                for s in (S_QKV + 2, S_Z, S_Z + 1):
                    pe.wait_ge(*landed(s))
                    for t in range(NT):
                        token_tile(pe, i, slot_k(s), t)
                        i += 1

            @block.scalar
            def _(act):
                i = 0
                for s in range(2):
                    for b in range(4):
                        for c in range(NC):
                            act.wait_ge(tile_done.sem, tile_done.at(i + 1))
                            act.activation((qT, kT)[s][:, b, c * TC:(c + 1) * TC], PS[:, i % 8, 0:TC], ACT.Copy,
                                           scale=(HD ** -0.5, 1.0)[s]).then_inc(tile_free.sem, 1)
                            i += 1
                for t in range(NT):
                    act.wait_ge(tile_done.sem, tile_done.at(i + 1))
                    act.activation(vtok[:, t, :], PS[:, i % 8, :], ACT.Copy).then_inc(tile_free.sem, 1)
                    i += 1
                spill_gate_act(act, i, ACT.Silu)
        close_tiles(51)
        spilled.close(16)
        close_gate()

        T2 = F1[:, 4608:6400].rearrange("p (s r c) -> p s r c", s=2, r=14)
        TI = F1[:, 6400:7552].rearrange("p (s r c) -> p s r c", s=2, r=9)
        kcT_sb = F1[:, 7552:8064].rearrange("p (b t) -> p b t", b=4)
        vc_sb = F1[:, 8064:8576]
        yna = XT[:, 0:4608].rearrange("p (t n) -> p t n", t=NT)
        SS = XT[:, 4608:6016].rearrange("p (s n) -> p s n", s=2)
        PT = XT[:, 6016:7552].rearrange("p (s n) -> p s n", s=2)
        mx, nmx, rs, ri = (XT[:, 7552 + 2 * n:7554 + 2 * n] for n in range(4))
        ynaT = F1[:, 4608:9216].rearrange("p (b t) -> p b t", b=4)
        NA = 72

        def na_step(n):
            if n >= 64:
                return n - 64, 0, False, 0, 0
            h, j = n // 8, n % 8
            s = min(max(2 * j - 4, 0), 8)
            return h, s // 2, 2 <= j <= 5, s - 2 * j + 6, 1 + j

        def width(n):
            return 128 if n >= 64 else (704 if na_step(n)[2] else 640)

        def chunks(n):
            h, kt, nine, _, _ = na_step(n)
            v = slice(h * HD, (h + 1) * HD)
            if n >= 64:
                return [(0, P, vtok[:, 0, v])]
            out = [(i * P, P, vtok[:, 1 + kt + i, v]) for i in range(4)] + [(512, P, vc_sb[:, v])]
            if nine:
                out.append((640, 64, vtok[0:64, 1 + kt + 4, v]))
            return out

        with nc.Block() as block:
            @block.sync
            def _(sp):
                sp.dma_start(kcT_sb, kcT).then_inc(loaded.sem, 16)
                sp.dma_start(vc_sb, vc).then_inc(loaded.sem, 16)
                sp.dma_start(o_k, kT[:, :, 0:P]).then_inc(stored.sem, 16)
                sp.dma_start(o_v, vtok[:, 0, :]).then_inc(stored.sem, 16)
                for h in range(NH):
                    if h >= 2:
                        sp.wait_ge(scores_taken.sem, scores_taken.at(8 * (h - 1)))
                        sp.wait_ge(bias_ready.sem, bias_ready.at(h - 1))
                    sp.dma_start(T2[:, h % 2, :, :], rpbT[h]).then_inc(bias_loaded[h % 2].sem, 16)
                sp.wait_ge(stored.sem, stored.at(32))

            @block.gpsimd
            def _(pool):
                col = const("col").unsqueeze(1)
                for h in range(NH):
                    pool.wait_ge(bias_loaded[h % 2].sem, bias_loaded[h % 2].at(16 * (h // 2 + 1)))
                    if h >= 2:
                        pool.wait_ge(scores_taken.sem, scores_taken.at(8 * (h - 1)))
                    nc.gpsimd.tensor_tensor(T2[:, h % 2, :, :], T2[:, h % 2, :, :],
                                                            col.broadcast_to((P, 14, 64)), ALU.add).then_inc(pool_own.sem, pool_own.one())
                    pool.wait_ge(pool_own.sem, pool_own.n)
                    nc.gpsimd.tensor_copy(TI[:, h % 2, :, :], T2[:, h % 2, 2:11, :]).then_inc(pool_own.sem, pool_own.one())
                    pool.wait_ge(pool_own.sem, pool_own.n)
                    nc.gpsimd.memset(TI[0:64, h % 2, 8, :], NEG).then_inc(pool_own.sem, pool_own.one())
                    nc.gpsimd.memset(TI[64:128, h % 2, 0, :], NEG).then_inc(pool_own.sem, pool_own.one())
                    pool.wait_ge(pool_own.sem, pool_own.n)
                    pool.sem_inc(bias_ready.sem, 1)

            @block.tensor
            def _(pe):
                def scores(n):
                    h, kt, nine, _, qt = na_step(n)
                    r = slice(64 * (h % 2), 64 * (h % 2) + 64)
                    q = qT[r, h // 2, qt * P:(qt + 1) * P]
                    b = 2 * (n % 2)
                    if n >= 2:
                        pe.wait_ge(scores_taken.sem, scores_taken.at(n - 1))
                    if n >= 64:
                        nc.tensor.matmul(PS[:, b, 0:P], q, kT[r, h // 2, 0:P], start=True, stop=True).then_inc(scores_done.sem, 1)
                        return
                    if n == 0:
                        pe.wait_ge(loaded.sem, loaded.at(32))
                    k0 = (1 + kt) * P
                    nc.tensor.matmul(PS[:, b, :], q, kT[r, h // 2, k0:k0 + 512], start=True, stop=True)
                    mm = nc.tensor.matmul(PS[:, b + 1, 0:P], q, kcT_sb[r, h // 2, :], start=True, stop=True)
                    if nine:
                        mm = nc.tensor.matmul(PS[:, b + 1, P:P + 64], q, kT[r, h // 2, k0 + 512:k0 + 576],
                                              start=True, stop=True)
                    mm.then_inc(scores_done.sem, 1)

                def turn(n):
                    pe.wait_ge(probs_ready.sem, probs_ready.at(n + 1))
                    if n >= 1:
                        pe.wait_ge(probsT_ready.sem, probsT_ready.at(n))
                    for i, (a, m, _) in enumerate(chunks(n)):
                        mm = nc.tensor.transpose(PS[0:m, 4 + i // 4, (i % 4) * P:(i % 4) * P + P],
                                                 SS[:, n % 2, a:a + m], ident)
                    mm.then_inc(probs_turned.sem, 1)

                def values(n):
                    pe.wait_ge(probsT_ready.sem, probsT_ready.at(n + 1))
                    if n >= 2:
                        pe.wait_ge(output_taken.sem, output_taken.at(n - 1))
                    cs = chunks(n)
                    for i, (_, m, v) in enumerate(cs):
                        mm = nc.tensor.matmul(PS[:, 6 + n % 2, 0:HD], PT[0:m, n % 2, i * P:(i + 1) * P], v,
                                              start=(i == 0), stop=(i == len(cs) - 1))
                    mm.then_inc(values_summed.sem, 1)

                scores(0)
                for n in range(NA):
                    if n + 1 < NA:
                        scores(n + 1)
                    turn(n)
                    if n >= 1:
                        values(n - 1)
                values(NA - 1)

            @block.vector
            def _(dve):
                def softmax_max(n):
                    h, _, nine, r0, _ = na_step(n)
                    b = 2 * (n % 2)
                    dve.wait_ge(scores_done.sem, scores_done.at(n + 1))
                    if n >= 2:
                        dve.wait_ge(probs_turned.sem, probs_turned.at(n - 1))
                    s = SS[:, n % 2, :]
                    if n >= 64:
                        nc.vector.tensor_copy(s[:, 0:P], PS[:, b, 0:P]).then_inc(scores_taken.sem, 1)
                    else:
                        if n % 8 == 0:
                            dve.wait_ge(bias_ready.sem, bias_ready.at(h + 1))
                        bias = (TI[:, h % 2, :, :] if nine else T2[:, h % 2, r0:r0 + 8, :]).rearrange("p r c -> p (r c)")
                        nc.vector.tensor_tensor(s[:, 0:512], PS[:, b, :], bias[:, 0:512], ALU.add).then_inc(dve_own.sem, dve_own.one())
                        if nine:
                            nc.vector.tensor_tensor(s[:, 640:704], PS[:, b + 1, P:P + 64],
                                                                   bias[:, 512:576], ALU.add).then_inc(dve_own.sem, dve_own.one())
                        dve.wait_ge(dve_own.sem, dve_own.n)
                        nc.vector.tensor_copy(s[:, 512:640], PS[:, b + 1, 0:P]).then_inc(scores_taken.sem, 1)
                    dve.wait_ge(scores_taken.sem, scores_taken.at(n + 1))
                    nc.vector.tensor_reduce(mx[:, n % 2:n % 2 + 1], s[:, 0:width(n)], AX.X, ALU.max).then_inc(dve_own.sem, dve_own.one())
                    dve.wait_ge(dve_own.sem, dve_own.n)
                    nc.vector.tensor_scalar(nmx[:, n % 2:n % 2 + 1], mx[:, n % 2:n % 2 + 1], -1.0, None, ALU.mult)\
                      .then_inc(max_ready.sem, 1)

                def normalise(n):
                    h, _, _, _, qt = na_step(n)
                    dve.wait_ge(values_summed.sem, values_summed.at(n + 1))
                    nc.vector.reciprocal(ri[:, n % 2:n % 2 + 1], rs[:, n % 2:n % 2 + 1]).then_inc(dve_own.sem, dve_own.one())
                    dve.wait_ge(dve_own.sem, dve_own.n)
                    nc.vector.tensor_scalar(yna[:, qt, h * HD:(h + 1) * HD], PS[:, 6 + n % 2, 0:HD],
                                            ri[:, n % 2:n % 2 + 1], None, ALU.mult).then_inc(output_taken.sem, 1)

                for n in range(NA):
                    softmax_max(n)
                    if n >= 2:
                        normalise(n - 2)
                normalise(NA - 2)
                normalise(NA - 1)

            @block.scalar
            def _(act):
                def probs(n):
                    act.wait_ge(max_ready.sem, max_ready.at(n + 1))
                    if n >= 2:
                        act.wait_ge(output_taken.sem, output_taken.at(n - 1))
                    s = SS[:, n % 2, 0:width(n)]
                    act.activation(s, s, ACT.Exp, bias=nmx[:, n % 2:n % 2 + 1], accum_out=rs[:, n % 2:n % 2 + 1])\
                       .then_inc(probs_ready.sem, 1)

                def take(n):
                    act.wait_ge(probs_turned.sem, probs_turned.at(n + 1))
                    if n >= 2:
                        act.wait_ge(values_summed.sem, values_summed.at(n - 1))
                    cs = chunks(n)
                    k = min(len(cs), 4) * P
                    ins = act.activation(PT[:, n % 2, 0:k], PS[:, 4, 0:k], ACT.Copy)
                    if len(cs) > 5:
                        ins = act.activation(PT[0:64, n % 2, 640:768], PS[0:64, 5, P:2 * P], ACT.Copy)
                    if len(cs) > 4:
                        ins.then_inc(act_own.sem, act_own.one())
                        ins = act.activation(PT[:, n % 2, 512:640], PS[:, 5, 0:P], ACT.Copy)
                    ins.then_inc(probsT_ready.sem, 1)

                probs(0)
                for n in range(1, NA):
                    probs(n)
                    take(n - 1)
                take(NA - 1)
        loaded.close(32)
        stored.close(32)
        bias_loaded[0].close(64)
        bias_loaded[1].close(64)
        for e in (scores_taken, scores_done, max_ready, probs_ready, probs_turned, probsT_ready, values_summed, output_taken):
            e.close(NA)
        bias_ready.close(NH)

        with nc.Block() as block:
            @block.tensor
            def _(pe):
                for t in range(NT):
                    if t >= 4:
                        pe.wait_ge(attn_taken.sem, attn_taken.at(t - 3))
                    for b in range(4):
                        mm = nc.tensor.transpose(PS[:, t % 4, b * P:(b + 1) * P], yna[:, t, b * P:(b + 1) * P], ident)
                    mm.then_inc(attn_turned.sem, 1)

            @block.scalar
            def _(act):
                for t in range(NT):
                    act.wait_ge(attn_turned.sem, attn_turned.at(t + 1))
                    act.activation(ynaT[:, :, t * P:(t + 1) * P], PS[:, t % 4, :].rearrange("p (b n) -> p b n", b=4),
                                   ACT.Copy).then_inc(attn_taken.sem, 1)
        attn_turned.close(NT)
        attn_taken.close(NT)

        def conv_phase(s0, nblocks, raw, cv, silu_out, turned, w, bias, spill_x=False):
            turns = [b for b in range(nblocks) if turned(b) is not None]
            frees(range(s0, s0 + nblocks // 4), [12] * (nblocks // 4))
            with nc.Block() as block:
                @block.sync
                def _(sp):
                    if spill_x:
                        sp.dma_start(x_spill, XT[:, 0:9216]).then_inc(spilled.sem, 16)
                        sp.wait_ge(spilled.sem, spilled.at(16))
                    feed(sp, s0 + nblocks // 4 + (2 if s0 == S_QK else 0))

                @block.gpsimd
                def _(pool):
                    for n in range(2):
                        for a, z in ((0, 1), (129, 131), (1155, 1156)):
                            nc.gpsimd.memset(raw[:, n, a:z], 0.0).then_inc(borders_zero.sem, 1)

                @block.tensor
                def _(pe):
                    def turn(b):
                        n = turns.index(b)
                        pe.wait_ge(silu_done.sem, silu_done.at(b + 1))
                        for c in range(3):
                            j = 3 * n + c
                            if j >= 3:
                                pe.wait_ge(turned_taken.sem, turned_taken.at(j - 2))
                            for t in range(3):
                                mm = nc.tensor.transpose(PS[:, 5 + j % 3, t * P:(t + 1) * P],
                                                         silu_out(b)[:, (3 * c + t) * P:(3 * c + t + 1) * P], ident)
                            mm.then_inc(block_turned.sem, 1)

                    for b in range(nblocks):
                        if b % 4 == 0:
                            pe.wait_ge(*landed(s0 + b // 4))
                        for c in range(NC):
                            feature_tile(pe, b * NC + c, slot_k(s0 + b // 4), (b % 4) * P, c, banks=5)
                        if b >= 1 and (b - 1) in turns:
                            turn(b - 1)
                    if nblocks - 1 in turns:
                        turn(nblocks - 1)

                @block.scalar
                def _(act):
                    def silu(b):
                        act.wait_ge(conv_done.sem, conv_done.at(b + 1))
                        if turned(b) is not None and turns.index(b) >= 2:
                            act.wait_ge(block_turned.sem, block_turned.at(3 * (turns.index(b) - 1)))
                        dst = silu_out(b)
                        act.activation(dst[:, 0:CTX], cv[:, b % 2, 0:CTX], ACT.Silu).then_inc(act_own.sem, act_own.one())
                        act.activation(dst[:, CTX:T], cv[:, b % 2, CTX + 2:T + 2], ACT.Silu).then_inc(silu_done.sem, 1)

                    act.wait_ge(borders_zero.sem, borders_zero.at(6))
                    for b in range(nblocks):
                        if b >= 2:
                            act.wait_ge(conv_done.sem, conv_done.at(b - 1))
                        for c in range(NC):
                            i = b * NC + c
                            act.wait_ge(tile_done.sem, tile_done.at(i + 1))
                            r = raw[:, b % 2, :]
                            if c == 0:
                                act.activation(r[:, 1:129], PS[:, i % 5, 0:CTX], ACT.Copy).then_inc(act_own.sem, act_own.one())
                                act.activation(r[:, 131:387], PS[:, i % 5, CTX:TC], ACT.Copy).then_inc(tile_free.sem, 1)
                            else:
                                act.activation(r[:, c * TC + 3:(c + 1) * TC + 3], PS[:, i % 5, 0:TC], ACT.Copy)\
                                   .then_inc(tile_free.sem, 1)
                        if b >= 1:
                            silu(b - 1)
                    silu(nblocks - 1)

                @block.vector
                def _(dve):
                    def take(b):
                        n = turns.index(b)
                        for c in range(3):
                            dve.wait_ge(block_turned.sem, block_turned.at(3 * n + c + 1))
                            nc.vector.tensor_copy(turned(b)[:, 3 * c:3 * c + 3, :],
                                                  PS[:, 5 + (3 * n + c) % 3, 0:TC].rearrange("p (t n) -> p t n", t=3))\
                              .then_inc(turned_taken.sem, 1)

                    dve.wait_ge(borders_zero.sem, borders_zero.at(6))
                    for b in range(nblocks):
                        dve.wait_ge(tile_free.sem, tile_free.at(NC * (b + 1)))
                        if b >= 2:
                            dve.wait_ge(silu_done.sem, silu_done.at(b - 1))
                        r, o = raw[:, b % 2, :], cv[:, b % 2, :]
                        nc.vector.tensor_scalar(o, r[:, 1:1155], w[:, b, 1:2], bias[:, b:b + 1],
                                                               ALU.mult, ALU.add).then_inc(dve_own.sem, dve_own.one())
                        dve.wait_ge(dve_own.sem, dve_own.n)
                        nc.vector.scalar_tensor_tensor(out=o, in0=r[:, 0:1154], scalar=w[:, b, 0:1],
                                                                      in1=o, op0=ALU.mult, op1=ALU.add).then_inc(dve_own.sem, dve_own.one())
                        dve.wait_ge(dve_own.sem, dve_own.n)
                        nc.vector.scalar_tensor_tensor(out=o, in0=r[:, 2:1156], scalar=w[:, b, 2:3],
                                                       in1=o, op0=ALU.mult, op1=ALU.add).then_inc(conv_done.sem, 1)
                        if b >= 1 and (b - 1) in turns:
                            take(b - 1)
                    if nblocks - 1 in turns:
                        take(nblocks - 1)
            close_tiles(NC * nblocks)
            borders_zero.close(6)
            conv_done.close(nblocks)
            silu_done.close(nblocks)
            block_turned.close(3 * len(turns))
            turned_taken.close(3 * len(turns))

        xs = F0[:, :].rearrange("p (t n) -> p t n", t=NT)
        bcT = F1[:, 0:4608].rearrange("p (b t) -> p b t", b=4)
        btok = XT[:, 0:2304].rearrange("p (t n) -> p t n", t=NT)
        cs = XT[:, 6924:9228].rearrange("p (s t) -> p s t", s=2)

        conv_phase(S_XBC, 12,
                   XT[:, 2304:4616].rearrange("p (s t) -> p s t", s=2), XT[:, 4616:6924].rearrange("p (s t) -> p s t", s=2),
                   lambda b: cs[:, b % 2, :] if b < 8 else bcT[:, b - 8, :],
                   lambda b: xs[:, :, b * P:(b + 1) * P] if b < 8 else (btok[:, :, (b - 8) * P:(b - 7) * P] if b < 10 else None),
                   vecs("cw").rearrange("p (b j) -> p b j", j=3), vecs("cb"))

        def softplus_dve(dve, x, out, s):
            e, u, l, d, r = (s[:, n, :] for n in range(1, 6))

            def chained(ins):
                ins.then_inc(dve_own.sem, dve_own.one())
                dve.wait_ge(dve_own.sem, dve_own.n)
            dve.wait_ge(softplus_act_part.sem, softplus_act_part.at(1))
            nc.vector.tensor_scalar(u, e, 1.0, None, ALU.add).then_inc(softplus_dve_part.sem, 1)
            dve.wait_ge(softplus_dve_part.sem, softplus_dve_part.at(2))
            chained(nc.vector.tensor_scalar(d, u, -1.0, None, ALU.add))
            chained(nc.vector.tensor_scalar(r, d, 1e-30, None, ALU.max))
            chained(nc.vector.reciprocal(r, r))
            chained(nc.vector.tensor_tensor(r, r, e, ALU.mult))
            dve.wait_ge(softplus_act_part.sem, softplus_act_part.at(2))
            chained(nc.vector.tensor_tensor(r, r, l, ALU.mult))
            chained(nc.vector.scalar_tensor_tensor(out=d, in0=d, scalar=0.0, in1=e, op0=ALU.is_equal, op1=ALU.mult))
            chained(nc.vector.tensor_tensor(d, d, r, ALU.add))
            chained(nc.vector.scalar_tensor_tensor(out=out, in0=x, scalar=0.0, in1=d, op0=ALU.max, op1=ALU.add))

        def softplus_act(act, x, s):
            a, e, u, l = (s[:, n, :] for n in range(4))
            act.wait_ge(softplus_dve_part.sem, softplus_dve_part.at(1))
            act.activation(a, x, ACT.Abs).then_inc(act_own.sem, act_own.one())
            act.wait_ge(act_own.sem, act_own.n)
            act.activation(e, a, ACT.Exp, scale=-1.0).then_inc(softplus_act_part.sem, 1)
            act.wait_ge(softplus_dve_part.sem, softplus_dve_part.at(2))
            act.activation(l, u, ACT.Ln).then_inc(softplus_act_part.sem, 1)

        def small_products(pe, l):
            for t in range(NT):
                for k in range(KD):
                    mm = nc.tensor.matmul(PS[:, 0, 32 * t:32 * t + 32], hk[:, k, t * P:(t + 1) * P], WS[:, l, k, :],
                                          start=(k == 0), stop=(k == KD - 1))
            mm.then_inc(tile_done.sem, 1)

        DT, DTA, ECUM, WEND, TOT = (SM[:, 16 + 288 * n:304 + 288 * n].rearrange("p (t c) -> p t c", t=NT) for n in range(5))
        flat = lambda a: a.rearrange("p t c -> p (t c)")
        GB = XT[:, 2304:6912].rearrange("p (t d g i) -> p t d g i", t=NT, d=2, g=2)
        ytok = HT[:, :].rearrange("p (t n) -> p t n", t=NT)
        sp_s = MI[:, 0:1728].rearrange("p (n c) -> p n c", n=6)
        negA = MI[:, 1728:1760]
        x0 = MI[:, 1760:2048]

        with nc.Block() as block:
            @block.tensor
            def _(pe):
                small_products(pe, 0)
                for t in range(NT):
                    if t >= 3:
                        pe.wait_ge(cb_masked.sem, cb_masked.at(2 * (t - 2)))
                    for g in range(2):
                        mm = nc.tensor.matmul(PS[:, 1 + t % 3, g * P:(g + 1) * P], bcT[:, g, t * P:(t + 1) * P],
                                              bcT[:, 2 + g, t * P:(t + 1) * P], start=True, stop=True)
                    mm.then_inc(cb_done.sem, 1)
                pe.wait_ge(decay_ready.sem, decay_ready.at(1))
                for bank, (f, b) in enumerate((("le", "ge"), ("gt", "lt"), ("ones", "ones"))):
                    for d, m in enumerate((f, b)):
                        mm = nc.tensor.matmul(PS[:, 4 + bank, 0:288].rearrange("p (t c) -> p t c", t=NT)[:, :, 16 * d:16 * d + 16],
                                              const(m), DTA[:, :, 16 * d:16 * d + 16], start=True, stop=True)
                mm.then_inc(decay_summed.sem, 1)

            @block.scalar
            def _(act):
                act.activation(negA, vecs("a_log"), ACT.Exp).then_inc(act_own.sem, act_own.one())
                softplus_act(act, x0, sp_s)
                act.wait_ge(decay_summed.sem, decay_summed.at(1))
                for bank, dst in enumerate((ECUM, WEND, TOT)):
                    act.activation(flat(dst), PS[:, 4 + bank, 0:288], ACT.Exp).then_inc(softplus_act_part.sem, 1)

            @block.vector
            def _(dve):
                dve.wait_ge(tile_done.sem, tile_done.at(1))
                bias = vecs("dt_bias").unsqueeze(1).broadcast_to((P, NT, 32))
                nc.vector.tensor_tensor(x0.rearrange("p (t c) -> p t c", t=NT),
                                        PS[:, 0, 0:288].rearrange("p (t c) -> p t c", t=NT), bias, ALU.add)\
                  .then_inc(softplus_dve_part.sem, 1)
                softplus_dve(dve, x0, flat(DT), sp_s)
                nc.vector.scalar_tensor_tensor(out=DTA, in0=DT, scalar=-1.0,
                                               in1=negA.unsqueeze(1).broadcast_to((P, NT, 32)),
                                               op0=ALU.mult, op1=ALU.mult).then_inc(decay_ready.sem, 1)
                for t in range(NT):
                    dve.wait_ge(cb_done.sem, cb_done.at(t + 1))
                    for d, m in enumerate(("le", "ge")):
                        nc.vector.tensor_tensor(GB[:, t, d, :, :], PS[:, 1 + t % 3, 0:256].rearrange("p (g i) -> p g i", g=2),
                                                const(m).unsqueeze(1).broadcast_to((P, 2, P)), ALU.mult).then_inc(cb_masked.sem, 1)
                dve.wait_ge(softplus_act_part.sem, softplus_act_part.at(5))
                nc.vector.tensor_tensor(flat(WEND), flat(WEND), flat(DT), ALU.mult)

            @block.gpsimd
            def _(pool):
                pool.wait_ge(tile_done.sem, tile_done.at(1))
                for t in range(NT):
                    nc.gpsimd.tensor_tensor(ytok[:, t, :].rearrange("p (h n) -> p h n", h=SH),
                                            xs[:, t, :].rearrange("p (h n) -> p h n", h=SH),
                                            vecs("ssd_d").unsqueeze(2).broadcast_to((P, SH, SP)), ALU.mult)
        tile_done.close(1)
        for e, n in ((softplus_dve_part, 2), (softplus_act_part, 5), (decay_ready, 1), (decay_summed, 1), (cb_done, NT), (cb_masked, 2 * NT)):
            e.close(n)

        EW = WR[:, 0, :].rearrange("p (s h i) -> p s h i", s=2, h=SH)
        RW = WR[:, 1, :].rearrange("p (s h i) -> p s h i", s=2, h=SH)
        xdt = MI[:, 0:2048].rearrange("p (s h n) -> p s h n", s=2, h=SH)
        xw = MI[:, 2048:4096].rearrange("p (s h n) -> p s h n", s=2, h=SH)
        HS = XT[:, 6912:8960].rearrange("p (d n) -> p d n", d=2)
        steps = [(0, 0), (1, 0)] + [x for t in range(8) for x in ((0, 1 + t), (1, 8 - t))]
        NS = len(steps)

        with nc.Block() as block:
            @block.sync
            def _(sp):
                for d in range(2):
                    sp.wait_ge(step_taken.sem, step_taken.at(d + 1))
                    sp.dma_start(o_ssd[:, d, :], HS[:, d, :]).then_inc(stored.sem, 16)
                sp.wait_ge(stored.sem, stored.at(32))
                for d in range(2):
                    sp.dma_start(HS[:, d, :], ssd0[:, d, :]).then_inc(loaded.sem, 16)

            @block.gpsimd
            def _(pool):
                for n, (d, t) in enumerate(steps):
                    hs = slice(16 * d, 16 * d + 16)
                    if n >= 2:
                        pool.wait_ge(decays_summed.sem, decays_summed.at(4 * (n - 1)))
                    nc.gpsimd.tensor_tensor(RW[:, n % 2, :, :], DTA[:, t, hs].unsqueeze(2).broadcast_to((P, SH, P)),
                                            const(("le", "ge")[d]).unsqueeze(1).broadcast_to((P, SH, P)), ALU.mult)\
                      .then_inc(masked_decay_ready.sem, 1)
                    if n >= 2:
                        pool.wait_ge(chunk_summed.sem, chunk_summed.at(n - 1))
                    x = xs[:, t, :].rearrange("p (h n) -> p h n", h=SH)
                    nc.gpsimd.tensor_tensor(xdt[:, n % 2, :, :], x,
                                                            DT[:, t, hs].unsqueeze(2).broadcast_to((P, SH, SP)), ALU.mult).then_inc(pool_own.sem, pool_own.one())
                    pool.wait_ge(pool_own.sem, pool_own.n)
                    nc.gpsimd.tensor_tensor(xw[:, n % 2, :, :], x, WEND[:, t, hs].unsqueeze(2).broadcast_to((P, SH, SP)),
                                            ALU.mult).then_inc(x_scaled.sem, 1)

            @block.tensor
            def _(pe):
                def decays(n):
                    pe.wait_ge(masked_decay_ready.sem, masked_decay_ready.at(n + 1))
                    for q in range(4):
                        j = 4 * n + q
                        if j >= 2:
                            pe.wait_ge(decays_taken.sem, decays_taken.at(j - 1))
                        nc.tensor.matmul(PS[:, q % 2, :], const(("gt", "lt")[steps[n][0]]),
                                         RW[:, n % 2, 4 * q:4 * q + 4, :], start=True, stop=True).then_inc(decays_summed.sem, 1)

                decays(0)
                for n, (d, t) in enumerate(steps):
                    if n + 1 < NS:
                        decays(n + 1)
                    if n >= 2:
                        if n == 2:
                            pe.wait_ge(loaded.sem, loaded.at(32))
                        pe.wait_ge(step_taken.sem, step_taken.at(n - 1))
                        if n >= 3:
                            pe.wait_ge(step_taken.sem, step_taken.at(n))
                        for g in range(2):
                            mm = nc.tensor.matmul(PS[:, 3 + g, :], bcT[:, 2 + g, t * P:(t + 1) * P],
                                                  HS[:, d, 512 * g:512 * g + 512], start=True, stop=True)
                        mm.then_inc(state_read.sem, 1)
                    pe.wait_ge(x_scaled.sem, x_scaled.at(n + 1))
                    if n >= 1:
                        pe.wait_ge(step_taken.sem, step_taken.at(n))
                    for g, bank in enumerate((2, 7)):
                        mm = nc.tensor.matmul(PS[:, bank, :], btok[:, t, g * P:(g + 1) * P],
                                              xw[:, n % 2, 8 * g:8 * g + 8, :], start=True, stop=True)
                    mm.then_inc(update_summed.sem, 1)
                    pe.wait_ge(weights_ready.sem, weights_ready.at(n + 1))
                    for h in range(SH):
                        mm = nc.tensor.matmul(PS[:, 5 + h // 8, (h % 8) * SP:(h % 8 + 1) * SP], EW[:, n % 2, h, :],
                                              xdt[:, n % 2, h, :], start=True, stop=True)
                    mm.then_inc(chunk_summed.sem, 1)

            @block.scalar
            def _(act):
                for n in range(NS):
                    if n >= 2:
                        act.wait_ge(chunk_summed.sem, chunk_summed.at(n - 1))
                    for q in range(4):
                        act.wait_ge(decays_summed.sem, decays_summed.at(4 * n + q + 1))
                        act.activation(EW[:, n % 2, 4 * q:4 * q + 4, :], PS[:, q % 2, :].rearrange("p (h i) -> p h i", h=4),
                                       ACT.Exp).then_inc(decays_taken.sem, 1)

            @block.vector
            def _(dve):
                def weights(n):
                    d, t = steps[n]
                    dve.wait_ge(decays_taken.sem, decays_taken.at(4 * n + 4))
                    for g in range(2):
                        e = EW[:, n % 2, 8 * g:8 * g + 8, :]
                        ins = nc.vector.tensor_tensor(e, e, GB[:, t, d, g, :].unsqueeze(1).broadcast_to((P, 8, P)), ALU.mult)
                        if g == 0:
                            ins.then_inc(dve_own.sem, dve_own.one())
                    ins.then_inc(weights_ready.sem, 1)

                weights(0)
                for n, (d, t) in enumerate(steps):
                    if n + 1 < NS:
                        weights(n + 1)
                    hs = slice(16 * d, 16 * d + 16)
                    y = ytok[:, t, :]
                    ci = PS[:, 3:5, :].rearrange("p b (h n) -> p (b h) n", h=8)
                    if n >= 2:
                        dve.wait_ge(state_read.sem, state_read.at(n - 1))
                        dve.wait_ge(dve_own.sem, dve_own.n)
                        nc.vector.tensor_tensor(ci, ci, ECUM[:, t, hs].unsqueeze(2).broadcast_to((P, SH, SP)),
                                                               ALU.mult).then_inc(dve_own.sem, dve_own.one())
                        dve.wait_ge(dve_own.sem, dve_own.n)
                        nc.vector.tensor_tensor(y, y, PS[:, 3:5, :].rearrange("p b n -> p (b n)"), ALU.add).then_inc(dve_own.sem, dve_own.one())
                        h = HS[:, d, :].rearrange("p (h n) -> p h n", h=SH)
                        dve.wait_ge(update_summed.sem, update_summed.at(n + 1))
                        nc.vector.tensor_tensor(h, h, TOT[:, t, hs].unsqueeze(2).broadcast_to((P, SH, SP)),
                                                               ALU.mult).then_inc(dve_own.sem, dve_own.one())
                        dve.wait_ge(dve_own.sem, dve_own.n)
                        for g, bank in enumerate((2, 7)):
                            s = HS[:, d, 512 * g:512 * g + 512]
                            nc.vector.tensor_tensor(s, s, PS[:, bank, :], ALU.add).then_inc(dve_own.sem, dve_own.one())
                        dve.wait_ge(chunk_summed.sem, chunk_summed.at(n + 1))
                        dve.wait_ge(dve_own.sem, dve_own.n)
                        nc.vector.tensor_tensor(y, y, PS[:, 5:7, :].rearrange("p b n -> p (b n)"), ALU.add)\
                          .then_inc(step_taken.sem, 1)
                    else:
                        dve.wait_ge(update_summed.sem, update_summed.at(n + 1))
                        for g, bank in enumerate((2, 7)):
                            nc.vector.tensor_copy(HS[:, d, 512 * g:512 * g + 512], PS[:, bank, :]).then_inc(dve_own.sem, dve_own.one())
                        dve.wait_ge(chunk_summed.sem, chunk_summed.at(n + 1))
                        dve.wait_ge(dve_own.sem, dve_own.n)
                        nc.vector.tensor_tensor(y, y, PS[:, 5:7, :].rearrange("p b n -> p (b n)"), ALU.add).then_inc(dve_own.sem, dve_own.one())
                        dve.wait_ge(dve_own.sem, dve_own.n)
                        dve.sem_inc(step_taken.sem, 1)
                        if n == 1:
                            dve.wait_ge(loaded.sem, loaded.at(32))
        stored.close(32)
        loaded.close(32)
        for e, n in ((masked_decay_ready, NS), (decays_summed, 4 * NS), (decays_taken, 4 * NS), (x_scaled, NS), (state_read, NS - 2), (weights_ready, NS), (chunk_summed, NS),
                     (step_taken, NS), (update_summed, NS)):
            e.close(n)

        def gate(l, next_slot):
            zt = MI[:, 0:2048].rearrange("p (s n) -> p s n", s=2)
            sq = MI[:, 2048:3072]
            ss = MI[:, 3072:3072 + 4 * NT].rearrange("p (n t) -> p n t", n=4)
            normed = l == 0
            with nc.Block() as block:
                @block.sync
                def _(sp):
                    sp.dma_start(XT[:, 0:9216], x_spill).then_inc(xback.sem, 16)
                    for t in range(NT):
                        if t >= 2:
                            sp.wait_ge(gated.sem, gated.at(t - 1))
                        sp.dma_start(zt[:, t % 2, :], z_spill[t, :, :]).then_inc(gate_loaded[t % 2].sem, 16)
                    feed(sp, next_slot + 2)

                def scaled(dve, t):
                    dve.wait_ge(gate_rms_ready.sem, gate_rms_ready.at(t + 1))
                    nc.vector.tensor_scalar(ytok[:, t, :], ytok[:, t, :], ss[:, 3, t:t + 1], None, ALU.mult)\
                      .then_inc(gate_scaled.sem, 1)

                @block.vector
                def _(dve):
                    for t in range(NT):
                        y = ytok[:, t, :]
                        dve.wait_ge(gate_loaded[t % 2].sem, gate_loaded[t % 2].at(16 * (t // 2 + 1)))
                        nc.vector.tensor_tensor(y, y, zt[:, t % 2, :], ALU.mult).then_inc(gated.sem, 1)
                        if normed:
                            dve.wait_ge(square_sum_ready.sem, square_sum_ready.at(t + 1))
                            nc.vector.tensor_scalar(ss[:, 1, t:t + 1], ss[:, 0, t:t + 1], 1.0 / D, EPS,
                                                                   ALU.mult, ALU.add).then_inc(dve_own.sem, dve_own.one())
                            dve.wait_ge(dve_own.sem, dve_own.n)
                            nc.vector.reciprocal(ss[:, 2, t:t + 1], ss[:, 1, t:t + 1]).then_inc(gate_mean_ready.sem, 1)
                        if normed and t >= 1:
                            scaled(dve, t - 1)
                    if normed:
                        scaled(dve, NT - 1)

                ready = gate_scaled if normed else gated

                @block.tensor
                def _(pe):
                    for t in range(NT):
                        pe.wait_ge(ready.sem, ready.at(t + 1))
                        for g in range(2):
                            j = 2 * t + g
                            if j >= 4:
                                pe.wait_ge(mix_taken.sem, mix_taken.at(j - 3))
                            for b in range(4):
                                mm = nc.tensor.transpose(PS[:, j % 4, b * P:(b + 1) * P],
                                                         ytok[:, t, (4 * g + b) * P:(4 * g + b + 1) * P], ident)
                            mm.then_inc(mix_turned.sem, 1)

                @block.scalar
                def _(act):
                    def take(t):
                        for g in range(2):
                            j = 2 * t + g
                            act.wait_ge(mix_turned.sem, mix_turned.at(j + 1))
                            for b in range(4):
                                ins = act.activation(f0k[:, 4 * g + b, t * P:(t + 1) * P], PS[:, j % 4, b * P:(b + 1) * P],
                                                     ACT.Copy) if not normed else \
                                    act.activation(f0k[:, 4 * g + b, t * P:(t + 1) * P], PS[:, j % 4, b * P:(b + 1) * P],
                                                   ACT.Identity, scale=vecs("ssd_norm")[:, 4 * g + b:4 * g + b + 1])
                                if b < 3:
                                    ins.then_inc(act_own.sem, act_own.one())
                            act.wait_ge(act_own.sem, act_own.n)
                            ins.then_inc(mix_taken.sem, 1)

                    for t in range(NT):
                        if normed:
                            act.wait_ge(gated.sem, gated.at(t + 1))
                            if t >= 1:
                                act.wait_ge(act_own.sem, act_own.n)
                            act.activation(sq, ytok[:, t, :], ACT.Square, accum_out=ss[:, 0, t:t + 1]).then_inc(act_own.sem, act_own.one())
                            act.wait_ge(act_own.sem, act_own.n)
                            act.sem_inc(square_sum_ready.sem, 1)
                            act.wait_ge(gate_mean_ready.sem, gate_mean_ready.at(t + 1))
                            act.activation(ss[:, 3, t:t + 1], ss[:, 2, t:t + 1], ACT.Sqrt).then_inc(gate_rms_ready.sem, 1)
                        if t >= 1:
                            take(t - 1)
                    take(NT - 1)
            for e in (gate_loaded[0], gate_loaded[1]):
                e.close(16 * len(range(gate_loaded.index(e), NT, 2)))
            gated.close(NT)
            if normed:
                for e in (square_sum_ready, gate_mean_ready, gate_rms_ready, gate_scaled):
                    e.close(NT)
            mix_turned.close(2 * NT)
            mix_taken.close(2 * NT)

        def add_gated(dve, l, gate_at, b, c, bank, last):
            for a, e, cond, tc in SEGS:
                if tc != c:
                    continue
                x = xk[:, b, a:e]
                ins = nc.vector.scalar_tensor_tensor(out=x, in0=PS[:, bank, a - c * TC:e - c * TC],
                                                     scalar=MOD[:, l, gate_at + b, cond:cond + 1], in1=x,
                                                     op0=ALU.mult, op1=ALU.add)
                if e != (c + 1) * TC:
                    ins.then_inc(dve_own.sem, dve_own.one())
            last(ins)

        def out_projection(l, s0, nslots, blocks, next_slot):
            per = KD // nslots
            kk = len(blocks)
            frees(range(s0, s0 + nslots), [per * NC] * nslots)
            with nc.Block() as block:
                @block.sync
                def _(sp):
                    feed(sp, next_slot)

                @block.tensor
                def _(pe):
                    i = 0
                    for s in range(nslots):
                        pe.wait_ge(*landed(s0 + s))
                        w = WR[:, (s0 + s) % 2, 0:kk * per * P].rearrange("p (k n) -> p k n", k=kk)
                        for b in range(per):
                            for c in range(NC):
                                tile_products(pe, i, P, TC, [(w[:, k, b * P:(b + 1) * P], blocks[k][:, c * TC:(c + 1) * TC])
                                                             for k in range(kk)])
                                i += 1

                @block.vector
                def _(dve):
                    dve.wait_ge(xback.sem, xback.at(16))
                    for i in range(KD * NC):
                        dve.wait_ge(tile_done.sem, tile_done.at(i + 1))
                        add_gated(dve, l, 16, i // NC, i % NC, i % 8, lambda ins: ins.then_inc(tile_free.sem, 1))
            close_tiles(KD * NC)
            xback.close(16)

        raw_unit = None

        def mlp(l):
            nonlocal raw_unit
            mem = ExitStack()

            def f32(name, shape):
                return mem.enter_context(nc.sbuf_tensor(f"{name}_{l}", shape, F32))

            def f32r(name, shape):
                return mem.enter_context(nc.sbuf_tensor(f"{name}_{l}", shape, F32R))

            HH, HL = f32r("h_high", [P, KD, T]), f32r("h_low", [P, KD, T])
            raw_unit = f32("raw_unit", [P, 2, 1024])
            with (nc.sbuf_tensor(f"squares_{l}", [P, 8, TC], F32) as SQ, nc.sbuf_tensor(f"rms_{l}", [P, T], F32) as RB,
                  nc.sbuf_tensor(f"split_{l}", [P, 8, TC], F32) as tmp):
                norm(l, 1, None, SQ, RB, 0, split=(tmp, HH, HL))
            WH, WL = f32r("w_high", [P, 4, 1024]), f32r("w_low", [P, 4, 1024])
            AH, AL = f32r("a_high", [P, 2, 2, T]), f32r("a_low", [P, 2, 2, T])
            rt, sq = f32("relu", [P, 2, TC]), f32("square", [P, 2, TC])
            NP = NG - 2

            def at(c, per_step, g, i, n):
                return i * (2 * per_step) + c.at(per_step * g + n)

            with nc.Block() as block:
                @block.sync
                def _(sp):
                    with sp.Fori(0, 31) as i:
                        for s in range(2):
                            sp.wait_ge(unit_split.sem, at(unit_split, 1, 0, i, s + 1))
                            sp.dma_start(raw_unit[:, s, :],
                                         wff[l, bass.ds(i * 2 + (2 + s), 1), :, :].rearrange("a p n -> p (a n)"))\
                              .then_inc(unit_loaded[s].sem, 16)

                @block.tensor
                def _(pe):
                    def passes(out, w, ks, rhs, cols):
                        n = 0
                        for k in ks:
                            for wt, at_ in ((WH, 0), (WH, 1), (WL, 0)):
                                mm = nc.tensor.matmul(out, wt[:, w(k), cols(k)], rhs[at_](k), start=(n == 0),
                                                      stop=(n == 3 * len(ks) - 1))
                                n += 1
                        return mm

                    def up(g, i, first=False):
                        for j in range(6):
                            m, c = j // NC, j % NC
                            if j % NC == 0:
                                n = (g == 0) * m + (g > 0) * (m - 2)
                                pe.wait_ge(unit_split.sem, at(unit_split, 4, g, i, n + 1))
                            if not (first and j < 3):
                                pe.wait_ge(up_taken.sem, at(up_taken, 6, g, i, j - 2))
                            t = slice(c * TC, (c + 1) * TC)
                            passes(PS[:, j % 3, 0:TC], lambda k: m, range(KD),
                                   (lambda k: HH[:, k, t], lambda k: HL[:, k, t]),
                                   lambda k: slice(k * P, (k + 1) * P)).then_inc(up_done.sem, 1)

                    def down(g, i, unit, first=False):
                        pe.wait_ge(unit_split.sem, at(unit_split, 4, g, i, unit))
                        pe.wait_ge(hidden_split.sem, at(hidden_split, 6, g, i, 6))
                        for j in range(24):
                            b, c = j // NC, j % NC
                            if not (first and j < 4):
                                pe.wait_ge(down_taken.sem, at(down_taken, 24, g, i, j - 3))
                            t = slice(c * TC, (c + 1) * TC)
                            passes(PS[:, 3 + j % 4, 0:TC], lambda k: 2 + k, range(2),
                                   (lambda k: AH[:, g % 2, k, t], lambda k: AL[:, g % 2, k, t]),
                                   lambda k: slice(b * P, (b + 1) * P)).then_inc(down_done.sem, 1)

                    up(0, 0, first=True)
                    up(1, 0)
                    down(0, 0, 6, first=True)
                    up(2, 0)
                    down(1, 0, 6)
                    with pe.Fori(0, NP // 2 - 1) as i:
                        up(3, i)
                        down(2, i, 6)
                        up(4, i)
                        down(3, i, 6)
                    up(NG - 1, 0)
                    down(NG - 2, 0, 6)
                    down(NG - 1, 0, 4)

                def unit_places(kind):
                    return (0, 1) if kind == "W1" else (2, 3)

                @block.scalar
                def _(act):
                    def unit(n, g, i, place, used):
                        act.wait_ge(unit_loaded[n % 2].sem, i * 64 + unit_loaded[n % 2].at(16 * ((4 * g + n) // 2 + 1)))
                        if used:
                            act.wait_ge(*used)
                        act.activation(WH[:, place, :], raw_unit[:, n % 2, :], ACT.Copy).then_inc(unit_hi.sem, 1)

                    def tile(g, i, j, first=False):
                        act.wait_ge(up_done.sem, at(up_done, 6, g, i, j + 1))
                        if not (first and j < 2):
                            act.wait_ge(squared.sem, at(squared, 6, g, i, j - 1))
                        act.activation(rt[:, j % 2, :], PS[:, j % 3, 0:TC], ACT.Relu).then_inc(up_taken.sem, 1)

                    def tile_high(g, i, j):
                        act.wait_ge(squared.sem, at(squared, 6, g, i, j + 1))
                        m, c = j // NC, j % NC
                        act.activation(AH[:, g % 2, m, c * TC:(c + 1) * TC], sq[:, j % 2, :], ACT.Copy)\
                           .then_inc(hidden_hi.sem, 1)

                    def step(g, i, w2=True, w1=True):
                        if w2:
                            for s in range(2):
                                unit(s, g, i, 2 + s, (down_done.sem, at(down_done, 24, g - 1, i, 0)))
                        for j in range(6):
                            tile(g, i, j, first=(g == 0))
                            if j >= 1:
                                tile_high(g, i, j - 1)
                            if w1 and j == 3:
                                unit(2, g, i, 0, (up_done.sem, at(up_done, 6, g, i, 3)))
                        tile_high(g, i, 5)
                        if w1:
                            unit(3, g, i, 1, (up_done.sem, at(up_done, 6, g, i, 6)))

                    unit(0, 0, 0, 0, None)
                    unit(1, 0, 0, 1, None)
                    step(0, 0, w2=False)
                    step(1, 0)
                    step(2, 0)
                    with act.Fori(0, NP // 2 - 1) as i:
                        step(3, i)
                        step(4, i)
                    step(NG - 1, 0, w1=False)
                    for s in range(2):
                        unit(2 + s, NG - 1, 0, 2 + s, (down_done.sem, at(down_done, 24, NG - 1, 0, 0)))

                @block.gpsimd
                def _(pool):
                    def step(g, i):
                        for j in range(6):
                            pool.wait_ge(up_taken.sem, at(up_taken, 6, g, i, j + 1))
                            if not (g == 0 and j < 2):
                                pool.wait_ge(hidden_split.sem, at(hidden_split, 6, g, i, j - 1))
                            nc.gpsimd.tensor_tensor(sq[:, j % 2, :], rt[:, j % 2, :], rt[:, j % 2, :], ALU.mult)\
                              .then_inc(squared.sem, 1)
                    step(0, 0)
                    step(1, 0)
                    step(2, 0)
                    with pool.Fori(0, NP // 2 - 1) as i:
                        step(3, i)
                        step(4, i)
                    step(NG - 1, 0)

                @block.vector
                def _(dve):
                    def unit(n, g, i, place):
                        dve.wait_ge(unit_hi.sem, at(unit_hi, 4, g, i, n + 1))
                        nc.vector.tensor_tensor(WL[:, place, :], raw_unit[:, n % 2, :], WH[:, place, :].bitcast(F32),
                                                ALU.subtract).then_inc(unit_split.sem, 1)

                    def tile(g, i, j):
                        dve.wait_ge(hidden_hi.sem, at(hidden_hi, 6, g, i, j + 1))
                        m, t = j // NC, slice(j % NC * TC, (j % NC + 1) * TC)
                        nc.vector.tensor_tensor(AL[:, g % 2, m, t], sq[:, j % 2, :], AH[:, g % 2, m, t].bitcast(F32),
                                                ALU.subtract).then_inc(hidden_split.sem, 1)

                    def sums(g, i):
                        for j in range(24):
                            b, c = j // NC, j % NC
                            dve.wait_ge(down_done.sem, at(down_done, 24, g, i, j + 1))
                            if j == 0:
                                dve.wait_ge(down_taken.sem, at(down_taken, 24, g, i, 0))
                            for a, e, cond, tc in SEGS:
                                if tc == c:
                                    x = xk[:, b, a:e]
                                    ins = nc.vector.scalar_tensor_tensor(
                                        out=x, in0=PS[:, 3 + j % 4, a - c * TC:e - c * TC],
                                        scalar=MOD[:, l, 40 + b, cond:cond + 1], in1=x, op0=ALU.mult, op1=ALU.add)
                            ins.then_inc(down_taken.sem, 1)

                    def step(g, i, w2=True, w1=True, down=True):
                        if w2:
                            unit(0, g, i, 2)
                            unit(1, g, i, 3)
                        for j in range(6):
                            tile(g, i, j)
                            if w1 and j == 2:
                                unit(2, g, i, 0)
                        if w1:
                            unit(3, g, i, 1)
                        if down:
                            sums(g - 1, i)

                    unit(0, 0, 0, 0)
                    unit(1, 0, 0, 1)
                    step(0, 0, w2=False, down=False)
                    step(1, 0)
                    step(2, 0)
                    with dve.Fori(0, NP // 2 - 1) as i:
                        step(3, i)
                        step(4, i)
                    step(NG - 1, 0, w1=False)
                    unit(2, NG - 1, 0, 2)
                    unit(3, NG - 1, 0, 3)
                    sums(NG - 1, 0)
            for c, n in ((unit_hi, 64), (unit_split, 64), (unit_loaded[0], 512), (unit_loaded[1], 512),
                         (up_done, 96), (up_taken, 96), (down_done, 384), (down_taken, 384), (squared, 96),
                         (hidden_hi, 96), (hidden_split, 96)):
                c.close(n)
            mem.close()

        gate(0, S_OUTE)
        out_projection(0, S_OUTE, 4, [ynaT[:, b, :] for b in range(4)] + [f0k[:, b, :] for b in range(8)], S_QK)
        mixer.close()
        mlp(0)
        mixer = ExitStack()
        HT = mixer_tensor("HT1", [P, 9216])
        F0 = mixer_tensor("F01", [P, 9216])
        F1 = mixer_tensor("F11", [P, 9216])
        WR = mixer_tensor("WR1", [P, 2, 4096])
        MI = mixer_tensor("MI1", [P, 4096])
        hk = HT[:, :].rearrange("p (k t) -> p k t", k=KD)
        f0k = F0[:, :].rearrange("p (k t) -> p k t", k=8)
        qT = F0[:, 0:4608].rearrange("p (b t) -> p b t", b=4)
        kT = F0[:, 4608:9216].rearrange("p (b t) -> p b t", b=4)
        ytok = HT[:, :].rearrange("p (t n) -> p t n", t=NT)
        zst = MI[:, 0:2048].rearrange("p (s n) -> p s n", s=4)
        norm_mixer(1, S_QK + 2)

        ktok = F1[:, 0:4608].rearrange("p (t n) -> p t n", t=NT)
        conv_phase(S_QK, 8,
                   F1[:, 4608:6920].rearrange("p (s t) -> p s t", s=2), MI[:, 0:2308].rearrange("p (s t) -> p s t", s=2),
                   lambda b: (qT[:, b, :] if b < 4 else kT[:, b - 4, :]),
                   lambda b: ktok[:, :, (b - 4) * P:(b - 3) * P] if b >= 4 else None,
                   vecs("mw").rearrange("p (b j) -> p b j", j=3), vecs("mb"),
                   spill_x=True)
        spilled.close(16)

        v1 = XT[:, :].rearrange("p (t h e) -> p t h e", t=NT, h=MH)
        x1 = MI[:, 2048:2336]
        frees(range(S_VO, S_OUTO), (9, 9, 9, 9))
        with nc.Block() as block:
            @block.sync
            def _(sp):
                feed(sp, S_OUTO)
                spill_gate_sp(sp, 18)

            @block.tensor
            def _(pe):
                i = 0
                for s in range(S_VO, S_OUTO):
                    pe.wait_ge(*landed(s))
                    for t in range(NT):
                        token_tile(pe, i, slot_k(s), t)
                        i += 1
                pe.wait_ge(tile_free.sem, tile_free.at(i))
                small_products(pe, 1)

            @block.gpsimd
            def _(pool):
                nc.gpsimd.memset(v1[:, :, :, MV:V1], 1.0)

            @block.scalar
            def _(act):
                i = 0
                for s in range(2):
                    for t in range(NT):
                        act.wait_ge(tile_done.sem, tile_done.at(i + 1))
                        act.activation(v1[:, t, 4 * s:4 * s + 4, 0:MV], PS[:, i % 8, :].rearrange("p (h e) -> p h e", h=4),
                                       ACT.Copy).then_inc(tile_free.sem, 1)
                        i += 1
                spill_gate_act(act, i, ACT.Sigmoid)

            @block.vector
            def _(dve):
                dve.wait_ge(tile_done.sem, tile_done.at(37))
                nc.vector.tensor_tensor(x1.rearrange("p (t c) -> p t c", t=NT),
                                        PS[:, 0, 0:288].rearrange("p (t c) -> p t c", t=NT),
                                        vecs("gate_b").unsqueeze(1).broadcast_to((P, NT, 32)), ALU.add)
        tile_done.close(37)
        tile_free.close(36)
        close_gate()

        R40 = slice(0, ROWS)
        row = lambda n: HT[R40, n * T:(n + 1) * T]
        LI, LF, M, CU, A, WI, EN, WK = (row(n) for n in range(8))
        B = F1[R40, 4608:4608 + T]
        CST = F1[:, 5760:6792].rearrange("p (d b e) -> p d b e", d=2, b=4)
        WCB = F1[:, 6792:6864].rearrange("p (d b t) -> p d b t", d=2, b=4)
        TA = SM[:, 0:1440].rearrange("p (t n r) -> p t n r", t=NT, n=4)
        SEL = WR[R40, 0, 0:2048].rearrange("p (n m) -> p n m", n=16)
        RST = WR[R40, 0, 2048:3200]
        HALF = WR[R40, 0, 3200:3328]
        PAIR = WR[R40, 0, 3328:3336]
        lf = MI[:, 0:144].rearrange("p (t c) -> p t c", t=NT)
        xf = MI[:, 144:288].rearrange("p (t c) -> p t c", t=NT)
        g_s = MI[:, 288:1152].rearrange("p (n c) -> p n c", n=6)
        tokG = MI[:, 1152:1872].rearrange("p (n t r) -> p n t r", n=2, t=NT)
        MP, ML, CL, WC, DL = (MI[R40, 2400 + 9 * n:2409 + 9 * n] for n in range(5))
        WX = MI[R40, 2448:2520].rearrange("p (n t) -> p n t", n=8)

        def seq3(a):
            return a.rearrange("p (t i) -> p t i", t=NT)

        with nc.Block() as block:
            @block.sync
            def _(sp):
                n0 = NCONST
                sp.dma_start(WR[R40, 0, 0:3336], consts[R40, n0:n0 + 3336]).then_inc(loaded.sem, 16)

            @block.vector
            def _(dve):
                def chained(ins):
                    ins.then_inc(dve_own.sem, dve_own.one())
                    dve.wait_ge(dve_own.sem, dve_own.n)
                raw = x1.rearrange("p (t n c) -> p t n c", t=NT, n=2)
                chained(nc.vector.memset(tokG, 0.0))
                nc.vector.tensor_scalar(xf, raw[:, :, 1, :], -1.0, None, ALU.mult).then_inc(softplus_dve_part.sem, 1)
                softplus_dve(dve, xf.rearrange("p t c -> p (t c)"), lf.rearrange("p t c -> p (t c)"), g_s)
                for d in range(2):
                    nc.vector.tensor_copy(tokG[:, 0, :, 32 * d:32 * d + 8], raw[:, :, 0, 8 * d:8 * d + 8]).then_inc(dve_own.sem, dve_own.one())
                    nc.vector.tensor_scalar(tokG[:, 1, :, 32 * d:32 * d + 8], lf[:, :, 8 * d:8 * d + 8],
                                                           -1.0, None, ALU.mult).then_inc(dve_own.sem, dve_own.one())
                dve.wait_ge(dve_own.sem, dve_own.n)
                dve.sem_inc(gates_ready.sem, 1)
                nc.vector.memset(M, 0.0).then_inc(dve_own.sem, dve_own.one())
                nc.vector.memset(CU, 0.0).then_inc(dve_own.sem, dve_own.one())
                nc.vector.memset(MP, 0.0).then_inc(dve_own.sem, dve_own.one())
                dve.wait_ge(rows_turned.sem, rows_turned.at(1))
                for n, dst in enumerate((LI, LF)):
                    nc.vector.tensor_copy(dst[:, 0:1024].rearrange("p (b t) -> p b t", b=2),
                                                         PS[R40, 3 * n:3 * n + 2, :]).then_inc(dve_own.sem, dve_own.one())
                    nc.vector.tensor_copy(dst[:, 1024:T], PS[R40, 3 * n + 2, 0:P]).then_inc(dve_own.sem, dve_own.one())
                dve.wait_ge(dve_own.sem, dve_own.n)
                dve.wait_ge(loaded.sem, loaded.at(16))
                for d in range(2):
                    r = slice(32 * d, 32 * d + 8)
                    way = slice(None, None, 1 if d == 0 else -1)
                    for a, b, m0 in ((0, CTX, 0.0), (CTX, T, vecs("m0")[r, :])):
                        nc.vector.tensor_tensor_scan(M[r, a:b][:, way], LF[r, a:b][:, way], LI[r, a:b][:, way],
                                                                    m0, op0=ALU.add, op1=ALU.max).then_inc(dve_own.sem, dve_own.one())
                    nc.vector.tensor_tensor_scan(CU[r, :][:, way], RST[r, :][:, way], LF[r, :][:, way], 0.0,
                                                                op0=ALU.mult, op1=ALU.add).then_inc(dve_own.sem, dve_own.one())
                dve.wait_ge(dve_own.sem, dve_own.n)
                m3, c3 = seq3(M), seq3(CU)
                nc.vector.tensor_copy(MP[0:8, 1:2], vecs("m0")[0:8, :]).then_inc(dve_own.sem, dve_own.one())
                nc.vector.tensor_copy(MP[0:8, 2:9], m3[0:8, 1:8, P - 1]).then_inc(dve_own.sem, dve_own.one())
                nc.vector.tensor_copy(MP[32:40, 8:9], vecs("m0")[32:40, :]).then_inc(dve_own.sem, dve_own.one())
                nc.vector.tensor_copy(MP[32:40, 1:8], m3[32:40, 2:9, 0]).then_inc(dve_own.sem, dve_own.one())
                for dst, src in ((ML, m3), (CL, c3)):
                    nc.vector.tensor_copy(dst[0:32, :], src[0:32, :, P - 1]).then_inc(dve_own.sem, dve_own.one())
                    nc.vector.tensor_copy(dst[32:40, :], src[32:40, :, 0]).then_inc(dve_own.sem, dve_own.one())
                chained(nc.vector.tensor_tensor(A, LI, CU, ALU.subtract))
                chained(nc.vector.tensor_tensor(B, CU, M, ALU.subtract))
                chained(nc.vector.tensor_tensor(DL, CL, ML, ALU.subtract))
                nc.vector.tensor_tensor(WC, DL, MP, ALU.add).then_inc(dve_own.sem, dve_own.one())
                nc.vector.tensor_tensor(seq3(WI), seq3(B), MP.unsqueeze(2).broadcast_to((ROWS, NT, P)), ALU.add).then_inc(dve_own.sem, dve_own.one())
                nc.vector.tensor_tensor(seq3(WK), seq3(A), DL.unsqueeze(2).broadcast_to((ROWS, NT, P)), ALU.add).then_inc(dve_own.sem, dve_own.one())
                dve.wait_ge(dve_own.sem, dve_own.n)
                dve.sem_inc(logs_ready.sem, 1)
                dve.wait_ge(exps_ready.sem, exps_ready.at(1))
                nc.vector.tensor_scalar(WI, WI, MQ ** -0.5, None, ALU.mult).then_inc(dve_own.sem, dve_own.one())
                nc.vector.tensor_tensor(WX, WC.unsqueeze(1).broadcast_to((ROWS, 8, NT)),
                                                       PAIR.unsqueeze(2).broadcast_to((ROWS, 8, NT)), ALU.mult).then_inc(dve_own.sem, dve_own.one())
                dve.wait_ge(dve_own.sem, dve_own.n)
                dve.sem_inc(rows_ready.sem, 1)
                dve.wait_ge(rows_back.sem, rows_back.at(1))
                for b in range(3):
                    nc.vector.tensor_copy(TA[:, 3 * b:3 * b + 3, :, :].rearrange("p t n r -> p (t n r)"), PS[:, b, 0:480])
                nc.vector.tensor_copy(WCB.rearrange("p d b t -> p (d b t)"), PS[:, 3, 0:72])

            @block.scalar
            def _(act):
                softplus_act(act, xf.rearrange("p t c -> p (t c)"), g_s)
                act.wait_ge(logs_ready.sem, logs_ready.at(1))
                act.activation(WI, WI, ACT.Exp).then_inc(act_own.sem, act_own.one())
                act.activation(WK, WK, ACT.Exp).then_inc(act_own.sem, act_own.one())
                act.activation(EN, M, ACT.Exp, scale=-1.0).then_inc(act_own.sem, act_own.one())
                act.activation(WC, WC, ACT.Exp).then_inc(act_own.sem, act_own.one())
                act.wait_ge(act_own.sem, act_own.n)
                act.sem_inc(exps_ready.sem, 1)

            @block.tensor
            def _(pe):
                pe.wait_ge(gates_ready.sem, gates_ready.at(1))
                for n in range(2):
                    for t in range(NT):
                        mm = nc.tensor.transpose(PS[R40, 3 * n + t // 4, (t % 4) * P:(t % 4 + 1) * P], tokG[:, n, t, :], ident)
                mm.then_inc(rows_turned.sem, 1)
                pe.wait_ge(rows_ready.sem, rows_ready.at(1))
                for t in range(NT):
                    for n, r in enumerate((A, WI, EN, WK)):
                        nc.tensor.transpose(PS[:, t // 3, ((t % 3) * 4 + n) * ROWS:((t % 3) * 4 + n + 1) * ROWS],
                                            r[:, t * P:(t + 1) * P], ident[R40, R40])
                nc.tensor.matmul(PS[:, 3, 0:72], HALF, WX.rearrange("p n t -> p (n t)"), start=True, stop=True)\
                  .then_inc(rows_back.sem, 1)
        for e, n in ((softplus_dve_part, 2), (softplus_act_part, 2), (gates_ready, 1), (rows_turned, 1), (logs_ready, 1), (exps_ready, 1), (rows_ready, 1), (rows_back, 1)):
            e.close(n)
        loaded.close(16)
        ML_out = ML

        XM = MI[:, 0:512].rearrange("p (s h i) -> p s h i", s=2, h=2)
        SW = MI[:, 512:1024].rearrange("p (s h i) -> p s h i", s=2, h=2)
        WV = MI[:, 1024:1540].rearrange("p (s h e) -> p s h e", s=2, h=2)
        IA = MI[:, 1540:2056].rearrange("p (s h e) -> p s h e", s=2, h=2)
        NU = MI[:, 2056:2314].rearrange("p (h e) -> p h e", h=2)
        den = MI[:, 2314:2318]
        msteps = [(d, 0, b) for d in range(2) for b in range(4)]
        msteps += [(d, t if d == 0 else 9 - t, b) for t in range(1, NT) for d in range(2) for b in range(4)]
        NM = len(msteps)

        with nc.Block() as block:
            @block.sync
            def _(sp):
                sp.dma_start(o_m, ML).then_inc(stored.sem, 16)
                sp.wait_ge(tail_done.sem, tail_done.at(8))
                sp.dma_start(o_mls, CST).then_inc(stored.sem, 16)
                sp.wait_ge(stored.sem, stored.at(32))
                sp.dma_start(CST, mls0).then_inc(loaded.sem, 16)

            @block.gpsimd
            def _(pool):
                for n, (d, t, b) in enumerate(msteps):
                    if n >= 2:
                        pool.wait_ge(memory_summed.sem, memory_summed.at(n - 1))
                    wk = TA[:, t, 3, 32 * d + 2 * b:32 * d + 2 * b + 2]
                    nc.gpsimd.tensor_tensor(WV[:, n % 2, :, :], v1[:, t, 2 * b:2 * b + 2, :],
                                            wk.unsqueeze(2).broadcast_to((P, 2, V1)), ALU.mult).then_inc(values_weighted.sem, 1)

            @block.tensor
            def _(pe):
                def exponents(n):
                    d, t, b = msteps[n]
                    if n >= 2:
                        pe.wait_ge(exponents_masked.sem, exponents_masked.at(n - 1))
                    for h in range(2):
                        mm = nc.tensor.matmul(PS[:, n % 2, h * P:(h + 1) * P], SEL[:, 8 * d + 2 * b + h, :],
                                              B[:, t * P:(t + 1) * P], start=True, stop=True)
                    mm.then_inc(exponents_done.sem, 1)

                def scores(n):
                    d, t, b = msteps[n]
                    if n >= 1:
                        pe.wait_ge(scores_weighted.sem, scores_weighted.at(n))
                    for h in range(2):
                        r = slice(64 * h, 64 * h + 64)
                        mm = nc.tensor.matmul(PS[:, 2 + h, 0:P], kT[r, b, t * P:(t + 1) * P], qT[r, b, t * P:(t + 1) * P],
                                              start=True, stop=True)
                    mm.then_inc(qk_done.sem, 1)

                exponents(0)
                scores(0)
                for n, (d, t, b) in enumerate(msteps):
                    if n + 1 < NM:
                        exponents(n + 1)
                    pe.wait_ge(scores_weighted.sem, scores_weighted.at(n + 1))
                    if n >= 1:
                        pe.wait_ge(intra_taken.sem, intra_taken.at(n))
                    for h in range(2):
                        mm = nc.tensor.matmul(PS[:, 4, h * V1:(h + 1) * V1], SW[:, n % 2, h, :], v1[:, t, 2 * b + h, :],
                                              start=True, stop=True)
                    mm.then_inc(intra_summed.sem, 1)
                    if n + 1 < NM:
                        scores(n + 1)
                    if n >= 1:
                        pe.wait_ge(tail_done.sem, tail_done.at(n))
                    if n >= 8:
                        if n == 8:
                            pe.wait_ge(loaded.sem, loaded.at(16))
                        for h in range(2):
                            r = slice(64 * h, 64 * h + 64)
                            nc.tensor.matmul(PS[:, 5 + h, 0:V1], qT[r, b, t * P:(t + 1) * P], CST[r, d, b, :],
                                             start=True, stop=True)
                    pe.wait_ge(values_weighted.sem, values_weighted.at(n + 1))
                    for h in range(2):
                        mm = nc.tensor.matmul(PS[64 * h:64 * h + 64, 7, 0:V1], ktok[:, t, (2 * b + h) * MQ:(2 * b + h + 1) * MQ],
                                              WV[:, n % 2, h, :], start=True, stop=True)
                    mm.then_inc(memory_summed.sem, 1)

            @block.scalar
            def _(act):
                def weights(n):
                    d, t, b = msteps[n]
                    act.wait_ge(exponents_masked.sem, exponents_masked.at(n + 1))
                    for h in range(2):
                        c = 32 * d + 2 * b + h
                        ins = act.activation(XM[:, n % 2, h, :], XM[:, n % 2, h, :], ACT.Exp, bias=TA[:, t, 0, c:c + 1])
                        if h == 0:
                            ins.then_inc(act_own.sem, act_own.one())
                    act.wait_ge(act_own.sem, act_own.n)
                    ins.then_inc(exp_ready.sem, 1)

                weights(0)
                for n in range(NM):
                    if n + 1 < NM:
                        weights(n + 1)
                    act.wait_ge(intra_summed.sem, intra_summed.at(n + 1))
                    if n >= 2:
                        act.wait_ge(tail_done.sem, tail_done.at(n - 1))
                    act.activation(IA[:, n % 2, :, :].rearrange("p h e -> p (h e)"), PS[:, 4, 0:2 * V1], ACT.Copy)\
                       .then_inc(intra_taken.sem, 1)

            @block.vector
            def _(dve):
                def masked(n):
                    d = msteps[n][0]
                    dve.wait_ge(exponents_done.sem, exponents_done.at(n + 1))
                    if n >= 2:
                        dve.wait_ge(scores_weighted.sem, scores_weighted.at(n - 1))
                    nc.vector.tensor_tensor(XM[:, n % 2, :, :], PS[:, n % 2, 0:256].rearrange("p (h i) -> p h i", h=2),
                                            const(("neg_f", "neg_b")[d]).unsqueeze(1).broadcast_to((P, 2, P)), ALU.add)\
                      .then_inc(exponents_masked.sem, 1)

                def weighted(n):
                    dve.wait_ge(qk_done.sem, qk_done.at(n + 1))
                    dve.wait_ge(exp_ready.sem, exp_ready.at(n + 1))
                    if n >= 2:
                        dve.wait_ge(intra_summed.sem, intra_summed.at(n - 1))
                    nc.vector.scalar_tensor_tensor(out=SW[:, n % 2, :, :], in0=PS[:, 2:4, 0:P], scalar=MQ ** -0.5,
                                                   in1=XM[:, n % 2, :, :], op0=ALU.mult, op1=ALU.mult).then_inc(scores_weighted.sem, 1)

                def tail(n):
                    d, t, b = msteps[n]
                    c = 32 * d + 2 * b
                    dve.wait_ge(intra_taken.sem, intra_taken.at(n + 1))
                    dve.wait_ge(memory_summed.sem, memory_summed.at(n + 1))
                    if n >= 8:
                        for h in range(2):
                            nc.vector.scalar_tensor_tensor(
                                out=NU[:, h, :], in0=PS[:, 5 + h, 0:V1], scalar=TA[:, t, 1, c + h:c + h + 1],
                                in1=IA[:, n % 2, h, :], op0=ALU.mult, op1=ALU.add).then_inc(dve_own.sem, dve_own.one())
                        dve.wait_ge(dve_own.sem, dve_own.n)
                        nc.vector.scalar_tensor_tensor(out=CST[:, d, b, :], in0=CST[:, d, b, :],
                                                                      scalar=WCB[:, d, b, t:t + 1], in1=PS[:, 7, 0:V1],
                                                                      op0=ALU.mult, op1=ALU.add).then_inc(dve_own.sem, dve_own.one())
                        nu = NU
                    else:
                        nc.vector.tensor_copy(CST[:, d, b, :], PS[:, 7, 0:V1]).then_inc(dve_own.sem, dve_own.one())
                        nu = IA[:, n % 2, :, :]
                    dd, rd = den[:, 0:2], den[:, 2:4]
                    nc.vector.scalar_tensor_tensor(out=dd, in0=nu[:, :, MV], scalar=-1.0, in1=nu[:, :, MV],
                                                                  op0=ALU.mult, op1=ALU.max).then_inc(dve_own.sem, dve_own.one())
                    dve.wait_ge(dve_own.sem, dve_own.n)
                    nc.vector.tensor_tensor(dd, dd, TA[:, t, 2, c:c + 2], ALU.max).then_inc(dve_own.sem, dve_own.one())
                    dve.wait_ge(dve_own.sem, dve_own.n)
                    nc.vector.reciprocal(rd, dd).then_inc(dve_own.sem, dve_own.one())
                    dve.wait_ge(dve_own.sem, dve_own.n)
                    for h in range(2):
                        y = ytok[:, t, (2 * b + h) * MV:(2 * b + h + 1) * MV]
                        if t == 0 and d == 0 or t > 0 and (d == 0) == (t <= 4):
                            ins = nc.vector.tensor_scalar(y, nu[:, h, 0:MV], rd[:, h:h + 1], None, ALU.mult)
                        else:
                            ins = nc.vector.scalar_tensor_tensor(out=y, in0=nu[:, h, 0:MV], scalar=rd[:, h:h + 1], in1=y,
                                                                 op0=ALU.mult, op1=ALU.add)
                        ins.then_inc(dve_own.sem, dve_own.one())
                    dve.wait_ge(dve_own.sem, dve_own.n)
                    dve.sem_inc(tail_done.sem, 1)
                    if n == 7:
                        dve.wait_ge(loaded.sem, loaded.at(16))

                masked(0)
                for n in range(NM):
                    weighted(n)
                    if n + 1 < NM:
                        masked(n + 1)
                    if n >= 1:
                        tail(n - 1)
                tail(NM - 1)
        stored.close(32)
        loaded.close(16)
        for e in (exponents_done, exponents_masked, qk_done, exp_ready, scores_weighted, intra_taken, memory_summed, tail_done, values_weighted, intra_summed):
            e.close(NM)

        gate(1, S_OUTO)
        out_projection(1, S_OUTO, 2, [f0k[:, b, :] for b in range(8)], NSLOT)
        mixer.close()
        mlp(1)
        with (nc.sbuf_tensor("y_out", [P, KD, T], F32) as yo, nc.sbuf_tensor("squares_f", [P, 8, TC], F32) as SQ,
              nc.sbuf_tensor("rms_f", [P, T], F32) as RB):
            norm(1, 2, yo, SQ, RB, 0, final=True)


def kernel(**inputs):
    import numpy as _np
    import concourse.bacc as _bacc
    from concourse import mybir as _mybir
    from concourse.bass_utils import run_bass_kernel_spmd as _run

    a = {k: _np.asarray(v) for k, v in inputs.items()}
    f32 = _np.float32

    def fm(x):
        return x.reshape(x.shape[0], -1, P).transpose(2, 1, 0)

    def cols(x):
        return x.reshape(-1, P).T

    def kslots(w, n):
        k = w.shape[0] // P
        return w.reshape(k, P, -1, n).transpose(2, 1, 0, 3).reshape(-1, P, k * n)

    def rows(x):
        return _np.broadcast_to(x.reshape(1, -1), (P, x.size))

    m0 = _np.zeros((P, 1), f32)
    m0[0:8, 0] = a["state_mlstm_m"][0, 0, 0]
    m0[32:40, 0] = a["state_mlstm_m"][0, 0, 1]
    parts = {
        "cond": fm(_np.concatenate([a["c_ctx"][None], a["c"]], 0)).reshape(P, -1),
        "b_mod": cols(a["b_mod"]), "norm_mix": cols(a["norm_mix"]), "norm_ffn": cols(a["norm_ffn"]),
        "norm_f": cols(a["norm_f"]), "ssd_norm": cols(a["ssd_norm"][0]),
        "cw": fm(a["ssd_conv_w"][0]).reshape(P, -1), "cb": cols(a["ssd_conv_b"][0]),
        "mw": fm(a["ml_conv_w"][0]).reshape(P, -1), "mb": cols(a["ml_conv_b"][0]),
        "dt_bias": rows(a["ssd_dt_bias"][0]), "a_log": rows(a["ssd_a_log"][0]), "ssd_d": rows(a["ssd_d"][0]),
        "gate_b": rows(a["ml_gate_b"][0]), "m0": m0,
    }
    vec = _np.concatenate([parts[k] for k in VECS], 1)

    wi, wo = a["w_in_even"][0], a["w_in_odd"][0]
    out_e = _np.zeros((4, P, 4096), f32)
    out_e[:, :, 0:3072] = kslots(a["w_out_even"][0], 256)
    slots = [kslots(a["w_mod"][0], 512), kslots(a["w_mod"][1], 512),
             kslots(wi[:, 0:1536], 512), kslots(wi[:, 1536:2560], 512), kslots(wi[:, 2560:4096], 512), out_e,
             kslots(wo[:, 0:3072], 512), kslots(a["w_out_odd"][0], 512)]
    wslots = _np.concatenate(slots, 0)
    wff = _np.zeros((2, 4 * NG, P, 1024), f32)
    for l in range(2):
        w1 = kslots(a["w_ff1"][l], P)
        w2 = a["w_ff2"][l].reshape(FF // P, P, D)
        wff[l, 0:4] = w1[0:4]
        for g in range(1, NG - 1):
            wff[l, 4 * g:4 * g + 2] = w2[2 * g - 2:2 * g]
            wff[l, 4 * g + 2:4 * g + 4] = w1[2 * g + 2:2 * g + 4]
        wff[l, 4 * NG - 4:4 * NG] = w2[FF // P - 4:FF // P]
    wsmall = _np.stack([kslots(wi[:, 4096:4128], 32)[0], kslots(wo[:, 3072:3104], 32)[0]], 1).reshape(P, 2, KD, 32)

    r = _np.arange(1, 15)[None, :, None]
    half = (_np.arange(P) // 64)[:, None, None]
    c = (_np.arange(P) % 64)[:, None, None]
    cc = _np.clip(_np.arange(64)[None, None, :] - c + 15, 0, 30)
    rpbT = a["na_rpb"][0][:, r - half, cc]

    kc = a["cache_na_k"][0, 0].reshape(4, 2, CTX, HD).transpose(1, 3, 0, 2).reshape(P, 4, CTX)
    vc = a["cache_na_v"][0, 0].transpose(1, 0, 2).reshape(CTX, 512)
    ssd0 = a["state_ssd"][0, 0].transpose(3, 0, 1, 2).reshape(SN, 2, SH * SP)
    mc = a["state_mlstm_c"][0, 0].reshape(2, 4, 2, MV, MQ).transpose(2, 4, 0, 1, 3)
    mn = a["state_mlstm_n"][0, 0].reshape(2, 4, 2, MQ).transpose(2, 3, 0, 1)[..., None]
    mls0 = _np.concatenate([mc, mn], -1).reshape(P, 2, 4, V1)
    xT = fm(_np.concatenate([a["x_prompt"][0], a["x_sample"][0]], 0)).reshape(P, -1)

    given = {"xT": xT, "vec": vec, "consts": row_consts(), "wslots": wslots, "wff": wff, "wsmall": wsmall, "rpbT": rpbT,
             "kcT": kc, "vc": vc, "ssd0": ssd0, "mls0": mls0}
    nc = _bacc.Bacc("TRN2", target_bir_lowering=False, num_devices=1)
    arrays, args = {}, []
    for name, x in given.items():
        x = _np.ascontiguousarray(x)
        arrays[f"in_{name}"] = x
        args.append(nc.dram_tensor(f"in_{name}", x.shape, _mybir.dt.from_np(x.dtype), kind="ExternalInput").ap())
    outs = {"y": (P, KD, T), "k": (P, 4, CTX), "v": (CTX, 512), "ssd": (SN, 2, SH * SP), "mls": (P, 2, 4, V1), "m": (ROWS, NT)}
    for name, shape in outs.items():
        args.append(nc.dram_tensor(f"out_{name}", shape, _mybir.dt.float32, kind="ExternalOutput").ap())
    hybrid_step(nc, *args)
    r = _run(nc, [arrays], core_ids=[0]).results[0]

    y = r["out_y"].transpose(2, 1, 0).reshape(T, D)
    nk = r["out_k"].reshape(2, HD, 4, CTX).transpose(2, 0, 3, 1).reshape(1, 1, NH, CTX, HD)
    nv = r["out_v"].reshape(CTX, NH, HD).transpose(1, 0, 2).reshape(1, 1, NH, CTX, HD)
    ns = r["out_ssd"].reshape(SN, 2, SH, SP).transpose(1, 2, 3, 0).reshape(1, 1, 2, SH, SP, SN)
    m = r["out_mls"].reshape(2, MQ, 2, 4, V1).transpose(2, 3, 0, 4, 1).reshape(2, MH, V1, MQ)
    nm = _np.stack([r["out_m"][0:8, 0], r["out_m"][32:40, 0]], 0).reshape(1, 1, 2, MH)
    return (y[None, 0:CTX], y[None, CTX:T], nk, nv, ns, m[:, :, 0:MV, :].reshape(1, 1, 2, MH, MV, MQ),
            m[:, :, MV, :].reshape(1, 1, 2, MH, MQ), nm)
```

```python
import numpy as np

import concourse.bass as bass
from concourse import mybir
from contextlib import ExitStack

F32 = mybir.dt.float32
F32R = mybir.dt.float32r
ALU = mybir.AluOpType
ACT = mybir.ActivationFunctionType
AX = mybir.AxisListType

P = 128
D = 1024
KD = D // P
CTX, LAT = 128, 1024
T = CTX + LAT
NT = T // P
TC = 384
NC = T // TC
EPS = 1e-6
FF = 4 * D
NH, HD = 8, 64
SH, SP, SN = 16, 64, 128
MH, MQ, MV = 8, 64, 128
V1 = MV + 1
ROWS = 40
NEG = -1e30
SEGS = [(0, 128, 0, 0), (128, 384, 1, 0), (384, 768, 1, 1), (768, 1152, 1, 2)]

CONSTS = {}


def const_table():
    k = np.arange(P)[:, None]
    i = np.arange(P)[None, :]
    parts = {
        "ident": (k == i) * 1.0,
        "ones": np.ones((P, P)),
        "le": (k <= i) * 1.0,
        "ge": (k >= i) * 1.0,
        "gt": (k > i) * 1.0,
        "lt": (k < i) * 1.0,
        "neg_f": np.where(k <= i, 0.0, NEG),
        "neg_b": np.where(k >= i, 0.0, NEG),
    }
    c = np.arange(P) % 64
    start = np.clip(c - 8, 0, 48)
    cc = np.arange(64)[None, :]
    parts["col"] = np.where((cc >= start[:, None]) & (cc < start[:, None] + 16), 0.0, NEG)
    reset = np.ones((P, NT, P))
    reset[0:8, :, 0] = 0.0
    reset[32:40, :, P - 1] = 0.0
    parts["reset"] = reset.reshape(P, -1)
    at, cols = 0, []
    for name, a in parts.items():
        CONSTS[name] = (at, a.shape[1])
        at += a.shape[1]
        cols.append(a)
    return np.concatenate(cols, 1).astype(np.float32)


def row_consts():
    base = const_table()
    row = np.arange(P)[:, None]
    m = np.arange(P)[None, :]
    half = (row % 2 == m // 64) * 1.0
    n = np.arange(8)[None, :]
    pair = (row // 32 == n // 4) & (row % 32 // 2 == n % 4)
    return np.concatenate([base, half.astype(np.float32), pair.astype(np.float32)], 1)


const_table()
NCONST = 8 * P + 64

VECS = {}
for _name, _n in [("cond", 16), ("b_mod", 96), ("norm_mix", 16), ("norm_ffn", 16), ("norm_f", 8), ("ssd_norm", 8),
                  ("cw", 36), ("cb", 12), ("mw", 24), ("mb", 8), ("dt_bias", 32), ("a_log", 32), ("ssd_d", 16),
                  ("gate_b", 32), ("m0", 1)]:
    VECS[_name] = (sum(n for _, n in VECS.values()), _n)
NVEC = sum(n for _, n in VECS.values())

S_QKV, S_Z, S_XBC, S_OUTE, S_QK, S_VO, S_OUTO = 0, 3, 5, 8, 10, 12, 16
S_MORE = 18
NMOD = 24
GH = 256
NG = FF // GH


class Count:

    def __init__(self, sem):
        self.sem, self.base = sem, 0

    def at(self, n):
        return self.base + n

    def close(self, n):
        self.base += n


class Chain:

    def __init__(self, sem):
        self.sem, self.n = sem, 0

    def one(self):
        self.n += 1
        return 1


def hybrid_step(nc, xT, vec, consts, wmod, wslots, wff, wsmall, rpbT, kcT, vc, ssd0, mls0, yT, o_k, o_v, o_ssd, o_mls, o_m):
    ctx = ExitStack()
    with ctx:
        def sb(name, shape):
            return ctx.enter_context(nc.sbuf_tensor(name, shape, F32))

        def count(name):
            return Count(ctx.enter_context(nc.semaphore(name)))

        XT = sb("XT", [P, 9288])
        CO = sb("CO", [P, NCONST])
        VE = sb("VE", [P, NVEC])
        WS = sb("WS", [P, 2, KD, 32])
        MOD = sb("MOD", [P, 2, 48, 2])
        GM = sb("GM", [P, 2, 2, KD, 2])
        SM = sb("SM", [P, 1472])

        mixer = ExitStack()

        def mixer_tensor(name, shape):
            return mixer.enter_context(nc.sbuf_tensor(name, shape, F32))

        HT = mixer_tensor("HT", [P, 9216])
        F0 = mixer_tensor("F0", [P, 9216])
        F1 = mixer_tensor("F1", [P, 9216])
        WR = mixer_tensor("WR", [P, 2, 4096])
        MI = mixer_tensor("MI", [P, 4096])
        MX = mixer_tensor("MX", [P, 2 * V1])
        PS = ctx.enter_context(nc.psum_tensor("PS", [P, 8, 512], F32))

        x_spill = nc.dram_tensor("x_spill", (P, 9216), F32).ap()
        z_spill = nc.dram_tensor("z_spill", (NT, P, D), F32).ap()
        y_spill = nc.dram_tensor("y_spill", (2, NT, P, D), F32).ap()

        def const(name):
            a, n = CONSTS[name]
            return CO[:, a:a + n]

        def vecs(name):
            a, n = VECS[name]
            return VE[:, a:a + n]

        ident, ones = const("ident"), const("ones")
        xk = XT[:, 0:9216].rearrange("p (k t) -> p k t", k=KD)
        hk = HT[:, :].rearrange("p (k t) -> p k t", k=KD)
        f0k = F0[:, :].rearrange("p (k t) -> p k t", k=8)

        w_ready = [count("w_ready0"), count("w_ready1")]
        mod_loaded = [count(f"mod_loaded{n}") for n in range(4)]
        mod_begun = count("mod_begun")
        mod_folded = count("mod_folded")
        mod_used = count("mod_used")
        mod_ready = count("mod_ready")
        o_done, o_taken = count("o_done"), count("o_taken")
        y_stored = [count("y_stored0"), count("y_stored1")]
        small_done = count("small_done")
        y_back = [count(f"y_back{n}") for n in range(5)]
        gate_act = count("gate_act")
        y_summed = count("y_summed")
        more_ready = [count("more_ready0"), count("more_ready1")]
        unit_loaded = [count("unit_loaded0"), count("unit_loaded1")]
        unit_hi = count("unit_hi")
        unit_split = count("unit_split")
        up_done, up_taken = count("up_done"), count("up_taken")
        down_done, down_taken = count("down_done"), count("down_taken")
        squared, hidden_hi, hidden_split = count("squared"), count("hidden_hi"), count("hidden_split")
        shifted, high_ready, low_ready = count("shifted"), count("high_ready"), count("low_ready")
        tile_done = count("tile_done")
        tile_free = count("tile_free")
        first_in, small_in = count("first_in"), count("small_in")
        x_in = [count(f"x_in{c}") for c in range(3)]
        spilled = count("spilled")
        xback = count("xback")
        stored = count("stored")
        loaded = count("loaded")
        cond_silu = count("cond_silu")
        squares_ready = count("squares_ready")
        squares_added = count("squares_added")
        squares_summed = count("squares_summed")
        mean_ready = count("mean_ready")
        rms_ready = count("rms_ready")
        scaled_ready = count("scaled_ready")
        scores_taken = count("scores_taken")
        scores_done = count("scores_done")
        max_ready = count("max_ready")
        probs_ready = count("probs_ready")
        probs_turned = count("probs_turned")
        probsT_ready = count("probsT_ready")
        values_summed = count("values_summed")
        output_taken = count("output_taken")
        bias_ready = count("bias_ready")
        attn_turned = count("attn_turned")
        attn_taken = count("attn_taken")
        borders_zero = count("borders_zero")
        conv_done = count("conv_done")
        silu_done = count("silu_done")
        block_turned = count("block_turned")
        turned_taken = count("turned_taken")
        softplus_dve_part = count("softplus_dve_part")
        softplus_act_part = count("softplus_act_part")
        decay_ready = count("decay_ready")
        decays_ready = count("decays_ready")
        decay_summed = count("decay_summed")
        cb_done = count("cb_done")
        cb_masked = count("cb_masked")
        masked_decay_ready = count("masked_decay_ready")
        decays_summed = count("decays_summed")
        decays_taken = count("decays_taken")
        x_scaled = count("x_scaled")
        state_read = count("state_read")
        state_out, state_in = [count(f"state_out{d}") for d in range(2)], [count(f"state_in{d}") for d in range(2)]
        weights_ready = count("weights_ready")
        chunk_summed = count("chunk_summed")
        step_taken = count("step_taken")
        update_summed = count("update_summed")
        gated = count("gated")
        square_sum_ready = count("square_sum_ready")
        gate_mean_ready = count("gate_mean_ready")
        gate_rms_ready = count("gate_rms_ready")
        gate_scaled = count("gate_scaled")
        mix_turned = count("mix_turned")
        mix_taken = count("mix_taken")
        gates_ready = count("gates_ready")
        rows_turned = count("rows_turned")
        logs_ready = count("logs_ready")
        exps_ready = count("exps_ready")
        rows_ready = count("rows_ready")
        rows_back = count("rows_back")
        exponents_done = count("exponents_done")
        exponents_masked = count("exponents_masked")
        qk_done = count("qk_done")
        exp_ready = count("exp_ready")
        scores_weighted = count("scores_weighted")
        intra_taken = count("intra_taken")
        memory_summed = count("memory_summed")
        tail_done = count("tail_done")
        values_weighted = count("values_weighted")
        intra_summed = count("intra_summed")
        z_stage = [count(f"z_stage{n}") for n in range(4)]
        bias_loaded = [count(f"bias_loaded{n}") for n in range(2)]
        gate_loaded = [count(f"gate_loaded{n}") for n in range(6)]
        dve_own = Chain(count("dve_own").sem)
        act_own = Chain(count("act_own").sem)
        pool_own = Chain(count("pool_own").sem)

        fed = [0]

        free_at = {}

        def feed(sp, upto):
            while fed[0] < upto:
                n = fed[0]
                if n >= 2:
                    sp.wait_ge(*free_at[n - 2])
                cols = 3072 if S_OUTE <= n < S_QK else 4096
                sp.dma_start(WR[:, n % 2, 0:cols], wslots[n, :, 0:cols]).then_inc(w_ready[n % 2].sem, 16)
                fed[0] += 1

        def landed(n):
            return w_ready[n % 2].sem, 16 * (n // 2 + 1)

        mod_first = [HT[:, 0:4096], HT[:, 4096:8192], F0[:, 0:4096], F0[:, 4096:8192]]
        with nc.Block() as block:
            @block.sync
            def _(sp):
                sp.dma_start(VE[:, :], vec).then_inc(first_in.sem, 16)
                sp.dma_start(CO[:, :], consts[:, 0:NCONST]).then_inc(first_in.sem, 16)
                for n in range(4):
                    sp.dma_start(mod_first[n], wmod[n, :, :]).then_inc(mod_loaded[n].sem, 16)
                for c in range(NC):
                    t = slice(c * TC, (c + 1) * TC)
                    sp.dma_start(xk[:, :, t], xT.rearrange("p (k t) -> p k t", k=KD)[:, :, t]).then_inc(x_in[c].sem, 16)
                feed(sp, 2)
                sp.dma_start(WS[:, :, :, :], wsmall).then_inc(small_in.sem, 16)

            @block.scalar
            def _(act):
                act.wait_ge(first_in.sem, 32)
                act.activation(SM[:, 0:16], vecs("cond"), ACT.Silu).then_inc(cond_silu.sem, 1)
        condT = SM[:, 0:16].rearrange("p (k c) -> p k c", k=KD)

        folds = MI[:, 0:2048].rearrange("p (s c n) -> p s c n", s=2, c=2)

        def mod_begin(act, n, w):
            if n >= 2:
                act.wait_ge(mod_used.sem, n - 1)
            for c in range(2):
                act.activation(folds[:, n % 2, c, :], w[:, 0:512], ACT.Copy, scale=condT[:, 0, c:c + 1])\
                   .then_inc(mod_begun.sem, 1)

        def mod_fold(dve, n, w, blocks):
            w = w.rearrange("p (k n) -> p k n", k=KD)
            dve.wait_ge(mod_begun.sem, 2 * n + 2)
            for k in range(1, blocks):
                for c in range(2):
                    f, g = folds[:, n % 2, c, :], condT[:, k, c:c + 1]
                    last = k == blocks - 1 and c == 1
                    if k >= 2:
                        dve.wait_ge(dve_own.sem, dve_own.n - (0 if last else 1))
                    ins = nc.vector.scalar_tensor_tensor(out=f, in0=w[:, k, :], scalar=g, in1=f, op0=ALU.mult, op1=ALU.add)
                    if last:
                        ins.then_inc(mod_folded.sem, 1)
                    else:
                        ins.then_inc(dve_own.sem, dve_own.one())

        def mod_products(pe, n, w, blocks):
            pe.wait_ge(mod_folded.sem, n + 1)
            w = w.rearrange("p (k n) -> p k n", k=KD)
            for j in range(4):
                at, cols = 8 * n + 2 * j, slice(j * P, (j + 1) * P)
                for k in range(blocks, KD):
                    nc.tensor.matmul(PS[:, 7, 256 + at:258 + at], w[:, k, cols], condT[:, k, :],
                                     start=(k == blocks), stop=(k == KD - 1))
                for c in range(2):
                    mm = nc.tensor.matmul(PS[:, 7, at + c:at + c + 1], folds[:, n % 2, c, cols], ones[:, 0:1],
                                          start=True, stop=True)
            mm.then_inc(mod_used.sem, 1)

        def mod_values(dve, l, j0, j1, halves=1):
            raw = PS[:, 7, 96 * l:96 * l + 96].rearrange("p (j c) -> p j c", c=2)
            b = vecs("b_mod").rearrange("p (l j) -> p l j", l=2)[:, l, :]
            for c in range(2):
                nc.vector.tensor_tensor(MOD[:, l, j0:j1, c], raw[:, j0:j1, c], b[:, j0:j1], ALU.add)\
                  .then_inc(dve_own.sem, dve_own.one())
            dve.wait_ge(dve_own.sem, dve_own.n)
            if halves == 2:
                more = PS[:, 7, 256 + 96 * l:352 + 96 * l].rearrange("p (j c) -> p j c", c=2)
                nc.vector.tensor_tensor(MOD[:, l, j0:j1, :], MOD[:, l, j0:j1, :], more[:, j0:j1, :], ALU.add)\
                  .then_inc(dve_own.sem, dve_own.one())
                dve.wait_ge(dve_own.sem, dve_own.n)

        def mod_gains(dve, l, n):
            g = vecs(("norm_mix", "norm_ffn")[n]).rearrange("p (l k) -> p l k", l=2)[:, l, :]
            for c in range(2):
                nc.vector.scalar_tensor_tensor(out=GM[:, l, n, :, c], in0=MOD[:, l, (3 * n + 1) * 8:(3 * n + 1) * 8 + 8, c],
                                               scalar=1.0, in1=g, op0=ALU.add, op1=ALU.mult)\
                  .then_inc(dve_own.sem, dve_own.one())

        def norm_squares(act, c, SQ, places=8):
            for i in range(c * KD, (c + 1) * KD):
                if i >= places:
                    act.wait_ge(squares_summed.sem, squares_summed.at(i - 7))
                act.activation(SQ[:, i % places, :], xk[:, i % KD, c * TC:(c + 1) * TC], ACT.Square)\
                   .then_inc(squares_ready.sem, 1)

        def norm_sums(pe, c, SQ, bank):
            for i in range(c * KD, (c + 1) * KD):
                pe.wait_ge(squares_ready.sem, squares_ready.at(i + 1))
                nc.tensor.matmul(PS[:, bank, 0:TC], ones, SQ[:, i % 8, :], start=(i % KD == 0),
                                 stop=(i % KD == KD - 1)).then_inc(squares_summed.sem, 1)

        def norm_mean(dve, c, RB, bank):
            dve.wait_ge(squares_summed.sem, squares_summed.at(KD * (c + 1)))
            r = RB[:, c * TC:(c + 1) * TC]
            nc.vector.tensor_scalar(r, PS[:, bank, 0:TC], 1.0 / D, EPS, ALU.mult, ALU.add)\
              .then_inc(dve_own.sem, dve_own.one())
            dve.wait_ge(dve_own.sem, dve_own.n)
            nc.vector.reciprocal(r, r).then_inc(mean_ready.sem, 1)

        def norm_root(act, c, RB):
            act.wait_ge(mean_ready.sem, mean_ready.at(c + 1))
            act.activation(RB[:, c * TC:(c + 1) * TC], RB[:, c * TC:(c + 1) * TC], ACT.Sqrt).then_inc(rms_ready.sem, 1)

        def norm(l, which, dst, SQ, RB, upto, split=None, final=False, first=False, done=0):
            with nc.Block() as block:
                @block.sync
                def _(sp):
                    if final:
                        for s, (a, b, _, _) in enumerate(SEGS):
                            sp.wait_ge(scaled_ready.sem, scaled_ready.at(KD * (s + 1)))
                            sp.dma_start(yT[:, :, a:b], dst[:, :, a:b]).then_inc(stored.sem, 16)
                        sp.wait_ge(stored.sem, stored.at(64))
                    elif upto:
                        feed(sp, upto)
                    else:
                        for s in range(2):
                            sp.dma_start(raw_unit[:, s, :], wff[l, s, :, :]).then_inc(unit_loaded[s].sem, 16)

                @block.scalar
                def _(act):
                    def shifts(s):
                        a, b, c, _ = SEGS[s]
                        for n in range(s * KD, (s + 1) * KD):
                            k = n % KD
                            act.wait_ge(scaled_ready.sem, scaled_ready.at(n + 1))
                            x = split[0][:, n % 4, 0:b - a] if split else dst[:, k, a:b]
                            y = split[0][:, 4 + n % 4, 0:b - a] if split else x
                            if split and n >= 4:
                                act.wait_ge(low_ready.sem, low_ready.at(n - 3))
                            act.activation(y, x, ACT.Identity, bias=MOD[:, l, 24 * which + k, c:c + 1])\
                               .then_inc(shifted.sem, 1)

                    if first:
                        for n in range(4):
                            act.wait_ge(mod_loaded[n].sem, 16)
                            mod_begin(act, n, mod_first[n])
                    for c in range(done, NC):
                        if first:
                            act.wait_ge(x_in[c].sem, 16)
                        norm_squares(act, c, SQ)
                        if c == 1:
                            norm_root(act, 0, RB)
                    if first:
                        act.wait_ge(mod_ready.sem, mod_ready.at(1))
                    for s in range(4):
                        if not final:
                            shifts(s)
                        if done <= s + 1 < NC:
                            norm_root(act, s + 1, RB)

                @block.tensor
                def _(pe):
                    if first:
                        for n in range(3):
                            mod_products(pe, n, mod_first[n], 6)
                    for c in range(done, NC):
                        norm_sums(pe, c, SQ, c)
                        if first and c == 0:
                            mod_products(pe, 3, mod_first[3], 6)

                @block.vector
                def _(dve):
                    def high(n):
                        a, b, cond, _ = SEGS[n // KD]
                        dve.wait_ge(scaled_ready.sem, scaled_ready.at(n + 1))
                        nc.vector.tensor_scalar(split[1][:, n % KD, a:b], split[0][:, n % 4, 0:b - a],
                                                MOD[:, l, 24 * which + n % KD, cond:cond + 1], None, ALU.add)\
                          .then_inc(high_ready.sem, 1)

                    if first:
                        for n in range(4):
                            dve.wait_ge(mod_loaded[n].sem, 16)
                            mod_fold(dve, n, mod_first[n], 6)
                    if not done:
                        norm_mean(dve, 0, RB, 0)
                    if first:
                        dve.wait_ge(x_in[0].sem, 16)
                        dve.wait_ge(mod_used.sem, 4)
                        mod_values(dve, 0, 0, 16, halves=2)
                        mod_gains(dve, 0, 0)
                        dve.wait_ge(dve_own.sem, dve_own.n)
                        dve.sem_inc(mod_ready.sem, 1)

                    n = 0
                    for a, b, cond, c in SEGS:
                        if n and max(done, 1) <= n // KD < NC:
                            norm_mean(dve, n // KD, RB, n // KD)
                        dve.wait_ge(rms_ready.sem, rms_ready.at(c + 1))
                        if first and c > 0 and a == c * TC:
                            dve.wait_ge(x_in[c].sem, 16)
                        for k in range(KD):
                            if split and n >= 4:
                                dve.wait_ge(shifted.sem, shifted.at(n - 3))
                            g = vecs("norm_f")[:, k:k + 1] if final else GM[:, l, which, k, cond:cond + 1]
                            y = split[0][:, n % 4, 0:b - a] if split else dst[:, k, a:b]
                            nc.vector.scalar_tensor_tensor(out=y, in0=xk[:, k, a:b], scalar=g,
                                                           in1=RB[:, a:b], op0=ALU.mult, op1=ALU.mult)\
                              .then_inc(scaled_ready.sem, 1)
                            if split and n >= 1:
                                high(n - 1)
                            n += 1
                    if split:
                        high(n - 1)

                @block.gpsimd
                def _(pool):
                    if split:
                        for n in range(4 * KD):
                            a, b, _, _ = SEGS[n // KD]
                            pool.wait_ge(shifted.sem, shifted.at(n + 1))
                            pool.wait_ge(high_ready.sem, high_ready.at(n + 1))
                            nc.gpsimd.tensor_tensor(split[2][:, n % KD, a:b], split[0][:, 4 + n % 4, 0:b - a],
                                                    split[1][:, n % KD, a:b].bitcast(F32), ALU.subtract)\
                              .then_inc(low_ready.sem, 1)
            squares_ready.close(24)
            squares_summed.close(24)
            mean_ready.close(NC)
            rms_ready.close(NC)
            scaled_ready.close(4 * KD)
            if final:
                stored.close(64)
            else:
                shifted.close(4 * KD)
            if split:
                high_ready.close(4 * KD)
                low_ready.close(4 * KD)

        def tile_products(pe, i, m, n, terms, banks=8):
            if i >= banks:
                pe.wait_ge(tile_free.sem, tile_free.at(i - banks + 1))
            for t, (lhs, rhs) in enumerate(terms):
                mm = nc.tensor.matmul(PS[0:m, i % banks, 0:n], lhs, rhs, start=(t == 0), stop=(t == len(terms) - 1))
            mm.then_inc(tile_done.sem, 1)

        def feature_tile(pe, i, w, col, c, banks=8):
            tile_products(pe, i, P, TC, [(w[:, k, col:col + P], hk[:, k, c * TC:(c + 1) * TC]) for k in range(KD)], banks)

        def token_tile(pe, i, w, t, banks=8):
            tile_products(pe, i, P, 512, [(hk[:, k, t * P:(t + 1) * P], w[:, k, :]) for k in range(KD)], banks)

        def slot_k(n):
            return WR[:, n % 2, :].rearrange("p (k n) -> p k n", k=KD)

        def frees(slots, per_slot):
            at = 0
            for n, k in zip(slots, per_slot):
                at += k
                free_at[n] = (tile_done.sem, tile_done.at(at))

        def close_tiles(n):
            tile_done.close(n)
            tile_free.close(n)

        zst = MI[:, 0:2048].rearrange("p (s n) -> p s n", s=4)

        def gate_product(pe, q, s0, banks):
            i, k = q // KD, q % KD
            s, t = i // NT, i % NT
            if k == 0:
                if t == 0:
                    pe.wait_ge(*landed(s0 + s))
                if i >= 2:
                    pe.wait_ge(o_taken.sem, o_taken.at(i - 1))
            mm = nc.tensor.matmul(PS[:, banks[i % 2], :], hk[:, k, t * P:(t + 1) * P], slot_k(s0 + s)[:, k, :],
                                  start=(k == 0), stop=(k == KD - 1))
            if k == KD - 1:
                mm.then_inc(o_done.sem, 1)

        def gate_take(act, i, banks):
            act.wait_ge(o_done.sem, o_done.at(i + 1))
            if i >= 4:
                act.wait_ge(z_stage[i % 4].sem, z_stage[i % 4].at(16 * (i // 4)))
            act.activation(zst[:, i % 4, :], PS[:, banks[i % 2], :], ACT.Copy).then_inc(o_taken.sem, 1)

        def gate_store(sp, i):
            s, t = i // NT, i % NT
            sp.wait_ge(o_taken.sem, o_taken.at(i + 1))
            sp.dma_start(z_spill[t, :, s * 512:(s + 1) * 512], zst[:, i % 4, :]).then_inc(z_stage[i % 4].sem, 16)

        def gate_stored(sp):
            for n in range(4):
                sp.wait_ge(z_stage[n].sem, z_stage[n].at(16 * len(range(n, 18, 4))))

        def close_gate():
            for n in range(4):
                z_stage[n].close(16 * len(range(n, 18, 4)))
            o_done.close(18)
            o_taken.close(18)

        def norm_mixer(l, upto):
            norm(l, 0, hk, F1[:, 4608:7680].rearrange("p (n t) -> p n t", n=8), F1[:, 7680:7680 + T], upto, first=(l == 0))

        norm_mixer(0, S_QKV + 2)
        for n in range(4):
            mod_loaded[n].close(16)

        qT = F0[:, 0:4608].rearrange("p (b t) -> p b t", b=4)
        kT = F0[:, 4608:9216].rearrange("p (b t) -> p b t", b=4)
        vtok = F1[:, 0:4608].rearrange("p (t n) -> p t n", t=NT)
        mod_place = [F1[:, 4608:8704], XT[:, 0:4096], XT[:, 4096:8192]]
        frees(range(S_QKV, S_Z), (12, 12, 9))
        for s in range(2):
            free_at[S_Z + s] = (o_done.sem, o_done.at(NT * (s + 1)))

        with nc.Block() as block:
            @block.sync
            def _(sp):
                def mod_load(n):
                    sp.dma_start(mod_place[(n - 4) % 3], wmod[n, :, :]).then_inc(mod_loaded[(n - 4) % 3].sem, 16)

                mod_load(4)
                sp.dma_start(x_spill, XT[:, 0:9216]).then_inc(spilled.sem, 16)
                sp.wait_ge(spilled.sem, spilled.at(16))
                mod_load(5)
                mod_load(6)
                for n in range(7, NMOD):
                    if n in (12, 20):
                        feed(sp, S_Z if n == 12 else S_Z + 1)
                    sp.wait_ge(mod_folded.sem, n - 2)
                    mod_load(n)
                feed(sp, S_XBC)

            @block.tensor
            def _(pe):
                i, n = 0, 4
                for s in range(3):
                    pe.wait_ge(*landed(S_QKV + s))
                    for j in range(12 if s < 2 else NT):
                        if s < 2:
                            feature_tile(pe, i, slot_k(S_QKV + s), (j // NC) * P, j % NC, banks=7)
                        else:
                            token_tile(pe, i, slot_k(S_QKV + s), j, banks=7)
                        i += 1
                        if n < NMOD and 2 * i >= 8 + 3 * (n - 4):
                            mod_products(pe, n, mod_place[(n - 4) % 3], KD)
                            n += 1
                assert n == NMOD

            @block.scalar
            def _(act):
                n = 4
                for i in range(33):
                    if n < NMOD and 2 * i >= 3 * (n - 4):
                        place = mod_loaded[(n - 4) % 3]
                        act.wait_ge(place.sem, place.at(16 * ((n - 4) // 3 + 1)))
                        mod_begin(act, n, mod_place[(n - 4) % 3])
                        n += 1
                    act.wait_ge(tile_done.sem, tile_done.at(i + 1))
                    s, b, c = i // 12, i % 12 // NC, i % NC
                    if s < 2:
                        act.activation((qT, kT)[s][:, b, c * TC:(c + 1) * TC], PS[:, i % 7, 0:TC], ACT.Copy,
                                       scale=(HD ** -0.5, 1.0)[s]).then_inc(tile_free.sem, 1)
                    else:
                        act.activation(vtok[:, i - 24, :], PS[:, i % 7, :], ACT.Copy).then_inc(tile_free.sem, 1)
                assert n == NMOD

            @block.vector
            def _(dve):
                for n in range(4, NMOD):
                    place = mod_loaded[(n - 4) % 3]
                    dve.wait_ge(place.sem, place.at(16 * ((n - 4) // 3 + 1)))
                    mod_fold(dve, n, mod_place[(n - 4) % 3], KD)
                dve.wait_ge(mod_used.sem, NMOD)
                mod_values(dve, 0, 16, 48)
                mod_values(dve, 1, 0, 48)
                for l, n in ((0, 1), (1, 0), (1, 1)):
                    mod_gains(dve, l, n)
        close_tiles(33)
        spilled.close(16)

        T2 = F1[:, 4608:6400].rearrange("p (s r c) -> p s r c", s=2, r=14)
        TI = F1[:, 6400:7552].rearrange("p (s r c) -> p s r c", s=2, r=9)
        kcT_sb = F1[:, 7552:8064].rearrange("p (b t) -> p b t", b=4)
        vc_sb = F1[:, 8064:8576]
        yna = XT[:, 0:4608].rearrange("p (t n) -> p t n", t=NT)
        SS = XT[:, 4608:6016].rearrange("p (s n) -> p s n", s=2)
        PT = XT[:, 6016:7552].rearrange("p (s n) -> p s n", s=2)
        mx, nmx, rs, ri = (XT[:, 7552 + 2 * n:7554 + 2 * n] for n in range(4))
        ynaT = F1[:, 4608:9216].rearrange("p (b t) -> p b t", b=4)
        NA = 72

        def na_step(n):
            if n >= 64:
                return n - 64, 0, False, 0, 0
            h, j = n // 8, n % 8
            s = min(max(2 * j - 4, 0), 8)
            return h, s // 2, 2 <= j <= 5, s - 2 * j + 6, 1 + j

        def width(n):
            return 128 if n >= 64 else (704 if na_step(n)[2] else 640)

        def chunks(n):
            h, kt, nine, _, _ = na_step(n)
            v = slice(h * HD, (h + 1) * HD)
            if n >= 64:
                return [(0, P, vtok[:, 0, v])]
            out = [(i * P, P, vtok[:, 1 + kt + i, v]) for i in range(4)] + [(512, P, vc_sb[:, v])]
            if nine:
                out.append((640, 64, vtok[0:64, 1 + kt + 4, v]))
            return out

        with nc.Block() as block:
            @block.sync
            def _(sp):
                sp.dma_start(kcT_sb, kcT).then_inc(loaded.sem, 16)
                sp.dma_start(vc_sb, vc).then_inc(loaded.sem, 16)
                sp.dma_start(o_k, kT[:, :, 0:P]).then_inc(stored.sem, 16)
                sp.dma_start(o_v, vtok[:, 0, :]).then_inc(stored.sem, 16)

                def bias_load(h):
                    if h >= 2:
                        sp.wait_ge(scores_taken.sem, scores_taken.at(8 * (h - 1)))
                        sp.wait_ge(bias_ready.sem, bias_ready.at(h - 1))
                    sp.dma_start(T2[:, h % 2, :, :], rpbT[h]).then_inc(bias_loaded[h % 2].sem, 16)

                bias_load(0)
                bias_load(1)
                for i in range(2 * NT):
                    if i >= 2 and i % 2 == 0 and i // 2 + 1 < NH:
                        bias_load(i // 2 + 1)
                    gate_store(sp, i)
                gate_stored(sp)
                feed(sp, S_XBC + 2)
                sp.wait_ge(stored.sem, stored.at(32))

            @block.gpsimd
            def _(pool):
                col = const("col").unsqueeze(1)
                for h in range(NH):
                    pool.wait_ge(bias_loaded[h % 2].sem, bias_loaded[h % 2].at(16 * (h // 2 + 1)))
                    if h >= 2:
                        pool.wait_ge(scores_taken.sem, scores_taken.at(8 * (h - 1)))
                    nc.gpsimd.tensor_tensor(T2[:, h % 2, :, :], T2[:, h % 2, :, :],
                                                            col.broadcast_to((P, 14, 64)), ALU.add).then_inc(pool_own.sem, pool_own.one())
                    pool.wait_ge(pool_own.sem, pool_own.n)
                    nc.gpsimd.tensor_copy(TI[:, h % 2, :, :], T2[:, h % 2, 2:11, :]).then_inc(pool_own.sem, pool_own.one())
                    pool.wait_ge(pool_own.sem, pool_own.n)
                    nc.gpsimd.memset(TI[0:64, h % 2, 8, :], NEG).then_inc(pool_own.sem, pool_own.one())
                    nc.gpsimd.memset(TI[64:128, h % 2, 0, :], NEG).then_inc(pool_own.sem, pool_own.one())
                    pool.wait_ge(pool_own.sem, pool_own.n)
                    pool.sem_inc(bias_ready.sem, 1)

            @block.tensor
            def _(pe):
                def scores(n):
                    h, kt, nine, _, qt = na_step(n)
                    r = slice(64 * (h % 2), 64 * (h % 2) + 64)
                    q = qT[r, h // 2, qt * P:(qt + 1) * P]
                    b = 2 * (n % 2)
                    if n >= 2:
                        pe.wait_ge(scores_taken.sem, scores_taken.at(n - 1))
                    if n >= 3:
                        pe.wait_ge(output_taken.sem, output_taken.at(n - 2))
                    if n >= 64:
                        nc.tensor.matmul(PS[:, b, 0:P], q, kT[r, h // 2, 0:P], start=True, stop=True).then_inc(scores_done.sem, 1)
                        return
                    if n == 0:
                        pe.wait_ge(loaded.sem, loaded.at(32))
                    k0 = (1 + kt) * P
                    nc.tensor.matmul(PS[:, b, :], q, kT[r, h // 2, k0:k0 + 512], start=True, stop=True)
                    mm = nc.tensor.matmul(PS[:, b + 1, 0:P], q, kcT_sb[r, h // 2, :], start=True, stop=True)
                    if nine:
                        mm = nc.tensor.matmul(PS[:, b + 1, P:P + 64], q, kT[r, h // 2, k0 + 512:k0 + 576],
                                              start=True, stop=True)
                    mm.then_inc(scores_done.sem, 1)

                def turn(n):
                    pe.wait_ge(probs_ready.sem, probs_ready.at(n + 1))
                    if n >= 1:
                        pe.wait_ge(probsT_ready.sem, probsT_ready.at(n))
                    for i, (a, m, _) in enumerate(chunks(n)):
                        mm = nc.tensor.transpose(PS[0:m, 4 + i // 4, (i % 4) * P:(i % 4) * P + P],
                                                 SS[:, n % 2, a:a + m], ident)
                    mm.then_inc(probs_turned.sem, 1)

                def values(n):
                    pe.wait_ge(probsT_ready.sem, probsT_ready.at(n + 1))
                    if n >= 2:
                        pe.wait_ge(output_taken.sem, output_taken.at(n - 1))
                    cs = chunks(n)
                    for i, (_, m, v) in enumerate(cs):
                        mm = nc.tensor.matmul(PS[:, 2 * ((n + 1) % 2) + 1, 256:256 + HD], PT[0:m, n % 2, i * P:(i + 1) * P], v,
                                              start=(i == 0), stop=(i == len(cs) - 1))
                    mm.then_inc(values_summed.sem, 1)

                scores(0)
                for n in range(NA):
                    gate_product(pe, 2 * n, S_Z, (6, 7))
                    if n + 1 < NA:
                        scores(n + 1)
                    turn(n)
                    gate_product(pe, 2 * n + 1, S_Z, (6, 7))
                    if n >= 1:
                        values(n - 1)
                values(NA - 1)

            @block.vector
            def _(dve):
                def softmax_max(n):
                    h, _, nine, r0, _ = na_step(n)
                    b = 2 * (n % 2)
                    dve.wait_ge(scores_done.sem, scores_done.at(n + 1))
                    if n >= 2:
                        dve.wait_ge(probs_turned.sem, probs_turned.at(n - 1))
                    s = SS[:, n % 2, :]
                    if n >= 64:
                        nc.vector.tensor_copy(s[:, 0:P], PS[:, b, 0:P]).then_inc(scores_taken.sem, 1)
                    else:
                        if n % 8 == 0:
                            dve.wait_ge(bias_ready.sem, bias_ready.at(h + 1))
                        bias = (TI[:, h % 2, :, :] if nine else T2[:, h % 2, r0:r0 + 8, :]).rearrange("p r c -> p (r c)")
                        nc.vector.tensor_tensor(s[:, 0:512], PS[:, b, :], bias[:, 0:512], ALU.add).then_inc(dve_own.sem, dve_own.one())
                        if nine:
                            nc.vector.tensor_tensor(s[:, 640:704], PS[:, b + 1, P:P + 64],
                                                                   bias[:, 512:576], ALU.add).then_inc(dve_own.sem, dve_own.one())
                        dve.wait_ge(dve_own.sem, dve_own.n)
                        nc.vector.tensor_copy(s[:, 512:640], PS[:, b + 1, 0:P]).then_inc(scores_taken.sem, 1)
                    dve.wait_ge(scores_taken.sem, scores_taken.at(n + 1))
                    nc.vector.tensor_reduce(mx[:, n % 2:n % 2 + 1], s[:, 0:width(n)], AX.X, ALU.max).then_inc(dve_own.sem, dve_own.one())
                    dve.wait_ge(dve_own.sem, dve_own.n)
                    nc.vector.tensor_scalar(nmx[:, n % 2:n % 2 + 1], mx[:, n % 2:n % 2 + 1], -1.0, None, ALU.mult)\
                      .then_inc(max_ready.sem, 1)

                def normalise(n):
                    h, _, _, _, qt = na_step(n)
                    dve.wait_ge(values_summed.sem, values_summed.at(n + 1))
                    nc.vector.reciprocal(ri[:, n % 2:n % 2 + 1], rs[:, n % 2:n % 2 + 1]).then_inc(dve_own.sem, dve_own.one())
                    dve.wait_ge(dve_own.sem, dve_own.n)
                    nc.vector.tensor_scalar(yna[:, qt, h * HD:(h + 1) * HD], PS[:, 2 * ((n + 1) % 2) + 1, 256:256 + HD],
                                            ri[:, n % 2:n % 2 + 1], None, ALU.mult).then_inc(output_taken.sem, 1)

                for n in range(NA):
                    softmax_max(n)
                    if n >= 2:
                        normalise(n - 2)
                normalise(NA - 2)
                normalise(NA - 1)

            @block.scalar
            def _(act):
                def probs(n):
                    act.wait_ge(max_ready.sem, max_ready.at(n + 1))
                    if n >= 2:
                        act.wait_ge(output_taken.sem, output_taken.at(n - 1))
                    s = SS[:, n % 2, 0:width(n)]
                    act.activation(s, s, ACT.Exp, bias=nmx[:, n % 2:n % 2 + 1], accum_out=rs[:, n % 2:n % 2 + 1])\
                       .then_inc(probs_ready.sem, 1)

                def take(n):
                    act.wait_ge(probs_turned.sem, probs_turned.at(n + 1))
                    if n >= 2:
                        act.wait_ge(values_summed.sem, values_summed.at(n - 1))
                    cs = chunks(n)
                    k = min(len(cs), 4) * P
                    ins = act.activation(PT[:, n % 2, 0:k], PS[:, 4, 0:k], ACT.Copy)
                    if len(cs) > 5:
                        ins = act.activation(PT[0:64, n % 2, 640:768], PS[0:64, 5, P:2 * P], ACT.Copy)
                    if len(cs) > 4:
                        ins.then_inc(act_own.sem, act_own.one())
                        ins = act.activation(PT[:, n % 2, 512:640], PS[:, 5, 0:P], ACT.Copy)
                    ins.then_inc(probsT_ready.sem, 1)

                probs(0)
                for n in range(1, NA):
                    take(n - 1)
                    probs(n)
                    if n % 4 == 0:
                        gate_take(act, n // 4 - 1, (6, 7))
                take(NA - 1)
                gate_take(act, 2 * NT - 1, (6, 7))
        loaded.close(32)
        stored.close(32)
        close_gate()
        bias_loaded[0].close(64)
        bias_loaded[1].close(64)
        for e in (scores_taken, scores_done, max_ready, probs_ready, probs_turned, probsT_ready, values_summed, output_taken):
            e.close(NA)
        bias_ready.close(NH)

        with nc.Block() as block:
            @block.tensor
            def _(pe):
                for t in range(NT):
                    if t >= 4:
                        pe.wait_ge(attn_taken.sem, attn_taken.at(t - 3))
                    for b in range(4):
                        mm = nc.tensor.transpose(PS[:, t % 4, b * P:(b + 1) * P], yna[:, t, b * P:(b + 1) * P], ident)
                    mm.then_inc(attn_turned.sem, 1)

            @block.scalar
            def _(act):
                for t in range(NT):
                    act.wait_ge(attn_turned.sem, attn_turned.at(t + 1))
                    act.activation(ynaT[:, :, t * P:(t + 1) * P], PS[:, t % 4, :].rearrange("p (b n) -> p b n", b=4),
                                   ACT.Copy).then_inc(attn_taken.sem, 1)
        attn_turned.close(NT)
        attn_taken.close(NT)

        def softplus_dve(dve, x, out, s):
            e, u, l, d, r = (s[:, n, :] for n in range(1, 6))

            def chained(ins):
                ins.then_inc(dve_own.sem, dve_own.one())
                dve.wait_ge(dve_own.sem, dve_own.n)
            dve.wait_ge(softplus_act_part.sem, softplus_act_part.at(1))
            nc.vector.tensor_scalar(u, e, 1.0, None, ALU.add).then_inc(softplus_dve_part.sem, 1)
            dve.wait_ge(softplus_dve_part.sem, softplus_dve_part.at(2))
            chained(nc.vector.tensor_scalar(d, u, -1.0, None, ALU.add))
            chained(nc.vector.tensor_scalar(r, d, 1e-30, None, ALU.max))
            chained(nc.vector.reciprocal(r, r))
            chained(nc.vector.tensor_tensor(r, r, e, ALU.mult))
            dve.wait_ge(softplus_act_part.sem, softplus_act_part.at(2))
            chained(nc.vector.tensor_tensor(r, r, l, ALU.mult))
            chained(nc.vector.scalar_tensor_tensor(out=d, in0=d, scalar=0.0, in1=e, op0=ALU.is_equal, op1=ALU.mult))
            chained(nc.vector.tensor_tensor(d, d, r, ALU.add))
            chained(nc.vector.scalar_tensor_tensor(out=out, in0=x, scalar=0.0, in1=d, op0=ALU.max, op1=ALU.add))

        def softplus_act(act, x, s):
            a, e, u, l = (s[:, n, :] for n in range(4))
            act.wait_ge(softplus_dve_part.sem, softplus_dve_part.at(1))
            act.activation(a, x, ACT.Abs).then_inc(act_own.sem, act_own.one())
            act.wait_ge(act_own.sem, act_own.n)
            act.activation(e, a, ACT.Exp, scale=-1.0).then_inc(softplus_act_part.sem, 1)
            act.wait_ge(softplus_dve_part.sem, softplus_dve_part.at(2))
            act.activation(l, u, ACT.Ln).then_inc(softplus_act_part.sem, 1)

        def small_products(pe, l, tiles):
            for t in tiles:
                for k in range(KD):
                    mm = nc.tensor.matmul(PS[:, 4, 32 * t:32 * t + 32], hk[:, k, t * P:(t + 1) * P], WS[:, l, k, :],
                                          start=(k == 0), stop=(k == KD - 1))
                if t == NT - 1:
                    mm.then_inc(small_done.sem, 1)

        def conv_phase(s0, nblocks, raw, cv, silu_out, turned, w, bias, l, small_act, small_dve):
            turns = [b for b in range(nblocks) if turned(b) is not None]
            if l == 0:
                small_tiles, small_after = [range(b - 1, b) if 1 <= b <= NT else range(0) for b in range(nblocks)], 10
            else:
                small_tiles, small_after = [range(2 * b, min(2 * b + 2, NT)) for b in range(nblocks)], 5
            frees(range(s0, s0 + nblocks // 4), [12] * (nblocks // 4))
            with nc.Block() as block:
                @block.sync
                def _(sp):
                    if l == 1:
                        sp.dma_start(x_spill, XT[:, 0:9216]).then_inc(spilled.sem, 16)
                        sp.wait_ge(spilled.sem, spilled.at(16))
                    feed(sp, s0 + nblocks // 4 + (2 if s0 == S_QK else 0))

                @block.gpsimd
                def _(pool):
                    for n in range(2):
                        for a, z in ((0, 1), (129, 131), (1155, 1156)):
                            nc.gpsimd.memset(raw[:, n, a:z], 0.0).then_inc(borders_zero.sem, 1)

                @block.tensor
                def _(pe):
                    def turn(b):
                        n = turns.index(b)
                        pe.wait_ge(silu_done.sem, silu_done.at(b + 1))
                        for c in range(3):
                            j = 3 * n + c
                            if j >= 3:
                                pe.wait_ge(turned_taken.sem, turned_taken.at(j - 2))
                            for t in range(3):
                                mm = nc.tensor.transpose(PS[:, 5 + j % 3, t * P:(t + 1) * P],
                                                         silu_out(b)[:, (3 * c + t) * P:(3 * c + t + 1) * P], ident)
                            mm.then_inc(block_turned.sem, 1)

                    pe.wait_ge(small_in.sem, 16)
                    for b in range(nblocks):
                        if b % 4 == 0:
                            pe.wait_ge(*landed(s0 + b // 4))
                        for c in range(NC):
                            feature_tile(pe, b * NC + c, slot_k(s0 + b // 4), (b % 4) * P, c, banks=4)
                        small_products(pe, l, small_tiles[b])
                        if b >= 1 and (b - 1) in turns:
                            turn(b - 1)
                    if nblocks - 1 in turns:
                        turn(nblocks - 1)

                @block.scalar
                def _(act):
                    def silu(b):
                        act.wait_ge(conv_done.sem, conv_done.at(b + 1))
                        if turned(b) is not None and turns.index(b) >= 2:
                            act.wait_ge(block_turned.sem, block_turned.at(3 * (turns.index(b) - 1)))
                        dst = silu_out(b)
                        act.activation(dst[:, 0:CTX], cv[:, b % 2, 0:CTX], ACT.Silu).then_inc(act_own.sem, act_own.one())
                        act.activation(dst[:, CTX:T], cv[:, b % 2, CTX + 2:T + 2], ACT.Silu).then_inc(silu_done.sem, 1)

                    act.wait_ge(borders_zero.sem, borders_zero.at(6))
                    for b in range(nblocks):
                        if b >= 2:
                            act.wait_ge(conv_done.sem, conv_done.at(b - 1))
                        for c in range(NC):
                            i = b * NC + c
                            act.wait_ge(tile_done.sem, tile_done.at(i + 1))
                            r = raw[:, b % 2, :]
                            if c == 0:
                                act.activation(r[:, 1:129], PS[:, i % 4, 0:CTX], ACT.Copy).then_inc(act_own.sem, act_own.one())
                                act.activation(r[:, 131:387], PS[:, i % 4, CTX:TC], ACT.Copy).then_inc(tile_free.sem, 1)
                            else:
                                act.activation(r[:, c * TC + 3:(c + 1) * TC + 3], PS[:, i % 4, 0:TC], ACT.Copy)\
                                   .then_inc(tile_free.sem, 1)
                        if b >= 1:
                            silu(b - 1)
                        if b == small_after:
                            small_act(act)
                    silu(nblocks - 1)

                @block.vector
                def _(dve):
                    def take(b):
                        n = turns.index(b)
                        for c in range(3):
                            dve.wait_ge(block_turned.sem, block_turned.at(3 * n + c + 1))
                            nc.vector.tensor_copy(turned(b)[:, 3 * c:3 * c + 3, :],
                                                  PS[:, 5 + (3 * n + c) % 3, 0:TC].rearrange("p (t n) -> p t n", t=3))\
                              .then_inc(turned_taken.sem, 1)

                    dve.wait_ge(borders_zero.sem, borders_zero.at(6))
                    for b in range(nblocks):
                        dve.wait_ge(tile_free.sem, tile_free.at(NC * (b + 1)))
                        if b >= 2:
                            dve.wait_ge(silu_done.sem, silu_done.at(b - 1))
                        r, o = raw[:, b % 2, :], cv[:, b % 2, :]
                        nc.vector.tensor_scalar(o, r[:, 1:1155], w[:, b, 1:2], bias[:, b:b + 1],
                                                               ALU.mult, ALU.add).then_inc(dve_own.sem, dve_own.one())
                        dve.wait_ge(dve_own.sem, dve_own.n)
                        nc.vector.scalar_tensor_tensor(out=o, in0=r[:, 0:1154], scalar=w[:, b, 0:1],
                                                                      in1=o, op0=ALU.mult, op1=ALU.add).then_inc(dve_own.sem, dve_own.one())
                        dve.wait_ge(dve_own.sem, dve_own.n)
                        nc.vector.scalar_tensor_tensor(out=o, in0=r[:, 2:1156], scalar=w[:, b, 2:3],
                                                       in1=o, op0=ALU.mult, op1=ALU.add).then_inc(conv_done.sem, 1)
                        if b >= 1 and (b - 1) in turns:
                            take(b - 1)
                        if b == small_after:
                            small_dve(dve)
                    if nblocks - 1 in turns:
                        take(nblocks - 1)
            close_tiles(NC * nblocks)
            small_done.close(1)
            softplus_dve_part.close(2)
            softplus_act_part.close(2)
            borders_zero.close(6)
            conv_done.close(nblocks)
            silu_done.close(nblocks)
            block_turned.close(3 * len(turns))
            turned_taken.close(3 * len(turns))

        xs = F0[:, :].rearrange("p (t n) -> p t n", t=NT)
        bcT = F1[:, 0:4608].rearrange("p (b t) -> p b t", b=4)
        btok = XT[:, 0:2304].rearrange("p (t n) -> p t n", t=NT)
        cs = XT[:, 6924:9228].rearrange("p (s t) -> p s t", s=2)

        DT, DTA, ECUM, WEND, TOT = (SM[:, 16 + 288 * n:304 + 288 * n].rearrange("p (t c) -> p t c", t=NT) for n in range(5))
        flat = lambda a: a.rearrange("p t c -> p (t c)")
        sp_s = MI[:, 0:1728].rearrange("p (n c) -> p n c", n=6)
        negA = MI[:, 1728:1760]
        x0 = MI[:, 1760:2048]

        def step_sizes_act(act):
            act.activation(negA, vecs("a_log"), ACT.Exp).then_inc(act_own.sem, act_own.one())
            softplus_act(act, x0, sp_s)

        def step_sizes_dve(dve):
            dve.wait_ge(small_done.sem, small_done.at(1))
            bias = vecs("dt_bias").unsqueeze(1).broadcast_to((P, NT, 32))
            nc.vector.tensor_tensor(x0.rearrange("p (t c) -> p t c", t=NT),
                                    PS[:, 4, 0:288].rearrange("p (t c) -> p t c", t=NT), bias, ALU.add)\
              .then_inc(softplus_dve_part.sem, 1)
            softplus_dve(dve, x0, flat(DT), sp_s)

        conv_phase(S_XBC, 12,
                   XT[:, 2304:4616].rearrange("p (s t) -> p s t", s=2), XT[:, 4616:6924].rearrange("p (s t) -> p s t", s=2),
                   lambda b: cs[:, b % 2, :] if b < 8 else bcT[:, b - 8, :],
                   lambda b: xs[:, :, b * P:(b + 1) * P] if b < 8 else (btok[:, :, (b - 8) * P:(b - 7) * P] if b < 10 else None),
                   vecs("cw").rearrange("p (b j) -> p b j", j=3), vecs("cb"), 0, step_sizes_act, step_sizes_dve)

        GB = XT[:, 2304:6912].rearrange("p (t d g i) -> p t d g i", t=NT, d=2, g=2)
        ytok = HT[:, :].rearrange("p (t n) -> p t n", t=NT)

        with nc.Block() as block:
            @block.tensor
            def _(pe):
                for t in range(NT):
                    if t >= 3:
                        pe.wait_ge(cb_masked.sem, cb_masked.at(2 * (t - 2)))
                    for g in range(2):
                        mm = nc.tensor.matmul(PS[:, 1 + t % 3, g * P:(g + 1) * P], bcT[:, g, t * P:(t + 1) * P],
                                              bcT[:, 2 + g, t * P:(t + 1) * P], start=True, stop=True)
                    mm.then_inc(cb_done.sem, 1)
                pe.wait_ge(decay_ready.sem, decay_ready.at(1))
                for bank, (f, b) in enumerate((("le", "ge"), ("gt", "lt"), ("ones", "ones"))):
                    for d, m in enumerate((f, b)):
                        mm = nc.tensor.matmul(PS[:, 4 + bank, 0:288].rearrange("p (t c) -> p t c", t=NT)[:, :, 16 * d:16 * d + 16],
                                              const(m), DTA[:, :, 16 * d:16 * d + 16], start=True, stop=True)
                mm.then_inc(decay_summed.sem, 1)

            @block.scalar
            def _(act):
                act.wait_ge(decay_summed.sem, decay_summed.at(1))
                for bank, dst in enumerate((ECUM, WEND, TOT)):
                    act.activation(flat(dst), PS[:, 4 + bank, 0:288], ACT.Exp).then_inc(decays_ready.sem, 1)

            @block.vector
            def _(dve):
                nc.vector.scalar_tensor_tensor(out=DTA, in0=DT, scalar=-1.0,
                                               in1=negA.unsqueeze(1).broadcast_to((P, NT, 32)),
                                               op0=ALU.mult, op1=ALU.mult).then_inc(decay_ready.sem, 1)
                for t in range(NT):
                    dve.wait_ge(cb_done.sem, cb_done.at(t + 1))
                    for d, m in enumerate(("le", "ge")):
                        nc.vector.tensor_tensor(GB[:, t, d, :, :], PS[:, 1 + t % 3, 0:256].rearrange("p (g i) -> p g i", g=2),
                                                const(m).unsqueeze(1).broadcast_to((P, 2, P)), ALU.mult).then_inc(cb_masked.sem, 1)
                for t in range(6, NT):
                    nc.vector.tensor_tensor(ytok[:, t, :].rearrange("p (h n) -> p h n", h=SH),
                                            xs[:, t, :].rearrange("p (h n) -> p h n", h=SH),
                                            vecs("ssd_d").unsqueeze(2).broadcast_to((P, SH, SP)), ALU.mult)
                dve.wait_ge(decays_ready.sem, decays_ready.at(3))
                nc.vector.tensor_tensor(flat(WEND), flat(WEND), flat(DT), ALU.mult)

            @block.gpsimd
            def _(pool):
                for t in range(6):
                    nc.gpsimd.tensor_tensor(ytok[:, t, :].rearrange("p (h n) -> p h n", h=SH),
                                            xs[:, t, :].rearrange("p (h n) -> p h n", h=SH),
                                            vecs("ssd_d").unsqueeze(2).broadcast_to((P, SH, SP)), ALU.mult)
        for e, n in ((decays_ready, 3), (decay_ready, 1), (decay_summed, 1), (cb_done, NT), (cb_masked, 2 * NT)):
            e.close(n)

        EW = WR[:, 0, :].rearrange("p (s h i) -> p s h i", s=2, h=SH)
        RW = WR[:, 1, :].rearrange("p (s h i) -> p s h i", s=2, h=SH)
        xdt = MI[:, 0:2048].rearrange("p (s h n) -> p s h n", s=2, h=SH)
        xw = MI[:, 2048:4096].rearrange("p (s h n) -> p s h n", s=2, h=SH)
        HS = XT[:, 6912:8960].rearrange("p (d n) -> p d n", d=2)
        steps = [(0, 0), (1, 0)] + [x for t in range(8) for x in ((0, 1 + t), (1, 8 - t))]
        NS = len(steps)

        with nc.Block() as block:
            @block.sync
            def _(sp):
                for d in range(2):
                    sp.wait_ge(step_taken.sem, step_taken.at(d + 1))
                    sp.dma_start(o_ssd[:, d, :], HS[:, d, :]).then_inc(state_out[d].sem, 16)
                for d in range(2):
                    sp.wait_ge(state_out[d].sem, 16)
                    sp.dma_start(HS[:, d, :], ssd0[:, d, :]).then_inc(state_in[d].sem, 16)

            @block.gpsimd
            def _(pool):
                for n, (d, t) in enumerate(steps):
                    hs = slice(16 * d, 16 * d + 16)
                    if n >= 2:
                        pool.wait_ge(decays_summed.sem, decays_summed.at(4 * (n - 1)))
                    nc.gpsimd.tensor_tensor(RW[:, n % 2, :, :], DTA[:, t, hs].unsqueeze(2).broadcast_to((P, SH, P)),
                                            const(("le", "ge")[d]).unsqueeze(1).broadcast_to((P, SH, P)), ALU.mult)\
                      .then_inc(masked_decay_ready.sem, 1)
                    if n >= 2:
                        pool.wait_ge(chunk_summed.sem, chunk_summed.at(n - 1))
                    x = xs[:, t, :].rearrange("p (h n) -> p h n", h=SH)
                    nc.gpsimd.tensor_tensor(xdt[:, n % 2, :, :], x,
                                                            DT[:, t, hs].unsqueeze(2).broadcast_to((P, SH, SP)), ALU.mult).then_inc(pool_own.sem, pool_own.one())
                    pool.wait_ge(pool_own.sem, pool_own.n)
                    nc.gpsimd.tensor_tensor(xw[:, n % 2, :, :], x, WEND[:, t, hs].unsqueeze(2).broadcast_to((P, SH, SP)),
                                            ALU.mult).then_inc(x_scaled.sem, 1)

            @block.tensor
            def _(pe):
                def decays(n):
                    pe.wait_ge(masked_decay_ready.sem, masked_decay_ready.at(n + 1))
                    for q in range(4):
                        j = 4 * n + q
                        if j >= 2:
                            pe.wait_ge(decays_taken.sem, decays_taken.at(j - 1))
                        nc.tensor.matmul(PS[:, q % 2, :], const(("gt", "lt")[steps[n][0]]),
                                         RW[:, n % 2, 4 * q:4 * q + 4, :], start=True, stop=True).then_inc(decays_summed.sem, 1)

                decays(0)
                for n, (d, t) in enumerate(steps):
                    if n + 1 < NS:
                        decays(n + 1)
                    if n >= 2:
                        if n < 4:
                            pe.wait_ge(state_in[d].sem, 16)
                        pe.wait_ge(step_taken.sem, step_taken.at(n - 1))
                        if n >= 3:
                            pe.wait_ge(step_taken.sem, step_taken.at(n))
                        for g in range(2):
                            mm = nc.tensor.matmul(PS[:, 3 + g, :], bcT[:, 2 + g, t * P:(t + 1) * P],
                                                  HS[:, d, 512 * g:512 * g + 512], start=True, stop=True)
                        mm.then_inc(state_read.sem, 1)
                    pe.wait_ge(x_scaled.sem, x_scaled.at(n + 1))
                    if n >= 1:
                        pe.wait_ge(step_taken.sem, step_taken.at(n))
                    for g, bank in enumerate((2, 7)):
                        mm = nc.tensor.matmul(PS[:, bank, :], btok[:, t, g * P:(g + 1) * P],
                                              xw[:, n % 2, 8 * g:8 * g + 8, :], start=True, stop=True)
                    mm.then_inc(update_summed.sem, 1)
                    pe.wait_ge(weights_ready.sem, weights_ready.at(n + 1))
                    for h in range(SH):
                        mm = nc.tensor.matmul(PS[:, 5 + h // 8, (h % 8) * SP:(h % 8 + 1) * SP], EW[:, n % 2, h, :],
                                              xdt[:, n % 2, h, :], start=True, stop=True)
                    mm.then_inc(chunk_summed.sem, 1)

            @block.scalar
            def _(act):
                for n in range(NS):
                    if n >= 2:
                        act.wait_ge(chunk_summed.sem, chunk_summed.at(n - 1))
                    for q in range(4):
                        act.wait_ge(decays_summed.sem, decays_summed.at(4 * n + q + 1))
                        act.activation(EW[:, n % 2, 4 * q:4 * q + 4, :], PS[:, q % 2, :].rearrange("p (h i) -> p h i", h=4),
                                       ACT.Exp).then_inc(decays_taken.sem, 1)

            @block.vector
            def _(dve):
                def weights(n):
                    d, t = steps[n]
                    dve.wait_ge(decays_taken.sem, decays_taken.at(4 * n + 4))
                    for g in range(2):
                        e = EW[:, n % 2, 8 * g:8 * g + 8, :]
                        ins = nc.vector.tensor_tensor(e, e, GB[:, t, d, g, :].unsqueeze(1).broadcast_to((P, 8, P)), ALU.mult)
                        if g == 0:
                            ins.then_inc(dve_own.sem, dve_own.one())
                    ins.then_inc(weights_ready.sem, 1)

                weights(0)
                for n, (d, t) in enumerate(steps):
                    if n + 1 < NS:
                        weights(n + 1)
                    hs = slice(16 * d, 16 * d + 16)
                    y = ytok[:, t, :]
                    ci = PS[:, 3:5, :].rearrange("p b (h n) -> p (b h) n", h=8)
                    if n >= 2:
                        dve.wait_ge(state_read.sem, state_read.at(n - 1))
                        dve.wait_ge(dve_own.sem, dve_own.n)
                        nc.vector.tensor_tensor(ci, ci, ECUM[:, t, hs].unsqueeze(2).broadcast_to((P, SH, SP)),
                                                               ALU.mult).then_inc(dve_own.sem, dve_own.one())
                        dve.wait_ge(dve_own.sem, dve_own.n)
                        nc.vector.tensor_tensor(y, y, PS[:, 3:5, :].rearrange("p b n -> p (b n)"), ALU.add).then_inc(dve_own.sem, dve_own.one())
                        h = HS[:, d, :].rearrange("p (h n) -> p h n", h=SH)
                        if n < 4:
                            dve.wait_ge(state_in[d].sem, 16)
                        dve.wait_ge(update_summed.sem, update_summed.at(n + 1))
                        nc.vector.tensor_tensor(h, h, TOT[:, t, hs].unsqueeze(2).broadcast_to((P, SH, SP)),
                                                               ALU.mult).then_inc(dve_own.sem, dve_own.one())
                        dve.wait_ge(dve_own.sem, dve_own.n)
                        for g, bank in enumerate((2, 7)):
                            s = HS[:, d, 512 * g:512 * g + 512]
                            nc.vector.tensor_tensor(s, s, PS[:, bank, :], ALU.add).then_inc(dve_own.sem, dve_own.one())
                        dve.wait_ge(chunk_summed.sem, chunk_summed.at(n + 1))
                        dve.wait_ge(dve_own.sem, dve_own.n)
                        nc.vector.tensor_tensor(y, y, PS[:, 5:7, :].rearrange("p b n -> p (b n)"), ALU.add)\
                          .then_inc(step_taken.sem, 1)
                    else:
                        dve.wait_ge(update_summed.sem, update_summed.at(n + 1))
                        for g, bank in enumerate((2, 7)):
                            nc.vector.tensor_copy(HS[:, d, 512 * g:512 * g + 512], PS[:, bank, :]).then_inc(dve_own.sem, dve_own.one())
                        dve.wait_ge(chunk_summed.sem, chunk_summed.at(n + 1))
                        dve.wait_ge(dve_own.sem, dve_own.n)
                        nc.vector.tensor_tensor(y, y, PS[:, 5:7, :].rearrange("p b n -> p (b n)"), ALU.add).then_inc(dve_own.sem, dve_own.one())
                        dve.wait_ge(dve_own.sem, dve_own.n)
                        dve.sem_inc(step_taken.sem, 1)
        for e, n in ((masked_decay_ready, NS), (decays_summed, 4 * NS), (decays_taken, 4 * NS), (x_scaled, NS), (state_read, NS - 2), (weights_ready, NS), (chunk_summed, NS),
                     (step_taken, NS), (update_summed, NS)):
            e.close(n)

        def gate(l, next_slot):
            zt = [F1[:, 1024 * n:1024 * n + 1024] for n in range(4)] + [MI[:, 0:1024], MI[:, 1024:2048]]
            yb = [F1[:, 4096 + 1024 * n:5120 + 1024 * n] for n in range(5)]
            sq = MI[:, 2048:3072]
            ss = MI[:, 3072:3072 + 4 * NT].rearrange("p (n t) -> p n t", n=4)
            normed = l == 0
            with nc.Block() as block:
                @block.sync
                def _(sp):
                    for t in range(NT):
                        if t >= 6:
                            sp.wait_ge(gated.sem, gated.at(t - 5))
                        sp.dma_start(zt[t % 6], z_spill[t, :, :]).then_inc(gate_loaded[t % 6].sem, 16)
                        if not normed:
                            if t >= 5:
                                sp.wait_ge(y_summed.sem, y_summed.at(t - 4))
                            sp.dma_start(ytok[:, t, :], y_spill[0, t, :, :]).then_inc(y_back[t % 5].sem, 16)
                            sp.dma_start(yb[t % 5], y_spill[1, t, :, :]).then_inc(y_back[t % 5].sem, 16)
                    feed(sp, next_slot + 2)
                    sp.dma_start(XT[:, 0:9216], x_spill).then_inc(xback.sem, 16)

                @block.vector
                def _(dve):
                    for t in range(NT):
                        y = ytok[:, t, :]
                        if not normed:
                            dve.wait_ge(y_back[t % 5].sem, y_back[t % 5].at(32 * (t // 5 + 1)))
                            nc.vector.tensor_tensor(y, y, yb[t % 5], ALU.add).then_inc(y_summed.sem, 1)
                            dve.wait_ge(y_summed.sem, y_summed.at(t + 1))
                        dve.wait_ge(gate_act.sem, gate_act.at(t + 1))
                        nc.vector.tensor_tensor(y, y, zt[t % 6], ALU.mult).then_inc(gated.sem, 1)
                    if normed:
                        dve.wait_ge(square_sum_ready.sem, square_sum_ready.at(NT))
                        nc.vector.tensor_scalar(ss[:, 1, :], ss[:, 0, :], 1.0 / D, EPS, ALU.mult, ALU.add)\
                          .then_inc(dve_own.sem, dve_own.one())
                        dve.wait_ge(dve_own.sem, dve_own.n)
                        nc.vector.reciprocal(ss[:, 2, :], ss[:, 1, :]).then_inc(gate_mean_ready.sem, 1)
                        gain = vecs("ssd_norm")
                        for j in range(2 * NT):
                            t, g = j // 2, j % 2
                            dve.wait_ge(mix_turned.sem, mix_turned.at(j + 1))
                            nc.vector.tensor_tensor(f0k[:, 4 * g:4 * g + 4, t * P:(t + 1) * P],
                                                    PS[:, j % 4, :].rearrange("p (b i) -> p b i", b=4),
                                                    gain[:, 4 * g:4 * g + 4].unsqueeze(2).broadcast_to((P, 4, P)),
                                                    ALU.mult).then_inc(mix_taken.sem, 1)

                ready = gate_scaled if normed else gated

                @block.tensor
                def _(pe):
                    for t in range(NT):
                        pe.wait_ge(ready.sem, ready.at(t + 1))
                        for g in range(2):
                            j = 2 * t + g
                            if j >= 4:
                                pe.wait_ge(mix_taken.sem, mix_taken.at(j - 3))
                            for b in range(4):
                                mm = nc.tensor.transpose(PS[:, j % 4, b * P:(b + 1) * P],
                                                         ytok[:, t, (4 * g + b) * P:(4 * g + b + 1) * P], ident)
                            mm.then_inc(mix_turned.sem, 1)

                @block.scalar
                def _(act):
                    for t in range(NT + 1):
                        if t < NT:
                            act.wait_ge(gate_loaded[t % 6].sem, gate_loaded[t % 6].at(16 * (t // 6 + 1)))
                            act.activation(zt[t % 6], zt[t % 6], ACT.Silu if normed else ACT.Sigmoid)\
                               .then_inc(gate_act.sem, 1)
                        if normed and t >= 1:
                            act.wait_ge(gated.sem, gated.at(t))
                            if t >= 2:
                                act.wait_ge(square_sum_ready.sem, square_sum_ready.at(t - 1))
                            act.activation(sq, ytok[:, t - 1, :], ACT.Square, accum_out=ss[:, 0, t - 1:t])\
                               .then_inc(square_sum_ready.sem, 1)
                        if not normed and t >= 1:
                            for j in (2 * t - 2, 2 * t - 1):
                                act.wait_ge(mix_turned.sem, mix_turned.at(j + 1))
                                act.activation(f0k[:, 4 * (j % 2):4 * (j % 2) + 4, (t - 1) * P:t * P],
                                               PS[:, j % 4, :].rearrange("p (b i) -> p b i", b=4), ACT.Copy)\
                                   .then_inc(mix_taken.sem, 1)
                    if normed:
                        act.wait_ge(gate_mean_ready.sem, gate_mean_ready.at(1))
                        act.activation(ss[:, 3, :], ss[:, 2, :], ACT.Sqrt).then_inc(gate_rms_ready.sem, 1)
                        act.wait_ge(gate_rms_ready.sem, gate_rms_ready.at(1))
                        for t in range(NT):
                            act.activation(ytok[:, t, :], ytok[:, t, :], ACT.Copy, scale=ss[:, 3, t:t + 1])\
                               .then_inc(gate_scaled.sem, 1)
            for n in range(6):
                gate_loaded[n].close(16 * len(range(n, NT, 6)))
            gate_act.close(NT)
            if not normed:
                y_summed.close(NT)
            gated.close(NT)
            if normed:
                for e in (square_sum_ready, gate_scaled):
                    e.close(NT)
                gate_mean_ready.close(1)
                gate_rms_ready.close(1)
            mix_turned.close(2 * NT)
            mix_taken.close(2 * NT)

        def add_gated(dve, l, gate_at, b, c, bank, last):
            for a, e, cond, tc in SEGS:
                if tc != c:
                    continue
                x = xk[:, b, a:e]
                ins = nc.vector.scalar_tensor_tensor(out=x, in0=PS[:, bank, a - c * TC:e - c * TC],
                                                     scalar=MOD[:, l, gate_at + b, cond:cond + 1], in1=x,
                                                     op0=ALU.mult, op1=ALU.add)
                if e != (c + 1) * TC:
                    ins.then_inc(dve_own.sem, dve_own.one())
            last(ins)

        def out_projection(l, s0, nslots, blocks):
            per = KD // nslots
            kk = len(blocks)
            places = [WR[:, 0, :], WR[:, 1, :], MI[:, :], F1[:, 0:4096]]
            SQ = HT[:, 0:16 * TC].rearrange("p (n t) -> p n t", n=16)
            added = HT[:, 16 * TC:18 * TC].rearrange("p (c t) -> p c t", c=2)
            RB = SM[:, 0:T]
            for s in range(2):
                free_at[s0 + s] = (tile_done.sem, tile_done.at(KD * NC))
            with nc.Block() as block:
                @block.sync
                def _(sp):
                    for s in range(2, nslots):
                        sp.dma_start(places[s][:, 0:kk * per * P], wslots[S_MORE + s - 2, :, 0:kk * per * P])\
                          .then_inc(more_ready[s - 2].sem, 16)

                @block.tensor
                def _(pe):
                    for i in range(NC * KD):
                        c, b = i // KD, i % KD
                        s = b // per
                        if c == 0 and b % per == 0:
                            if s < 2:
                                pe.wait_ge(*landed(s0 + s))
                            else:
                                pe.wait_ge(more_ready[s - 2].sem, 16)
                        w = places[s][:, 0:kk * per * P].rearrange("p (k n) -> p k n", k=kk)
                        tile_products(pe, i, P, TC, [(w[:, k, (b % per) * P:(b % per + 1) * P],
                                                      blocks[k][:, c * TC:(c + 1) * TC]) for k in range(kk)], banks=6)
                        if c >= 1 and b == 2:
                            pe.wait_ge(squares_added.sem, squares_added.at(c))
                            nc.tensor.matmul(PS[:, 5 + c, 0:TC], ones, added[:, c - 1, :], start=True, stop=True)\
                              .then_inc(squares_summed.sem, KD)

                @block.scalar
                def _(act):
                    for c in range(2):
                        act.wait_ge(tile_free.sem, tile_free.at(KD * (c + 1)))
                        norm_squares(act, c, SQ, 2 * KD)
                        norm_root(act, c, RB)

                @block.gpsimd
                def _(pool):
                    for i in range(2 * KD):
                        c, k = i // KD, i % KD
                        pool.wait_ge(squares_ready.sem, squares_ready.at(i + 1))
                        if k >= 2:
                            pool.wait_ge(pool_own.sem, pool_own.n)
                        if k >= 1:
                            ins = nc.gpsimd.tensor_tensor(added[:, c, :], SQ[:, i, :], SQ[:, i - 1, :] if k == 1 else added[:, c, :],
                                                          ALU.add)
                            if k < KD - 1:
                                ins.then_inc(pool_own.sem, pool_own.one())
                            else:
                                ins.then_inc(squares_added.sem, 1)

                @block.vector
                def _(dve):
                    dve.wait_ge(xback.sem, xback.at(16))
                    for i in range(NC * KD):
                        c, b = i // KD, i % KD
                        dve.wait_ge(tile_done.sem, tile_done.at(i + 1))
                        add_gated(dve, l, 16, b, c, i % 6, lambda ins: ins.then_inc(tile_free.sem, 1))
                        if c >= 1 and b == 4:
                            norm_mean(dve, c - 1, RB, 5 + c)
            close_tiles(KD * NC)
            xback.close(16)
            squares_added.close(2)

        raw_unit = None

        def mlp(l):
            nonlocal raw_unit
            mem = ExitStack()

            def f32(name, shape):
                return mem.enter_context(nc.sbuf_tensor(f"{name}_{l}", shape, F32))

            def f32r(name, shape):
                return mem.enter_context(nc.sbuf_tensor(f"{name}_{l}", shape, F32R))

            HH, HL = f32r("h_high", [P, KD, T]), f32r("h_low", [P, KD, T])
            raw_unit = f32("raw_unit", [P, 2, 1024])
            with nc.sbuf_tensor(f"squares_{l}", [P, 8, TC], F32) as SQ, nc.sbuf_tensor(f"split_{l}", [P, 8, TC], F32) as tmp:
                norm(l, 1, None, SQ, SM[:, 0:T], 0, split=(tmp, HH, HL), done=2)
            WH, WL = f32r("w_high", [P, 4, 1024]), f32r("w_low", [P, 4, 1024])
            AH, AL = f32r("a_high", [P, 2, 2, T]), f32r("a_low", [P, 2, 2, T])
            rt, sq = f32("relu", [P, 2, TC]), f32("square", [P, 2, TC])
            NP = NG - 2

            def at(c, per_step, g, i, n):
                return i * (2 * per_step) + c.at(per_step * g + n)

            with nc.Block() as block:
                @block.sync
                def _(sp):
                    with sp.Fori(0, 31) as i:
                        for s in range(2):
                            sp.wait_ge(unit_split.sem, at(unit_split, 1, 0, i, s + 1))
                            sp.dma_start(raw_unit[:, s, :],
                                         wff[l, bass.ds(i * 2 + (2 + s), 1), :, :].rearrange("a p n -> p (a n)"))\
                              .then_inc(unit_loaded[s].sem, 16)

                @block.tensor
                def _(pe):
                    def passes(out, w, ks, rhs, cols):
                        n = 0
                        for k in ks:
                            for wt, at_ in ((WH, 0), (WH, 1), (WL, 0)):
                                mm = nc.tensor.matmul(out, wt[:, w(k), cols(k)], rhs[at_](k), start=(n == 0),
                                                      stop=(n == 3 * len(ks) - 1))
                                n += 1
                        return mm

                    def up(g, i, first=False):
                        for j in range(6):
                            m, c = j // NC, j % NC
                            if j % NC == 0:
                                n = (g == 0) * m + (g > 0) * (m - 2)
                                pe.wait_ge(unit_split.sem, at(unit_split, 4, g, i, n + 1))
                            if not (first and j < 3):
                                pe.wait_ge(up_taken.sem, at(up_taken, 6, g, i, j - 2))
                            t = slice(c * TC, (c + 1) * TC)
                            passes(PS[:, j % 3, 0:TC], lambda k: m, range(KD),
                                   (lambda k: HH[:, k, t], lambda k: HL[:, k, t]),
                                   lambda k: slice(k * P, (k + 1) * P)).then_inc(up_done.sem, 1)

                    def down(g, i, unit, first=False):
                        pe.wait_ge(unit_split.sem, at(unit_split, 4, g, i, unit))
                        pe.wait_ge(hidden_split.sem, at(hidden_split, 6, g, i, 6))
                        for j in range(24):
                            b, c = j // NC, j % NC
                            if not (first and j < 4):
                                pe.wait_ge(down_taken.sem, at(down_taken, 24, g, i, j - 3))
                            t = slice(c * TC, (c + 1) * TC)
                            passes(PS[:, 3 + j % 4, 0:TC], lambda k: 2 + k, range(2),
                                   (lambda k: AH[:, g % 2, k, t], lambda k: AL[:, g % 2, k, t]),
                                   lambda k: slice(b * P, (b + 1) * P)).then_inc(down_done.sem, 1)

                    up(0, 0, first=True)
                    up(1, 0)
                    down(0, 0, 6, first=True)
                    up(2, 0)
                    down(1, 0, 6)
                    with pe.Fori(0, NP // 2 - 1) as i:
                        up(3, i)
                        down(2, i, 6)
                        up(4, i)
                        down(3, i, 6)
                    up(NG - 1, 0)
                    down(NG - 2, 0, 6)
                    down(NG - 1, 0, 4)

                def unit_places(kind):
                    return (0, 1) if kind == "W1" else (2, 3)

                @block.scalar
                def _(act):
                    def unit(n, g, i, place, used):
                        act.wait_ge(unit_loaded[n % 2].sem, i * 64 + unit_loaded[n % 2].at(16 * ((4 * g + n) // 2 + 1)))
                        if used:
                            act.wait_ge(*used)
                        act.activation(WH[:, place, :], raw_unit[:, n % 2, :], ACT.Copy).then_inc(unit_hi.sem, 1)

                    def tile(g, i, j, first=False):
                        act.wait_ge(up_done.sem, at(up_done, 6, g, i, j + 1))
                        if not (first and j < 2):
                            act.wait_ge(squared.sem, at(squared, 6, g, i, j - 1))
                        act.activation(rt[:, j % 2, :], PS[:, j % 3, 0:TC], ACT.Relu).then_inc(up_taken.sem, 1)

                    def tile_high(g, i, j):
                        act.wait_ge(squared.sem, at(squared, 6, g, i, j + 1))
                        m, c = j // NC, j % NC
                        act.activation(AH[:, g % 2, m, c * TC:(c + 1) * TC], sq[:, j % 2, :], ACT.Copy)\
                           .then_inc(hidden_hi.sem, 1)

                    def step(g, i, w2=True, w1=True):
                        if w2:
                            for s in range(2):
                                unit(s, g, i, 2 + s, (down_done.sem, at(down_done, 24, g - 1, i, 0)))
                        for j in range(6):
                            tile(g, i, j, first=(g == 0))
                            if j >= 1:
                                tile_high(g, i, j - 1)
                            if w1 and j == 3:
                                unit(2, g, i, 0, (up_done.sem, at(up_done, 6, g, i, 3)))
                        tile_high(g, i, 5)
                        if w1:
                            unit(3, g, i, 1, (up_done.sem, at(up_done, 6, g, i, 6)))

                    unit(0, 0, 0, 0, None)
                    unit(1, 0, 0, 1, None)
                    step(0, 0, w2=False)
                    step(1, 0)
                    step(2, 0)
                    with act.Fori(0, NP // 2 - 1) as i:
                        step(3, i)
                        step(4, i)
                    step(NG - 1, 0, w1=False)
                    for s in range(2):
                        unit(2 + s, NG - 1, 0, 2 + s, (down_done.sem, at(down_done, 24, NG - 1, 0, 0)))

                @block.gpsimd
                def _(pool):
                    def step(g, i):
                        for j in range(6):
                            pool.wait_ge(up_taken.sem, at(up_taken, 6, g, i, j + 1))
                            if not (g == 0 and j < 2):
                                pool.wait_ge(hidden_split.sem, at(hidden_split, 6, g, i, j - 1))
                            nc.gpsimd.tensor_tensor(sq[:, j % 2, :], rt[:, j % 2, :], rt[:, j % 2, :], ALU.mult)\
                              .then_inc(squared.sem, 1)
                    step(0, 0)
                    step(1, 0)
                    step(2, 0)
                    with pool.Fori(0, NP // 2 - 1) as i:
                        step(3, i)
                        step(4, i)
                    step(NG - 1, 0)

                @block.vector
                def _(dve):
                    def unit(n, g, i, place):
                        dve.wait_ge(unit_hi.sem, at(unit_hi, 4, g, i, n + 1))
                        nc.vector.tensor_tensor(WL[:, place, :], raw_unit[:, n % 2, :], WH[:, place, :].bitcast(F32),
                                                ALU.subtract).then_inc(unit_split.sem, 1)

                    def tile(g, i, j):
                        dve.wait_ge(hidden_hi.sem, at(hidden_hi, 6, g, i, j + 1))
                        m, t = j // NC, slice(j % NC * TC, (j % NC + 1) * TC)
                        nc.vector.tensor_tensor(AL[:, g % 2, m, t], sq[:, j % 2, :], AH[:, g % 2, m, t].bitcast(F32),
                                                ALU.subtract).then_inc(hidden_split.sem, 1)

                    def sums(g, i, between=None):
                        for j in range(24):
                            b, c = j // NC, j % NC
                            dve.wait_ge(down_done.sem, at(down_done, 24, g, i, j + 1))
                            if j == 0:
                                dve.wait_ge(down_taken.sem, at(down_taken, 24, g, i, 0))
                            for a, e, cond, tc in SEGS:
                                if tc == c:
                                    x = xk[:, b, a:e]
                                    ins = nc.vector.scalar_tensor_tensor(
                                        out=x, in0=PS[:, 3 + j % 4, a - c * TC:e - c * TC],
                                        scalar=MOD[:, l, 40 + b, cond:cond + 1], in1=x, op0=ALU.mult, op1=ALU.add)
                            ins.then_inc(down_taken.sem, 1)
                            if j == 3 and between:
                                between()

                    def step(g, i, w2=True, w1=True, down=True):
                        if w2:
                            unit(0, g, i, 2)
                            unit(1, g, i, 3)
                        for j in range(6):
                            tile(g, i, j)
                            if w1 and j == 2:
                                unit(2, g, i, 0)
                        if down:
                            sums(g - 1, i, (lambda: unit(3, g, i, 1)) if w1 else None)
                        else:
                            unit(3, g, i, 1)

                    unit(0, 0, 0, 0)
                    unit(1, 0, 0, 1)
                    step(0, 0, w2=False, down=False)
                    step(1, 0)
                    step(2, 0)
                    with dve.Fori(0, NP // 2 - 1) as i:
                        step(3, i)
                        step(4, i)
                    step(NG - 1, 0, w1=False)
                    unit(2, NG - 1, 0, 2)
                    unit(3, NG - 1, 0, 3)
                    sums(NG - 1, 0)
            for c, n in ((unit_hi, 64), (unit_split, 64), (unit_loaded[0], 512), (unit_loaded[1], 512),
                         (up_done, 96), (up_taken, 96), (down_done, 384), (down_taken, 384), (squared, 96),
                         (hidden_hi, 96), (hidden_split, 96)):
                c.close(n)
            mem.close()

        gate(0, S_OUTE)
        out_projection(0, S_OUTE, 4, [ynaT[:, b, :] for b in range(4)] + [f0k[:, b, :] for b in range(8)])
        mixer.close()
        mlp(0)
        mixer = ExitStack()
        HT = mixer_tensor("HT1", [P, 9216])
        F0 = mixer_tensor("F01", [P, 9216])
        F1 = mixer_tensor("F11", [P, 9216])
        WR = mixer_tensor("WR1", [P, 2, 4096])
        MI = mixer_tensor("MI1", [P, 4096])
        hk = HT[:, :].rearrange("p (k t) -> p k t", k=KD)
        f0k = F0[:, :].rearrange("p (k t) -> p k t", k=8)
        qT = F0[:, 0:4608].rearrange("p (b t) -> p b t", b=4)
        kT = F0[:, 4608:9216].rearrange("p (b t) -> p b t", b=4)
        ytok = HT[:, :].rearrange("p (t n) -> p t n", t=NT)
        zst = MI[:, 0:2048].rearrange("p (s n) -> p s n", s=4)
        norm_mixer(1, S_QK + 2)

        ktok = F1[:, 0:4608].rearrange("p (t n) -> p t n", t=NT)
        x1 = SM[:, 0:288]
        lf = SM[:, 288:432].rearrange("p (t c) -> p t c", t=NT)
        xf = SM[:, 432:576].rearrange("p (t c) -> p t c", t=NT)
        g_s = SM[:, 576:1440].rearrange("p (n c) -> p n c", n=6)
        raw_gates = x1.rearrange("p (t n c) -> p t n c", t=NT, n=2)

        def forget_gates_act(act):
            softplus_act(act, xf.rearrange("p t c -> p (t c)"), g_s)

        def forget_gates_dve(dve):
            dve.wait_ge(small_done.sem, small_done.at(1))
            nc.vector.tensor_tensor(x1.rearrange("p (t c) -> p t c", t=NT),
                                    PS[:, 4, 0:288].rearrange("p (t c) -> p t c", t=NT),
                                    vecs("gate_b").unsqueeze(1).broadcast_to((P, NT, 32)), ALU.add)\
              .then_inc(dve_own.sem, dve_own.one())
            dve.wait_ge(dve_own.sem, dve_own.n)
            nc.vector.tensor_scalar(xf, raw_gates[:, :, 1, :], -1.0, None, ALU.mult).then_inc(softplus_dve_part.sem, 1)
            softplus_dve(dve, xf.rearrange("p t c -> p (t c)"), lf.rearrange("p t c -> p (t c)"), g_s)

        conv_phase(S_QK, 8,
                   F1[:, 4608:6920].rearrange("p (s t) -> p s t", s=2), MI[:, 0:2308].rearrange("p (s t) -> p s t", s=2),
                   lambda b: (qT[:, b, :] if b < 4 else kT[:, b - 4, :]),
                   lambda b: ktok[:, :, (b - 4) * P:(b - 3) * P] if b >= 4 else None,
                   vecs("mw").rearrange("p (b j) -> p b j", j=3), vecs("mb"), 1, forget_gates_act, forget_gates_dve)
        spilled.close(16)

        v1 = XT[:, :].rearrange("p (t h e) -> p t h e", t=NT, h=MH)
        R40 = slice(0, ROWS)
        CU = B = F1[R40, 4608:4608 + T]
        LI = A = F1[R40, 5760:5760 + T]
        LF = WI = F1[R40, 6912:6912 + T]
        M = EN = F1[R40, 8064:8064 + T]
        WK = MI[R40, 0:T]
        CST = F1[:, 5760:6792].rearrange("p (d b e) -> p d b e", d=2, b=4)
        WCB = F1[:, 6792:6864].rearrange("p (d b t) -> p d b t", d=2, b=4)
        TA = SM[:, 0:1440].rearrange("p (t n r) -> p t n r", t=NT, n=4)
        RST = MI[R40, 2600:3752]
        HALF = MI[R40, 3752:3880]
        PAIR = MI[R40, 3880:3888]
        tokG = MI[:, 1152:1872].rearrange("p (n t r) -> p n t r", n=2, t=NT)
        MP, ML, CL, WC, DL = (MI[R40, 2400 + 9 * n:2409 + 9 * n] for n in range(5))
        WX = MI[R40, 2448:2520].rearrange("p (n t) -> p n t", n=8)
        frees(range(S_VO, S_VO + 2), (9, 9))
        for s in range(2):
            free_at[S_VO + 2 + s] = (o_done.sem, o_done.at(NT * (s + 1)))

        def seq3(a):
            return a.rearrange("p (t i) -> p t i", t=NT)

        with nc.Block() as block:
            @block.sync
            def _(sp):
                sp.dma_start(MI[R40, 2600:3888], consts[R40, NCONST:NCONST + 1288]).then_inc(loaded.sem, 16)
                sp.wait_ge(logs_ready.sem, logs_ready.at(1))
                sp.dma_start(o_m, ML).then_inc(stored.sem, 16)
                sp.wait_ge(stored.sem, stored.at(16))
                feed(sp, S_VO + 4)

            @block.tensor
            def _(pe):
                for i in range(2 * NT):
                    if i % NT == 0:
                        pe.wait_ge(*landed(S_VO + i // NT))
                    token_tile(pe, i, slot_k(S_VO + i // NT), i % NT, banks=2)
                    if i == 1:
                        pe.wait_ge(gates_ready.sem, gates_ready.at(1))
                        for n in range(2):
                            for t in range(NT):
                                mm = nc.tensor.transpose(PS[R40, 2 + 3 * n + t // 4, (t % 4) * P:(t % 4 + 1) * P],
                                                         tokG[:, n, t, :], ident)
                        mm.then_inc(rows_turned.sem, 1)
                    if i == 9:
                        pe.wait_ge(rows_ready.sem, rows_ready.at(1))
                        for t in range(NT):
                            for n, r in enumerate((A, WI, EN, WK)):
                                nc.tensor.transpose(PS[:, 2 + t // 3, ((t % 3) * 4 + n) * ROWS:((t % 3) * 4 + n + 1) * ROWS],
                                                    r[:, t * P:(t + 1) * P], ident[R40, R40])
                        nc.tensor.matmul(PS[:, 5, 0:72], HALF, WX.rearrange("p n t -> p (n t)"), start=True, stop=True)\
                          .then_inc(rows_back.sem, 1)

            @block.gpsimd
            def _(pool):
                nc.gpsimd.memset(v1[:, :, :, MV:V1], 1.0)

            @block.scalar
            def _(act):
                for i in range(2 * NT):
                    s, t = i // NT, i % NT
                    act.wait_ge(tile_done.sem, tile_done.at(i + 1))
                    act.activation(v1[:, t, 4 * s:4 * s + 4, 0:MV], PS[:, i % 2, :].rearrange("p (h e) -> p h e", h=4),
                                   ACT.Copy).then_inc(tile_free.sem, 1)
                    if i == 6:
                        act.wait_ge(logs_ready.sem, logs_ready.at(1))
                        act.activation(WI, WI, ACT.Exp).then_inc(act_own.sem, act_own.one())
                        act.activation(WK, WK, ACT.Exp).then_inc(act_own.sem, act_own.one())
                        act.activation(EN, M, ACT.Exp, scale=-1.0).then_inc(act_own.sem, act_own.one())
                        act.activation(WC, WC, ACT.Exp).then_inc(act_own.sem, act_own.one())
                        act.wait_ge(act_own.sem, act_own.n)
                        act.sem_inc(exps_ready.sem, 1)

            @block.vector
            def _(dve):
                def chained(ins):
                    ins.then_inc(dve_own.sem, dve_own.one())
                    dve.wait_ge(dve_own.sem, dve_own.n)
                chained(nc.vector.memset(tokG, 0.0))
                for d in range(2):
                    nc.vector.tensor_copy(tokG[:, 0, :, 32 * d:32 * d + 8], raw_gates[:, :, 0, 8 * d:8 * d + 8])\
                      .then_inc(dve_own.sem, dve_own.one())
                    nc.vector.tensor_scalar(tokG[:, 1, :, 32 * d:32 * d + 8], lf[:, :, 8 * d:8 * d + 8], -1.0, None, ALU.mult)\
                      .then_inc(dve_own.sem, dve_own.one())
                dve.wait_ge(dve_own.sem, dve_own.n)
                dve.sem_inc(gates_ready.sem, 1)
                nc.vector.memset(M, 0.0).then_inc(dve_own.sem, dve_own.one())
                nc.vector.memset(CU, 0.0).then_inc(dve_own.sem, dve_own.one())
                nc.vector.memset(MP, 0.0).then_inc(dve_own.sem, dve_own.one())
                dve.wait_ge(rows_turned.sem, rows_turned.at(1))
                for n, dst in enumerate((LI, LF)):
                    nc.vector.tensor_copy(dst[:, 0:1024].rearrange("p (b t) -> p b t", b=2), PS[R40, 3 * n + 2:3 * n + 4, :])\
                      .then_inc(dve_own.sem, dve_own.one())
                    nc.vector.tensor_copy(dst[:, 1024:T], PS[R40, 3 * n + 4, 0:P]).then_inc(dve_own.sem, dve_own.one())
                dve.wait_ge(dve_own.sem, dve_own.n)
                dve.wait_ge(loaded.sem, loaded.at(16))
                for d in range(2):
                    r = slice(32 * d, 32 * d + 8)
                    way = slice(None, None, 1 if d == 0 else -1)
                    for a, b, m0 in ((0, CTX, 0.0), (CTX, T, vecs("m0")[r, :])):
                        nc.vector.tensor_tensor_scan(M[r, a:b][:, way], LF[r, a:b][:, way], LI[r, a:b][:, way],
                                                     m0, op0=ALU.add, op1=ALU.max).then_inc(dve_own.sem, dve_own.one())
                    nc.vector.tensor_tensor_scan(CU[r, :][:, way], RST[r, :][:, way], LF[r, :][:, way], 0.0,
                                                 op0=ALU.mult, op1=ALU.add).then_inc(dve_own.sem, dve_own.one())
                dve.wait_ge(dve_own.sem, dve_own.n)
                m3, c3 = seq3(M), seq3(CU)
                nc.vector.tensor_copy(MP[0:8, 1:2], vecs("m0")[0:8, :]).then_inc(dve_own.sem, dve_own.one())
                nc.vector.tensor_copy(MP[0:8, 2:9], m3[0:8, 1:8, P - 1]).then_inc(dve_own.sem, dve_own.one())
                nc.vector.tensor_copy(MP[32:40, 8:9], vecs("m0")[32:40, :]).then_inc(dve_own.sem, dve_own.one())
                nc.vector.tensor_copy(MP[32:40, 1:8], m3[32:40, 2:9, 0]).then_inc(dve_own.sem, dve_own.one())
                for dst, src in ((ML, m3), (CL, c3)):
                    nc.vector.tensor_copy(dst[0:32, :], src[0:32, :, P - 1]).then_inc(dve_own.sem, dve_own.one())
                    nc.vector.tensor_copy(dst[32:40, :], src[32:40, :, 0]).then_inc(dve_own.sem, dve_own.one())
                chained(nc.vector.tensor_tensor(A, LI, CU, ALU.subtract))
                chained(nc.vector.tensor_tensor(B, CU, M, ALU.subtract))
                chained(nc.vector.tensor_tensor(DL, CL, ML, ALU.subtract))
                nc.vector.tensor_tensor(WC, DL, MP, ALU.add).then_inc(dve_own.sem, dve_own.one())
                nc.vector.tensor_tensor(seq3(WI), seq3(B), MP.unsqueeze(2).broadcast_to((ROWS, NT, P)), ALU.add)\
                  .then_inc(dve_own.sem, dve_own.one())
                nc.vector.tensor_tensor(seq3(WK), seq3(A), DL.unsqueeze(2).broadcast_to((ROWS, NT, P)), ALU.add)\
                  .then_inc(dve_own.sem, dve_own.one())
                dve.wait_ge(dve_own.sem, dve_own.n)
                dve.sem_inc(logs_ready.sem, 1)
                dve.wait_ge(exps_ready.sem, exps_ready.at(1))
                nc.vector.tensor_scalar(WI, WI, MQ ** -0.5, None, ALU.mult).then_inc(dve_own.sem, dve_own.one())
                nc.vector.tensor_tensor(WX, WC.unsqueeze(1).broadcast_to((ROWS, 8, NT)),
                                        PAIR.unsqueeze(2).broadcast_to((ROWS, 8, NT)), ALU.mult)\
                  .then_inc(dve_own.sem, dve_own.one())
                dve.wait_ge(dve_own.sem, dve_own.n)
                dve.sem_inc(rows_ready.sem, 1)
                dve.wait_ge(rows_back.sem, rows_back.at(1))
                for b in range(3):
                    nc.vector.tensor_copy(TA[:, 3 * b:3 * b + 3, :, :].rearrange("p t n r -> p (t n r)"), PS[:, 2 + b, 0:480])
                nc.vector.tensor_copy(WCB.rearrange("p d b t -> p (d b t)"), PS[:, 5, 0:72])
        close_tiles(18)
        for e in (gates_ready, rows_turned, logs_ready, exps_ready, rows_ready, rows_back):
            e.close(1)
        loaded.close(16)
        stored.close(16)

        XM = F1[:, 6912:7424].rearrange("p (s h i) -> p s h i", s=2, h=2)
        SW = F1[:, 7424:7936].rearrange("p (s h i) -> p s h i", s=2, h=2)
        WV = F1[:, 7936:8452].rearrange("p (s h e) -> p s h e", s=2, h=2)
        IA = F1[:, 8452:8968].rearrange("p (s h e) -> p s h e", s=2, h=2)
        ystage = MI[:, 2048:4096].rearrange("p (s n) -> p s n", s=2)
        NU = MX[:, :].rearrange("p (h e) -> p h e", h=2)
        den = SM[:, 1440:1444]
        msteps = [(d, 0, b) for d in range(2) for b in range(4)]
        msteps += [(d, t if d == 0 else 9 - t, b) for t in range(1, NT) for d in range(2) for b in range(4)]
        NM = len(msteps)

        with nc.Block() as block:
            @block.sync
            def _(sp):
                for q in range(2 * NT):
                    sp.wait_ge(tail_done.sem, tail_done.at(4 * q + 4))
                    d, t, _ = msteps[4 * q]
                    sp.dma_start(y_spill[d, t, :, :], ystage[:, q % 2, :]).then_inc(y_stored[q % 2].sem, 16)
                    if q == 1:
                        sp.dma_start(o_mls, CST).then_inc(stored.sem, 16)
                        sp.wait_ge(stored.sem, stored.at(16))
                        sp.dma_start(CST, mls0).then_inc(loaded.sem, 16)
                    gate_store(sp, q)
                    if q == 10:
                        feed(sp, S_OUTO + 1)
                gate_stored(sp)
                for n in range(2):
                    sp.wait_ge(y_stored[n].sem, y_stored[n].at(16 * NT))

            @block.gpsimd
            def _(pool):
                for n, (d, t, b) in enumerate(msteps):
                    if n >= 2:
                        pool.wait_ge(memory_summed.sem, memory_summed.at(n - 1))
                    wk = TA[:, t, 3, 32 * d + 2 * b:32 * d + 2 * b + 2]
                    nc.gpsimd.tensor_tensor(WV[:, n % 2, :, :], v1[:, t, 2 * b:2 * b + 2, :],
                                            wk.unsqueeze(2).broadcast_to((P, 2, V1)), ALU.mult).then_inc(values_weighted.sem, 1)

            @block.tensor
            def _(pe):
                def exponents(n):
                    d, t, b = msteps[n]
                    if n >= 1:
                        pe.wait_ge(exponents_masked.sem, exponents_masked.at(n))
                    for h in range(2):
                        mm = nc.tensor.matmul(PS[:, 0, h * P:(h + 1) * P],
                                              ident[R40, 32 * d + 2 * b + h:32 * d + 2 * b + h + 1].broadcast_to((ROWS, P)),
                                              B[:, t * P:(t + 1) * P], start=True, stop=True)
                    mm.then_inc(exponents_done.sem, 1)

                def scores(n):
                    d, t, b = msteps[n]
                    if n >= 1:
                        pe.wait_ge(scores_weighted.sem, scores_weighted.at(n))
                    for h in range(2):
                        r = slice(64 * h, 64 * h + 64)
                        mm = nc.tensor.matmul(PS[:, 2 + h, 0:P], kT[r, b, t * P:(t + 1) * P], qT[r, b, t * P:(t + 1) * P],
                                              start=True, stop=True)
                    mm.then_inc(qk_done.sem, 1)

                exponents(0)
                scores(0)
                for n, (d, t, b) in enumerate(msteps):
                    if n + 1 < NM:
                        exponents(n + 1)
                    gate_product(pe, 2 * n, S_VO + 2, (1, 7))
                    pe.wait_ge(scores_weighted.sem, scores_weighted.at(n + 1))
                    if n >= 1:
                        pe.wait_ge(intra_taken.sem, intra_taken.at(n))
                    for h in range(2):
                        mm = nc.tensor.matmul(PS[:, 4, h * V1:(h + 1) * V1], SW[:, n % 2, h, :], v1[:, t, 2 * b + h, :],
                                              start=True, stop=True)
                    mm.then_inc(intra_summed.sem, 1)
                    if n + 1 < NM:
                        scores(n + 1)
                    gate_product(pe, 2 * n + 1, S_VO + 2, (1, 7))
                    if n >= 1:
                        pe.wait_ge(tail_done.sem, tail_done.at(n))
                    if n >= 8:
                        if n == 8:
                            pe.wait_ge(loaded.sem, loaded.at(16))
                        for h in range(2):
                            r = slice(64 * h, 64 * h + 64)
                            nc.tensor.matmul(PS[:, 5 + h, 0:V1], qT[r, b, t * P:(t + 1) * P], CST[r, d, b, :],
                                             start=True, stop=True)
                    pe.wait_ge(values_weighted.sem, values_weighted.at(n + 1))
                    for h in range(2):
                        mm = nc.tensor.matmul(PS[64 * h:64 * h + 64, 5, V1:2 * V1], ktok[:, t, (2 * b + h) * MQ:(2 * b + h + 1) * MQ],
                                              WV[:, n % 2, h, :], start=True, stop=True)
                    mm.then_inc(memory_summed.sem, 1)

            @block.scalar
            def _(act):
                def weights(n):
                    d, t, b = msteps[n]
                    act.wait_ge(exponents_masked.sem, exponents_masked.at(n + 1))
                    for h in range(2):
                        c = 32 * d + 2 * b + h
                        ins = act.activation(XM[:, n % 2, h, :], XM[:, n % 2, h, :], ACT.Exp, bias=TA[:, t, 0, c:c + 1])
                        if h == 0:
                            ins.then_inc(act_own.sem, act_own.one())
                    act.wait_ge(act_own.sem, act_own.n)
                    ins.then_inc(exp_ready.sem, 1)

                weights(0)
                for n in range(NM):
                    if n + 1 < NM:
                        weights(n + 1)
                    act.wait_ge(intra_summed.sem, intra_summed.at(n + 1))
                    if n >= 2:
                        act.wait_ge(tail_done.sem, tail_done.at(n - 1))
                    act.activation(IA[:, n % 2, :, :].rearrange("p h e -> p (h e)"), PS[:, 4, 0:2 * V1], ACT.Copy)\
                       .then_inc(intra_taken.sem, 1)
                    if n % 4 == 0 and n > 0:
                        gate_take(act, n // 4 - 1, (1, 7))
                gate_take(act, 2 * NT - 1, (1, 7))

            @block.vector
            def _(dve):
                def masked(n):
                    d = msteps[n][0]
                    dve.wait_ge(exponents_done.sem, exponents_done.at(n + 1))
                    if n >= 2:
                        dve.wait_ge(scores_weighted.sem, scores_weighted.at(n - 1))
                    nc.vector.tensor_tensor(XM[:, n % 2, :, :], PS[:, 0, 0:256].rearrange("p (h i) -> p h i", h=2),
                                            const(("neg_f", "neg_b")[d]).unsqueeze(1).broadcast_to((P, 2, P)), ALU.add)\
                      .then_inc(exponents_masked.sem, 1)

                def weighted(n):
                    dve.wait_ge(qk_done.sem, qk_done.at(n + 1))
                    dve.wait_ge(exp_ready.sem, exp_ready.at(n + 1))
                    if n >= 2:
                        dve.wait_ge(intra_summed.sem, intra_summed.at(n - 1))
                    nc.vector.scalar_tensor_tensor(out=SW[:, n % 2, :, :], in0=PS[:, 2:4, 0:P], scalar=MQ ** -0.5,
                                                   in1=XM[:, n % 2, :, :], op0=ALU.mult, op1=ALU.mult).then_inc(scores_weighted.sem, 1)

                def tail(n):
                    d, t, b = msteps[n]
                    c = 32 * d + 2 * b
                    dve.wait_ge(intra_taken.sem, intra_taken.at(n + 1))
                    dve.wait_ge(memory_summed.sem, memory_summed.at(n + 1))
                    if n >= 8:
                        for h in range(2):
                            nc.vector.scalar_tensor_tensor(
                                out=NU[:, h, :], in0=PS[:, 5 + h, 0:V1], scalar=TA[:, t, 1, c + h:c + h + 1],
                                in1=IA[:, n % 2, h, :], op0=ALU.mult, op1=ALU.add).then_inc(dve_own.sem, dve_own.one())
                        dve.wait_ge(dve_own.sem, dve_own.n)
                        nc.vector.scalar_tensor_tensor(out=CST[:, d, b, :], in0=CST[:, d, b, :],
                                                                      scalar=WCB[:, d, b, t:t + 1], in1=PS[:, 5, V1:2 * V1],
                                                                      op0=ALU.mult, op1=ALU.add).then_inc(dve_own.sem, dve_own.one())
                        nu = NU
                    else:
                        nc.vector.tensor_copy(CST[:, d, b, :], PS[:, 5, V1:2 * V1]).then_inc(dve_own.sem, dve_own.one())
                        nu = IA[:, n % 2, :, :]
                    dd, rd = den[:, 0:2], den[:, 2:4]
                    nc.vector.scalar_tensor_tensor(out=dd, in0=nu[:, :, MV], scalar=-1.0, in1=nu[:, :, MV],
                                                                  op0=ALU.mult, op1=ALU.max).then_inc(dve_own.sem, dve_own.one())
                    dve.wait_ge(dve_own.sem, dve_own.n)
                    nc.vector.tensor_tensor(dd, dd, TA[:, t, 2, c:c + 2], ALU.max).then_inc(dve_own.sem, dve_own.one())
                    dve.wait_ge(dve_own.sem, dve_own.n)
                    nc.vector.reciprocal(rd, dd).then_inc(dve_own.sem, dve_own.one())
                    dve.wait_ge(dve_own.sem, dve_own.n)
                    q = n // 4
                    if b == 0 and q >= 2:
                        dve.wait_ge(y_stored[q % 2].sem, y_stored[q % 2].at(16 * (q // 2)))
                    for h in range(2):
                        nc.vector.tensor_scalar(ystage[:, q % 2, (2 * b + h) * MV:(2 * b + h + 1) * MV], nu[:, h, 0:MV],
                                                rd[:, h:h + 1], None, ALU.mult).then_inc(dve_own.sem, dve_own.one())
                    dve.wait_ge(dve_own.sem, dve_own.n)
                    dve.sem_inc(tail_done.sem, 1)
                    if n == 7:
                        dve.wait_ge(loaded.sem, loaded.at(16))

                masked(0)
                for n in range(NM):
                    weighted(n)
                    if n + 1 < NM:
                        masked(n + 1)
                    if n >= 1:
                        tail(n - 1)
                tail(NM - 1)
        stored.close(16)
        loaded.close(16)
        close_gate()
        for e in (exponents_done, exponents_masked, qk_done, exp_ready, scores_weighted, intra_taken, memory_summed, tail_done, values_weighted, intra_summed):
            e.close(NM)

        gate(1, S_OUTO)
        out_projection(1, S_OUTO, 2, [f0k[:, b, :] for b in range(8)])
        mixer.close()
        mlp(1)
        with (nc.sbuf_tensor("y_out", [P, KD, T], F32) as yo, nc.sbuf_tensor("squares_f", [P, 8, TC], F32) as SQ,
              nc.sbuf_tensor("rms_f", [P, T], F32) as RB):
            norm(1, 2, yo, SQ, RB, 0, final=True)


def kernel(**inputs):
    import numpy as _np
    import concourse.bacc as _bacc
    from concourse import mybir as _mybir
    from concourse.bass_utils import run_bass_kernel_spmd as _run

    a = {k: _np.asarray(v) for k, v in inputs.items()}
    f32 = _np.float32

    def fm(x):
        return x.reshape(x.shape[0], -1, P).transpose(2, 1, 0)

    def cols(x):
        return x.reshape(-1, P).T

    def kslots(w, n):
        k = w.shape[0] // P
        return w.reshape(k, P, -1, n).transpose(2, 1, 0, 3).reshape(-1, P, k * n)

    def rows(x):
        return _np.broadcast_to(x.reshape(1, -1), (P, x.size))

    m0 = _np.zeros((P, 1), f32)
    m0[0:8, 0] = a["state_mlstm_m"][0, 0, 0]
    m0[32:40, 0] = a["state_mlstm_m"][0, 0, 1]
    parts = {
        "cond": fm(_np.concatenate([a["c_ctx"][None], a["c"]], 0)).reshape(P, -1),
        "b_mod": cols(a["b_mod"]), "norm_mix": cols(a["norm_mix"]), "norm_ffn": cols(a["norm_ffn"]),
        "norm_f": cols(a["norm_f"]), "ssd_norm": cols(a["ssd_norm"][0]),
        "cw": fm(a["ssd_conv_w"][0]).reshape(P, -1), "cb": cols(a["ssd_conv_b"][0]),
        "mw": fm(a["ml_conv_w"][0]).reshape(P, -1), "mb": cols(a["ml_conv_b"][0]),
        "dt_bias": rows(a["ssd_dt_bias"][0]), "a_log": rows(a["ssd_a_log"][0]), "ssd_d": rows(a["ssd_d"][0]),
        "gate_b": rows(a["ml_gate_b"][0]), "m0": m0,
    }
    vec = _np.concatenate([parts[k] for k in VECS], 1)

    wi, wo = a["w_in_even"][0], a["w_in_odd"][0]
    out_e = _np.zeros((4, P, 4096), f32)
    out_e[:, :, 0:3072] = kslots(a["w_out_even"][0], 256)
    wmod = kslots(a["w_mod"].transpose(1, 0, 2).reshape(D, -1), 512)
    slots = [kslots(wi[:, 0:1536], 512), kslots(wi[:, 1536:2560], 512), kslots(wi[:, 2560:4096], 512), out_e[0:2],
             kslots(wo[:, 0:3072], 512), kslots(a["w_out_odd"][0], 512), out_e[2:4]]
    wslots = _np.concatenate(slots, 0)
    wff = _np.zeros((2, 4 * NG, P, 1024), f32)
    for l in range(2):
        w1 = kslots(a["w_ff1"][l], P)
        w2 = a["w_ff2"][l].reshape(FF // P, P, D)
        wff[l, 0:4] = w1[0:4]
        for g in range(1, NG - 1):
            wff[l, 4 * g:4 * g + 2] = w2[2 * g - 2:2 * g]
            wff[l, 4 * g + 2:4 * g + 4] = w1[2 * g + 2:2 * g + 4]
        wff[l, 4 * NG - 4:4 * NG] = w2[FF // P - 4:FF // P]
    wsmall = _np.stack([kslots(wi[:, 4096:4128], 32)[0], kslots(wo[:, 3072:3104], 32)[0]], 1).reshape(P, 2, KD, 32)

    r = _np.arange(1, 15)[None, :, None]
    half = (_np.arange(P) // 64)[:, None, None]
    c = (_np.arange(P) % 64)[:, None, None]
    cc = _np.clip(_np.arange(64)[None, None, :] - c + 15, 0, 30)
    rpbT = a["na_rpb"][0][:, r - half, cc]

    kc = a["cache_na_k"][0, 0].reshape(4, 2, CTX, HD).transpose(1, 3, 0, 2).reshape(P, 4, CTX)
    vc = a["cache_na_v"][0, 0].transpose(1, 0, 2).reshape(CTX, 512)
    ssd0 = a["state_ssd"][0, 0].transpose(3, 0, 1, 2).reshape(SN, 2, SH * SP)
    mc = a["state_mlstm_c"][0, 0].reshape(2, 4, 2, MV, MQ).transpose(2, 4, 0, 1, 3)
    mn = a["state_mlstm_n"][0, 0].reshape(2, 4, 2, MQ).transpose(2, 3, 0, 1)[..., None]
    mls0 = _np.concatenate([mc, mn], -1).reshape(P, 2, 4, V1)
    xT = fm(_np.concatenate([a["x_prompt"][0], a["x_sample"][0]], 0)).reshape(P, -1)

    given = {"xT": xT, "vec": vec, "consts": row_consts(), "wmod": wmod, "wslots": wslots, "wff": wff, "wsmall": wsmall, "rpbT": rpbT,
             "kcT": kc, "vc": vc, "ssd0": ssd0, "mls0": mls0}
    nc = _bacc.Bacc("TRN2", target_bir_lowering=False, num_devices=1)
    arrays, args = {}, []
    for name, x in given.items():
        x = _np.ascontiguousarray(x)
        arrays[f"in_{name}"] = x
        args.append(nc.dram_tensor(f"in_{name}", x.shape, _mybir.dt.from_np(x.dtype), kind="ExternalInput").ap())
    outs = {"y": (P, KD, T), "k": (P, 4, CTX), "v": (CTX, 512), "ssd": (SN, 2, SH * SP), "mls": (P, 2, 4, V1), "m": (ROWS, NT)}
    for name, shape in outs.items():
        args.append(nc.dram_tensor(f"out_{name}", shape, _mybir.dt.float32, kind="ExternalOutput").ap())
    hybrid_step(nc, *args)
    r = _run(nc, [arrays], core_ids=[0]).results[0]

    y = r["out_y"].transpose(2, 1, 0).reshape(T, D)
    nk = r["out_k"].reshape(2, HD, 4, CTX).transpose(2, 0, 3, 1).reshape(1, 1, NH, CTX, HD)
    nv = r["out_v"].reshape(CTX, NH, HD).transpose(1, 0, 2).reshape(1, 1, NH, CTX, HD)
    ns = r["out_ssd"].reshape(SN, 2, SH, SP).transpose(1, 2, 3, 0).reshape(1, 1, 2, SH, SP, SN)
    m = r["out_mls"].reshape(2, MQ, 2, 4, V1).transpose(2, 3, 0, 4, 1).reshape(2, MH, V1, MQ)
    nm = _np.stack([r["out_m"][0:8, 0], r["out_m"][32:40, 0]], 0).reshape(1, 1, 2, MH)
    return (y[None, 0:CTX], y[None, CTX:T], nk, nv, ns, m[:, :, 0:MV, :].reshape(1, 1, 2, MH, MV, MQ),
            m[:, :, MV, :].reshape(1, 1, 2, MH, MQ), nm)
```
